# Optimizing a Trainium2 kernel written in Bass

```python
import math
import jax, jax.numpy as jnp
from jax import lax
import numpy as np

D_MODEL = 1024
BATCH = 1
SEQ = 256
DEPTH = 1

A_HEADS = 4
A_HEAD_DIM = 128
A_WIDTH = A_HEADS * A_HEAD_DIM
A_CHUNK = 128
B_WIDTH = 512
B_KERNEL = 31
C_HEADS = 8
C_NOPE = 64
C_ROPE = 32
C_QK_DIM = C_NOPE + C_ROPE
C_VDIM = 64
C_Q_RANK = 384
C_KV_RANK = 256
Q_BLOCK = 128
ROPE_THETA = 10000.0
N_BRANCHES = 3
N_EXPERTS = 16
EXPERT_FF = 1536
CAPACITY_FACTOR = 2
EPS = 1e-6

IN_SIZES = (
    A_WIDTH,
    A_WIDTH,
    A_WIDTH,
    A_WIDTH,
    4 * A_HEADS,
    2 * B_WIDTH,
    C_Q_RANK,
    C_KV_RANK,
    C_ROPE,
    N_BRANCHES * D_MODEL,
)
IN_WIDTH = int(sum(IN_SIZES))
IN_OFFSETS = tuple(int(o) for o in np.cumsum(IN_SIZES)[:-1])


def _rmsnorm(x, g):
    xf = x.astype(jnp.float32)
    y = xf * lax.rsqrt(jnp.mean(xf * xf, axis=-1, keepdims=True) + EPS)
    return (y * g.astype(jnp.float32)).astype(x.dtype)

def _layernorm(x, g, b):
    xf = x.astype(jnp.float32)
    mu = jnp.mean(xf, axis=-1, keepdims=True)
    xc = xf - mu
    y = xc * lax.rsqrt(jnp.mean(xc * xc, axis=-1, keepdims=True) + EPS)
    return (y * g.astype(jnp.float32) + b.astype(jnp.float32)).astype(x.dtype)

def _mlstm_chunkwise(q, k, v, i_pre, f_pre):
    B, H, S, Dh = q.shape
    nc = S // A_CHUNK
    f32 = jnp.float32

    def chunks(t):
        return jnp.moveaxis(t.astype(f32).reshape(B, H, nc, A_CHUNK, *t.shape[3:]), 2, 0)

    qc = chunks(q)
    kc = chunks(k) * (Dh ** -0.5)
    vc = chunks(v)
    ic = chunks(i_pre)
    lfc = chunks(jax.nn.log_sigmoid(f_pre.astype(f32)))
    tril = jnp.tril(jnp.ones((A_CHUNK, A_CHUNK), dtype=bool))

    def step(carry, inp):
        C, n, m = carry
        qb, kb, vb, ib, lfb = inp
        bcum = jnp.cumsum(lfb, axis=-1)
        dlog = bcum[..., :, None] - bcum[..., None, :] + ib[..., None, :]
        dlog = jnp.where(tril, dlog, -jnp.inf)
        m_inter = bcum + m[..., None]
        m_t = jnp.maximum(m_inter, jnp.max(dlog, axis=-1))
        w_inter = jnp.exp(m_inter - m_t)
        scores = jnp.einsum('bhtd,bhsd->bhts', qb, kb) * jnp.exp(dlog - m_t[..., None])
        num = (w_inter[..., None] * jnp.einsum('bhtd,bhde->bhte', qb, C)
               + jnp.einsum('bhts,bhse->bhte', scores, vb))
        den = w_inter * jnp.einsum('bhtd,bhd->bht', qb, n) + jnp.sum(scores, axis=-1)
        h = num / jnp.maximum(jnp.abs(den), jnp.exp(-m_t))[..., None]
        g_tot = bcum[..., -1]
        a = g_tot[..., None] - bcum + ib
        m_new = jnp.maximum(g_tot + m, jnp.max(a, axis=-1))
        decay = jnp.exp(g_tot + m - m_new)
        wk = jnp.exp(a - m_new[..., None])
        C_new = decay[..., None, None] * C + jnp.einsum('bhs,bhsd,bhse->bhde', wk, kb, vb)
        n_new = decay[..., None] * n + jnp.einsum('bhs,bhsd->bhd', wk, kb)
        return (C_new, n_new, m_new), h

    init = (jnp.zeros((B, H, Dh, Dh), f32), jnp.zeros((B, H, Dh), f32), jnp.zeros((B, H), f32))
    _, h = lax.scan(step, init, (qc, kc, vc, ic, lfc))
    return jnp.moveaxis(h, 0, 2).reshape(B, H, S, Dh)

def _rope_tail(t, cos, sin):
    nope, r = t[..., :C_NOPE], t[..., C_NOPE:]
    r1, r2 = jnp.split(r, 2, axis=-1)
    c = cos[:, None, :].astype(t.dtype)
    s = sin[:, None, :].astype(t.dtype)
    return jnp.concatenate([nope, r1 * c - r2 * s, r2 * c + r1 * s], axis=-1)

def _dense_attention(q, k, v):
    B, H, S, Dq = q.shape
    nq = S // Q_BLOCK
    qb = jnp.moveaxis(q.reshape(B, H, nq, Q_BLOCK, Dq), 2, 0)
    scale = Dq ** -0.5

    def block(qi):
        s = jnp.einsum('bhqd,bhkd->bhqk', qi, k).astype(jnp.float32) * scale
        p = jax.nn.softmax(s, axis=-1).astype(v.dtype)
        return jnp.einsum('bhqk,bhkd->bhqd', p, v)

    o = lax.map(block, qb)
    return jnp.moveaxis(o, 0, 2).reshape(B, H, S, v.shape[-1])

def _mixer(x, cos, sin, norm_g, w_in, b_if, a_norm_g, w_a_out, conv_w, conv_b,
           conv_ln_g, conv_ln_b, w_b_out, cq_norm_g, w_uq, ckv_norm_g, w_ukv,
           q_norm_g, k_norm_g, w_c_out, w_out):
    B, S, _ = x.shape
    xn = _rmsnorm(x, norm_g)
    z = xn @ w_in
    a_q, a_k, a_v, a_o, a_g, b_glu, c_q, c_kv, c_kr, gts = jnp.split(z, IN_OFFSETS, axis=-1)

    def heads(t):
        return t.reshape(B, S, A_HEADS, A_HEAD_DIM).transpose(0, 2, 1, 3)
    q, k, v = heads(a_q), heads(a_k), heads(a_v)
    gate_pre = (a_g + b_if).reshape(B, S, 4, A_HEADS).transpose(2, 0, 3, 1)
    i_fw, f_fw, i_bw, f_bw = gate_pre[0], gate_pre[1], gate_pre[2], gate_pre[3]
    rev = lambda t: jnp.flip(t, axis=2)
    h_fw = _mlstm_chunkwise(q, k, v, i_fw, f_fw)
    h_bw = rev(_mlstm_chunkwise(rev(q), rev(k), rev(v), rev(i_bw), rev(f_bw)))
    h = _rmsnorm(h_fw + h_bw, a_norm_g[:, None, :])
    h = h.transpose(0, 2, 1, 3).reshape(B, S, A_WIDTH) * jax.nn.sigmoid(a_o)
    y_a = h @ w_a_out

    u_a, u_g = jnp.split(b_glu, 2, axis=-1)
    u = u_a * jax.nn.sigmoid(u_g)
    u = lax.conv_general_dilated(
        u, conv_w[:, None, :].astype(u.dtype), window_strides=(1,),
        padding=[(B_KERNEL // 2, B_KERNEL // 2)],
        dimension_numbers=('NWC', 'WIO', 'NWC'),
        feature_group_count=B_WIDTH) + conv_b
    u = jax.nn.silu(_layernorm(u, conv_ln_g, conv_ln_b))
    y_b = u @ w_b_out

    qh = (_rmsnorm(c_q, cq_norm_g) @ w_uq).reshape(B, S, C_HEADS, C_QK_DIM)
    kv = (_rmsnorm(c_kv, ckv_norm_g) @ w_ukv).reshape(B, S, C_HEADS, C_NOPE + C_VDIM)
    k_nope, v_c = kv[..., :C_NOPE], kv[..., C_NOPE:]
    k_r = jnp.broadcast_to(c_kr[:, :, None, :], (B, S, C_HEADS, C_ROPE))
    kh = jnp.concatenate([k_nope, k_r], axis=-1)
    qh = _rope_tail(_rmsnorm(qh, q_norm_g), cos, sin)
    kh = _rope_tail(_rmsnorm(kh, k_norm_g), cos, sin)
    o = _dense_attention(qh.transpose(0, 2, 1, 3), kh.transpose(0, 2, 1, 3),
                         v_c.transpose(0, 2, 1, 3))
    y_c = o.transpose(0, 2, 1, 3).reshape(B, S, C_HEADS * C_VDIM) @ w_c_out

    g = jax.nn.sigmoid(gts).reshape(B, S, N_BRANCHES, D_MODEL)
    merged = g[..., 0, :] * y_a + g[..., 1, :] * y_b + g[..., 2, :] * y_c
    return merged @ w_out

def _expert_choice_ffn(x, norm_g, w_router, w_e_gate, w_e_up, w_e_down):
    B, S, D = x.shape
    xn = _rmsnorm(x, norm_g)
    aff = jax.nn.softmax((xn @ w_router).astype(jnp.float32), axis=-1)
    cap = CAPACITY_FACTOR * S // N_EXPERTS
    gate, idx = lax.top_k(jnp.swapaxes(aff, 1, 2), cap)
    bidx = jnp.arange(B)[:, None, None]
    xg = xn[bidx, idx]
    h = (jax.nn.silu(jnp.einsum('becd,edf->becf', xg, w_e_gate))
         * jnp.einsum('becd,edf->becf', xg, w_e_up))
    yo = jnp.einsum('becf,efd->becd', h, w_e_down) * gate[..., None].astype(xg.dtype)
    return jnp.zeros((B, S, D), yo.dtype).at[bidx, idx].add(yo)

def first_inputs(seed: int = 0) -> dict:
    key = jax.random.key(seed)
    ks = jax.random.split(key, 32)
    L, D, H = DEPTH, D_MODEL, A_HEADS
    f32 = jnp.float32

    def nrm(k, shape, scale):
        return jax.random.normal(k, shape, f32) * scale

    def gain(k, shape):
        return 1.0 + 0.02 * jax.random.normal(k, shape, f32)

    b_i = 0.1 * jax.random.normal(ks[3], (L, 2, H), f32)
    b_f = 3.0 + 3.0 * jax.random.uniform(ks[4], (L, 2, H), f32)
    b_if = jnp.stack([b_i[:, 0], b_f[:, 0], b_i[:, 1], b_f[:, 1]], axis=1).reshape(L, 4 * H)

    return {
        "x": jax.random.normal(ks[0], (BATCH, SEQ, D), f32),
        "mix_norm_g": gain(ks[1], (L, D)),
        "w_in": nrm(ks[2], (L, D, IN_WIDTH), D ** -0.5),
        "b_if": b_if,
        "a_norm_g": gain(ks[5], (L, H, A_HEAD_DIM)),
        "w_a_out": nrm(ks[6], (L, A_WIDTH, D), A_WIDTH ** -0.5),
        "conv_w": nrm(ks[7], (L, B_KERNEL, B_WIDTH), B_KERNEL ** -0.5),
        "conv_b": 0.02 * jax.random.normal(ks[8], (L, B_WIDTH), f32),
        "conv_ln_g": gain(ks[9], (L, B_WIDTH)),
        "conv_ln_b": 0.02 * jax.random.normal(ks[10], (L, B_WIDTH), f32),
        "w_b_out": nrm(ks[11], (L, B_WIDTH, D), B_WIDTH ** -0.5),
        "cq_norm_g": gain(ks[12], (L, C_Q_RANK)),
        "w_uq": nrm(ks[13], (L, C_Q_RANK, C_HEADS * C_QK_DIM), C_Q_RANK ** -0.5),
        "ckv_norm_g": gain(ks[14], (L, C_KV_RANK)),
        "w_ukv": nrm(ks[15], (L, C_KV_RANK, C_HEADS * (C_NOPE + C_VDIM)), C_KV_RANK ** -0.5),
        "q_norm_g": gain(ks[16], (L, C_QK_DIM)),
        "k_norm_g": gain(ks[17], (L, C_QK_DIM)),
        "w_c_out": nrm(ks[18], (L, C_HEADS * C_VDIM, D), (C_HEADS * C_VDIM) ** -0.5),
        "w_out": nrm(ks[19], (L, D, D), D ** -0.5),
        "ffn_norm_g": gain(ks[20], (L, D)),
        "w_router": nrm(ks[21], (L, D, N_EXPERTS), D ** -0.5),
        "w_e_gate": nrm(ks[22], (L, N_EXPERTS, D, EXPERT_FF), D ** -0.5),
        "w_e_up": nrm(ks[23], (L, N_EXPERTS, D, EXPERT_FF), D ** -0.5),
        "w_e_down": nrm(ks[24], (L, N_EXPERTS, EXPERT_FF, D), EXPERT_FF ** -0.5),
    }

def first_block(x, mix_norm_g, w_in, b_if, a_norm_g, w_a_out, conv_w, conv_b, conv_ln_g,
              conv_ln_b, w_b_out, cq_norm_g, w_uq, ckv_norm_g, w_ukv, q_norm_g, k_norm_g,
              w_c_out, w_out, ffn_norm_g, w_router, w_e_gate, w_e_up, w_e_down):
    S = x.shape[1]
    pos = jnp.arange(S, dtype=jnp.float32)
    inv_freq = ROPE_THETA ** (-jnp.arange(0, C_ROPE, 2, dtype=jnp.float32) / C_ROPE)
    ang = pos[:, None] * inv_freq[None, :]
    cos, sin = jnp.cos(ang), jnp.sin(ang)
    for l in range(DEPTH):
        x = x + _mixer(x, cos, sin, mix_norm_g[l], w_in[l], b_if[l], a_norm_g[l], w_a_out[l],
                       conv_w[l], conv_b[l], conv_ln_g[l], conv_ln_b[l], w_b_out[l],
                       cq_norm_g[l], w_uq[l], ckv_norm_g[l], w_ukv[l], q_norm_g[l],
                       k_norm_g[l], w_c_out[l], w_out[l])
        x = x + _expert_choice_ffn(x, ffn_norm_g[l], w_router[l], w_e_gate[l], w_e_up[l],
                                   w_e_down[l])
    return x


GDN_HEADS = 4
GDN_DK = 128
GDN_DV = 128
HG_HEADS = 4
HG_DK = 128
HG_DV = 128
GDN_QK = GDN_HEADS * GDN_DK
GDN_V = GDN_HEADS * GDN_DV
HG_K = HG_HEADS * HG_DK
HG_V = HG_HEADS * HG_DV
D_MIX = GDN_V + HG_V
D_IN = 2 * GDN_QK + 2 * GDN_V + 2 * GDN_HEADS + 2 * HG_K + 2 * HG_V
CONV_K = 4
CHUNK = 64
N_EXPERTS_2 = 64
N_GROUPS = 8
TOPK_GROUPS = 4
TOP_K = 8
D_EXPERT = 256
D_SHARED = 256
ROUTE_SCALE = 2.5
MOE_BLOCK = 128


def rms_norm(x, w):
    xf = x.astype(jnp.float32)
    y = xf * lax.rsqrt(jnp.mean(xf * xf, axis=-1, keepdims=True) + EPS)
    return (y * w.astype(jnp.float32)).astype(x.dtype)

def l2_normalize(x):
    return x * lax.rsqrt(jnp.sum(x * x, axis=-1, keepdims=True) + EPS)

def causal_short_conv(x, w):
    T = x.shape[1]
    xp = jnp.pad(x, ((0, 0), (CONV_K - 1, 0), (0, 0)))
    y = sum(xp[:, j:j + T, :] * w[j] for j in range(CONV_K))
    return jax.nn.silu(y)

def to_chunks(t):
    B, T, H, D = t.shape
    return t.reshape(B, T // CHUNK, CHUNK, H, D).transpose(0, 3, 1, 2, 4)

def from_chunks(o):
    N, B, H, C, D = o.shape
    return o.transpose(1, 0, 3, 2, 4).reshape(B, N * C, H, D)

def gated_delta_chunked(q, k, v, g, beta):
    B, T, H, DK = q.shape
    DV = v.shape[-1]
    N = T // CHUNK
    qc, kc, vc = to_chunks(q), to_chunks(k), to_chunks(v)
    gc = jnp.cumsum(g.reshape(B, N, CHUNK, H).transpose(0, 3, 1, 2), axis=-1)
    bc = beta.reshape(B, N, CHUNK, H).transpose(0, 3, 1, 2)
    idx = jnp.arange(CHUNK)
    causal = idx[:, None] >= idx[None, :]
    strict = idx[:, None] > idx[None, :]
    decay = jnp.exp(jnp.where(causal, gc[..., :, None] - gc[..., None, :], -jnp.inf))
    kb = kc * bc[..., None]
    L = jnp.where(strict, jnp.einsum('bhncd,bhnsd->bhncs', kb, kc) * decay, 0.0)
    rhs = jnp.concatenate([vc * bc[..., None], kb * jnp.exp(gc)[..., None]], axis=-1)
    sol = lax.linalg.triangular_solve(L + jnp.eye(CHUNK, dtype=L.dtype), rhs,
                                      left_side=True, lower=True, unit_diagonal=True)
    u, w = sol[..., :DV], sol[..., DV:]
    attn = jnp.einsum('bhncd,bhnsd->bhncs', qc, kc) * decay
    q_dec = qc * jnp.exp(gc)[..., None]
    g_last = gc[..., -1]
    k_tail = kc * jnp.exp(g_last[..., None] - gc)[..., None]

    def step(S, xs):
        u_n, w_n, a_n, qd_n, kt_n, gl_n = xs
        v_new = u_n - jnp.einsum('bhcd,bhdv->bhcv', w_n, S)
        o = jnp.einsum('bhcd,bhdv->bhcv', qd_n, S) + jnp.einsum('bhcs,bhsv->bhcv', a_n, v_new)
        S = S * jnp.exp(gl_n)[..., None, None] + jnp.einsum('bhcd,bhcv->bhdv', kt_n, v_new)
        return S, o

    xs = tuple(jnp.moveaxis(t, 2, 0) for t in (u, w, attn, q_dec, k_tail, g_last))
    S0 = jnp.zeros((B, H, DK, DV), q.dtype)
    _, o = lax.scan(step, S0, xs)
    return from_chunks(o)

def hgrn2_chunked(q, k, v, logf):
    B, T, H, DK = q.shape
    DV = v.shape[-1]
    qc, kc, vc = to_chunks(q), to_chunks(k), to_chunks(v)
    bc = jnp.cumsum(to_chunks(logf), axis=3)
    idx = jnp.arange(CHUNK)
    causal = (idx[:, None] >= idx[None, :])[:, :, None]

    def step(S, xs):
        q_n, k_n, v_n, b_n = xs
        decay = jnp.exp(jnp.where(causal, b_n[..., :, None, :] - b_n[..., None, :, :], -jnp.inf))
        A = jnp.einsum('bhtd,bhsd,bhtsd->bhts', q_n, k_n, decay)
        b_last = b_n[..., -1:, :]
        o = jnp.einsum('bhts,bhsv->bhtv', A, v_n) + jnp.einsum('bhtd,bhdv->bhtv', q_n * jnp.exp(b_n), S)
        S = jnp.exp(b_last[..., 0, :])[..., :, None] * S + jnp.einsum('bhsd,bhsv->bhdv', k_n * jnp.exp(b_last - b_n), v_n)
        return S, o

    xs = tuple(jnp.moveaxis(t, 2, 0) for t in (qc, kc, vc, bc))
    S0 = jnp.zeros((B, H, DK, DV), q.dtype)
    _, o = lax.scan(step, S0, xs)
    return from_chunks(o)

def token_mixer(h, w_in, conv_w, a_log, dt_bias, gdn_norm_w, lb, hg_norm_w, w_out):
    B, T, _ = h.shape
    f32 = jnp.float32
    proj = jnp.einsum('btd,de->bte', h, w_in).astype(f32)
    qkv_w = 2 * GDN_QK + GDN_V
    qkv = causal_short_conv(proj[..., :qkv_w], conv_w.astype(f32))
    qA, kA, vA = jnp.split(qkv, [GDN_QK, 2 * GDN_QK], axis=-1)
    sizes = (GDN_V, GDN_HEADS, GDN_HEADS, HG_K, HG_V, HG_K, HG_V)
    cuts = np.cumsum(sizes)[:-1].tolist()
    gateA, beta_raw, a_raw, f_raw, iB, qB, gateB = jnp.split(proj[..., qkv_w:], cuts, axis=-1)

    qA = l2_normalize(qA.reshape(B, T, GDN_HEADS, GDN_DK)) * (GDN_DK ** -0.5)
    kA = l2_normalize(kA.reshape(B, T, GDN_HEADS, GDN_DK))
    vA = vA.reshape(B, T, GDN_HEADS, GDN_DV)
    beta = jax.nn.sigmoid(beta_raw)
    g_log = -jnp.exp(a_log.astype(f32)) * jax.nn.softplus(a_raw + dt_bias.astype(f32))
    oA = gated_delta_chunked(qA, kA, vA, g_log, beta)
    oA = rms_norm(oA, gdn_norm_w) * jax.nn.silu(gateA.reshape(B, T, GDN_HEADS, GDN_DV))
    oA = oA.reshape(B, T, GDN_V)

    lb = lb.reshape(HG_HEADS, HG_DK)
    f_raw = f_raw.reshape(B, T, HG_HEADS, HG_DK)
    logf = jnp.log(lb + (1.0 - lb) * jax.nn.sigmoid(f_raw))
    kB = (1.0 - lb) * jax.nn.sigmoid(-f_raw)
    qB = jax.nn.silu(qB.reshape(B, T, HG_HEADS, HG_DK))
    oB = hgrn2_chunked(qB, kB, iB.reshape(B, T, HG_HEADS, HG_DV), logf).reshape(B, T, HG_V)
    oB = rms_norm(oB, hg_norm_w) * jax.nn.silu(gateB)

    o = jnp.concatenate([oA, oB], axis=-1).astype(h.dtype)
    return jnp.einsum('bte,ed->btd', o, w_out)

def moe(h, w_router, router_bias, w_gate, w_up, w_down, ws_gate, ws_up, ws_down):
    B, T, D = h.shape
    xt = h.reshape(-1, D)
    M = xt.shape[0]
    scores = jax.nn.sigmoid(xt.astype(jnp.float32) @ w_router.astype(jnp.float32))
    sel = scores + router_bias.astype(jnp.float32)
    group_score = lax.top_k(sel.reshape(M, N_GROUPS, N_EXPERTS_2 // N_GROUPS), 2)[0].sum(-1)
    _, gidx = lax.top_k(group_score, TOPK_GROUPS)
    gmask = jax.nn.one_hot(gidx, N_GROUPS, dtype=jnp.float32).sum(-2) > 0
    emask = jnp.repeat(gmask, N_EXPERTS_2 // N_GROUPS, axis=-1)
    _, eidx = lax.top_k(jnp.where(emask, sel, -jnp.inf), TOP_K)
    wts = jnp.take_along_axis(scores, eidx, axis=-1)
    wts = wts / jnp.sum(wts, axis=-1, keepdims=True) * ROUTE_SCALE
    gates = jnp.einsum('mk,mke->me', wts, jax.nn.one_hot(eidx, N_EXPERTS_2, dtype=wts.dtype)).astype(h.dtype)

    def expert_block(args):
        x_b, g_b = args
        hg = jnp.einsum('td,edf->tef', x_b, w_gate)
        hu = jnp.einsum('td,edf->tef', x_b, w_up)
        return jnp.einsum('tef,efd->td', jax.nn.silu(hg) * hu * g_b[..., None], w_down)

    routed = lax.map(expert_block, (xt.reshape(-1, MOE_BLOCK, D), gates.reshape(-1, MOE_BLOCK, N_EXPERTS_2)))
    shared = (jax.nn.silu(xt @ ws_gate) * (xt @ ws_up)) @ ws_down
    return (routed.reshape(M, D) + shared).reshape(B, T, D)

def second_inputs(seed: int = 0) -> dict:
    key = jax.random.key(seed)
    ks = jax.random.split(key, 24)
    f32 = jnp.float32
    nrm = lambda k, s, sc: jax.random.normal(k, s, f32) * sc
    dt = jnp.exp(jax.random.uniform(ks[8], (DEPTH, GDN_HEADS), f32, np.log(1e-3), np.log(1e-1)))
    return {
        "x": nrm(ks[0], (BATCH, SEQ, D_MODEL), 1.0),
        "c": nrm(ks[1], (BATCH, D_MODEL), 1.0),
        "w_ada": nrm(ks[2], (DEPTH, D_MODEL, 6 * D_MODEL), 0.5 * D_MODEL ** -0.5),
        "b_ada": nrm(ks[3], (DEPTH, 6 * D_MODEL), 0.01),
        "norm1_w": 1.0 + nrm(ks[4], (DEPTH, D_MODEL), 0.02),
        "w_in": nrm(ks[5], (DEPTH, D_MODEL, D_IN), D_MODEL ** -0.5),
        "conv_w": nrm(ks[6], (DEPTH, CONV_K, 2 * GDN_QK + GDN_V), CONV_K ** -0.5),
        "gdn_a_log": jnp.log(jax.random.uniform(ks[7], (DEPTH, GDN_HEADS), f32, 1.0, 16.0)),
        "gdn_dt_bias": dt + jnp.log(-jnp.expm1(-dt)),
        "gdn_norm_w": 1.0 + nrm(ks[9], (DEPTH, GDN_DV), 0.02),
        "hg_lb": nrm(ks[10], (DEPTH + 1, HG_K), 0.1),
        "hg_norm_w": 1.0 + nrm(ks[11], (DEPTH, HG_V), 0.02),
        "w_out": nrm(ks[12], (DEPTH, D_MIX, D_MODEL), D_MIX ** -0.5),
        "norm2_w": 1.0 + nrm(ks[13], (DEPTH, D_MODEL), 0.02),
        "w_router": nrm(ks[14], (DEPTH, D_MODEL, N_EXPERTS_2), D_MODEL ** -0.5),
        "router_bias": nrm(ks[15], (DEPTH, N_EXPERTS_2), 0.01),
        "w_gate": nrm(ks[16], (DEPTH, N_EXPERTS_2, D_MODEL, D_EXPERT), D_MODEL ** -0.5),
        "w_up": nrm(ks[17], (DEPTH, N_EXPERTS_2, D_MODEL, D_EXPERT), D_MODEL ** -0.5),
        "w_down": nrm(ks[18], (DEPTH, N_EXPERTS_2, D_EXPERT, D_MODEL), D_EXPERT ** -0.5),
        "ws_gate": nrm(ks[19], (DEPTH, D_MODEL, D_SHARED), D_MODEL ** -0.5),
        "ws_up": nrm(ks[20], (DEPTH, D_MODEL, D_SHARED), D_MODEL ** -0.5),
        "ws_down": nrm(ks[21], (DEPTH, D_SHARED, D_MODEL), D_SHARED ** -0.5),
        "final_norm_w": 1.0 + nrm(ks[22], (D_MODEL,), 0.02),
    }

def second_block(x, c, w_ada, b_ada, norm1_w, w_in, conv_w, gdn_a_log, gdn_dt_bias, gdn_norm_w,
              hg_lb, hg_norm_w, w_out, norm2_w, w_router, router_bias, w_gate, w_up, w_down,
              ws_gate, ws_up, ws_down, final_norm_w):
    lb_all = jnp.cumsum(jax.nn.softmax(hg_lb.astype(jnp.float32), axis=0), axis=0)
    c_act = jax.nn.silu(c)
    for l in range(DEPTH):
        mod = jnp.einsum('bd,de->be', c_act, w_ada[l]) + b_ada[l]
        sh1, sc1, g1, sh2, sc2, g2 = jnp.split(mod, 6, axis=-1)
        h = rms_norm(x, norm1_w[l]) * (1.0 + sc1[:, None]) + sh1[:, None]
        x = x + g1[:, None] * token_mixer(h, w_in[l], conv_w[l], gdn_a_log[l], gdn_dt_bias[l],
                                          gdn_norm_w[l], lb_all[l], hg_norm_w[l], w_out[l])
        h = rms_norm(x, norm2_w[l]) * (1.0 + sc2[:, None]) + sh2[:, None]
        x = x + g2[:, None] * moe(h, w_router[l], router_bias[l], w_gate[l], w_up[l], w_down[l],
                                  ws_gate[l], ws_up[l], ws_down[l])
    return rms_norm(x, final_norm_w)


def setup_inputs(seed=0):
    out = dict(first_inputs(seed))
    for name, value in second_inputs(seed + 1).items():
        if name != "x":
            out[name + "_2"] = value
    return out


def reference(
    x, mix_norm_g, w_in, b_if, a_norm_g, w_a_out, conv_w, conv_b, conv_ln_g, conv_ln_b, w_b_out,
    cq_norm_g, w_uq, ckv_norm_g, w_ukv, q_norm_g, k_norm_g, w_c_out, w_out, ffn_norm_g,
    w_router, w_e_gate, w_e_up, w_e_down, c_2, w_ada_2, b_ada_2, norm1_w_2, w_in_2, conv_w_2,
    gdn_a_log_2, gdn_dt_bias_2, gdn_norm_w_2, hg_lb_2, hg_norm_w_2, w_out_2, norm2_w_2,
    w_router_2, router_bias_2, w_gate_2, w_up_2, w_down_2, ws_gate_2, ws_up_2, ws_down_2,
    final_norm_w_2,
):
    x = first_block(
        x, mix_norm_g, w_in, b_if, a_norm_g, w_a_out, conv_w, conv_b, conv_ln_g, conv_ln_b,
        w_b_out, cq_norm_g, w_uq, ckv_norm_g, w_ukv, q_norm_g, k_norm_g, w_c_out, w_out,
        ffn_norm_g, w_router, w_e_gate, w_e_up, w_e_down,
    )
    return second_block(
        x, c_2, w_ada_2, b_ada_2, norm1_w_2, w_in_2, conv_w_2, gdn_a_log_2, gdn_dt_bias_2,
        gdn_norm_w_2, hg_lb_2, hg_norm_w_2, w_out_2, norm2_w_2, w_router_2, router_bias_2,
        w_gate_2, w_up_2, w_down_2, ws_gate_2, ws_up_2, ws_down_2, final_norm_w_2,
    )


_drawn_inputs = setup_inputs


def setup_inputs(seed=0):
    import zlib

    import numpy as np

    out = dict(_drawn_inputs(seed))
    spreads = {}
    factors = {'conv_ln_b': 8.355,
     'cq_norm_g': 6.627,
     'ckv_norm_g': 3.955,
     'q_norm_g': 7.836,
     'k_norm_g': 4.671,
     'norm1_w_2': 3.488,
     'gdn_norm_w_2': 23.901,
     'hg_lb_2': 4.297,
     'hg_norm_w_2': 21.193,
     'final_norm_w_2': 8.706,
     'a_norm_g': 7.57,
     'conv_b': 5.151,
     'conv_ln_g': 8.0,
     'ffn_norm_g': 5.501,
     'norm2_w_2': 7.29,
     'router_bias_2': 5.324}
    for name, (base, spread) in spreads.items():
        noise = np.random.default_rng([zlib.crc32(name.encode()), seed]).standard_normal(out[name].shape)
        drawn = base * np.exp(spread * noise) if base else spread * noise
        out[name] = __import__('jax').numpy.asarray(drawn.astype(out[name].dtype))
    for name, factor in factors.items():
        out[name] = (out[name] * factor).astype(out[name].dtype)
    return out
```

```python
from contextlib import ExitStack

import numpy as np

import concourse.bass as bass
from concourse import mybir
from concourse.alu_op_type import AluOpType as ALU

F32 = mybir.dt.float32
ACT = mybir.ActivationFunctionType
AX = mybir.AxisListType

P = 128
S = 256
TT = S // P
D = 1024
KD = D // P
EPS = 1e-6

PC = 2048
SLOTS = 12

AH, AD = 4, 128
BW, BK = 512, 31
CH, CQK, CN, CR, CV = 8, 96, 64, 32, 64
CQR, CKR = 384, 256
E1, FF, CAP = 16, 1536, 32
GH, HH = 4, 4
CONV2 = 4
E2, DE, NG2, TOPG, TOPK = 64, 256, 8, 4, 8
ROUTE_SCALE = 2.5
LEVELS = 7

N_PIECES = 43 + 24 + 18 * E1 + 21 + 3 * (E2 + 1)

VEC = dict(mix_g=8, conv_w=124, conv_b=4, ln_g=4, ln_b=4, a_g=4, cq_g=3, ckv_g=2, qn_g=96, kn_g=96,
           b_i=1, b_f=1, ffn_g=8, router=128, c=8, b_ada=32, n1w=8, conv2_w=48, a_log=1, dt=1, og=8,
           lb0=4, lb1=4, n2w=8, router2=512, rbias=64)
CST = dict(ident=128, ones=128, tri=128, mmask=768, levels=LEVELS * 128, iota=32, gbefore=64,
           cos=32, sin=32, eps=1)


def offsets(widths):
    at, out = 0, {}
    for name, n in widths.items():
        out[name] = (at, at + n)
        at += n
    return out, at


VOFF, VN = offsets(VEC)
COFF, CN_ALL = offsets(CST)


def build(nc, x_in, stream_in, vec_in, cst_in, gbias_in, finw_in, out, order, e1_groups=E1 // 4,
          e2_groups=E2 // 4):
    ctx = ExitStack()
    with ctx:
        def sb(name, cols):
            return ctx.enter_context(nc.sbuf_tensor(name, [P, cols], F32))

        sems = {}

        def sem(name):
            if name not in sems:
                sems[name] = ctx.enter_context(nc.semaphore(name))
            return sems[name]

        ring = [sb(f"piece{i}", PC) for i in range(SLOTS)]
        x_t = sb("x_t", TT * D).ap().rearrange("p (t d) -> p t d", t=TT)
        xn_t = sb("xn_t", TT * D).ap().rearrange("p (t d) -> p t d", t=TT)
        xnT = sb("xnT", KD * S).ap().rearrange("p (k s) -> p k s", k=KD)
        vec = sb("vec", VN).ap()
        cst = sb("cst", CN_ALL).ap()
        gmod = sb("gmod", 2 * D).ap()
        small = sb("small", 256).ap()
        WORK = 16500
        work = sb("work", WORK).ap()
        bank = [ctx.enter_context(nc.psum_tensor(f"bank{i}", [P, 512], F32)).ap() for i in range(8)]

        def V(name, a=0, b=None):
            lo, hi = VOFF[name]
            return vec[:, lo + a:(hi if b is None else lo + b)]

        def C(name, a=0, b=None):
            lo, hi = COFF[name]
            return cst[:, lo + a:(hi if b is None else lo + b)]

        ident, ones, tri = C("ident"), C("ones"), C("tri")

        def cols(base, at, *dims):
            n = int(np.prod(dims))
            v = base[:, at:at + n]
            if len(dims) == 2:
                v = v.rearrange("p (a b) -> p a b", a=dims[0])
            if len(dims) == 3:
                v = v.rearrange("p (a b c) -> p a b c", a=dims[0], b=dims[1])
            if len(dims) == 4:
                v = v.rearrange("p (a b c d) -> p a b c d", a=dims[0], b=dims[1], c=dims[2])
            return v

        def spread(v, n):
            return v.unsqueeze(2).to_broadcast([v.shape[0], v.shape[1], n])

        def repeated(v, n):
            return v.unsqueeze(1).to_broadcast([v.shape[0], n, v.shape[1]])

        sq_sum = small[:, 0:2]
        rstd = small[:, 2:4]

        products = {}
        to_empty = [0] * 8
        bank_full = [sem(f"bank_full{i}") for i in range(8)]
        bank_emptied = [sem(f"bank_emptied{i}") for i in range(8)]

        fills = [0] * 8
        turns = {}

        def full(name):
            return products[name][1:]

        def was_emptied(name):
            return bank_emptied[products[name][0]], turns[name]

        def emptied(name):
            return bank_emptied[products[name][0]]

        def held(name):
            return bank[products[name][0]]

        class Steps:

            def __init__(self, eng, s):
                self.eng, self.s, self.n = eng, s, 0

            def mark(self, ins):
                ins.then_inc(self.s, 1)
                self.n += 1
                return self.n

            def settle(self, n=None):
                self.eng.wait_ge(self.s, self.n if n is None else n)

            def link(self, ins):
                self.mark(ins)
                self.settle()

        landed = [sem(f"landed{i}") for i in range(SLOTS)]
        piece_used = sem("piece_used")
        inputs_landed = sem("inputs_landed")

        flat = xn_t.rearrange("p t d -> p (t d)")
        c_t = cols(flat, 0, TT, CQR + CKR + CR)
        usq = cols(flat, 0, 4, S)
        uc = cols(gmod, 0, 4, S)
        oT = cols(gmod, 4 * S, 4, S)
        w0 = 0
        cT = cols(work, w0, 5, S)
        hT = cols(work, w0, 4, S)
        w0 += 5 * S
        fqk = cols(work, w0, 8, S)
        merged = cols(work, w0, 8, S)
        w0 += 8 * S
        v_ext = cols(work, w0, TT, AH, AD + 1)
        w0 += TT * AH * (AD + 1)
        so_t = cols(work, w0, TT, AH * AD)
        w0 += TT * AH * AD
        gsig, gtmp = cols(work, w0, 3, 512), cols(work, w0 + 1536, 2, 512)
        u_pad = cols(work, w0, 4, S + BK - 1)
        w0 += 4 * (S + BK - 1)
        sig_u = cols(work, w0, 4, S)
        qk_t = cols(work, w0, TT, 2 * CH, CQK)
        prob = [cols(work, w0 + 512 * i, TT, S) for i in range(2)]
        probT = [cols(work, w0 + 1024 + 512 * i, TT, S) for i in range(2)]
        w0 += TT * 2 * CH * CQK
        vc_t = cols(work, w0, TT, CH, CV)
        w0 += TT * CH * CV
        qkT = cols(work, w0, 2 * CH, S)
        qk_sq = cols(work, w0, TT, 2 * CH, CQK)
        junk = work[:, w0:w0 + CQR]
        warg = [work[:, w0 + 768 * i:w0 + 768 * (i + 1)] for i in range(2)]
        h_t = cols(work, w0 + 1536, TT, AH, AD)
        w0 += 2 * CH * S
        rows = {r: work[0:64, w0 + S * i:w0 + S * (i + 1)] for i, r in enumerate((0, 1, 3, 4, 5))}
        rows[2] = rows[0]
        w0 += 5 * S
        assert w0 <= WORK, w0
        ones_row = C("ones", 0, 1).to_broadcast([P, S])
        rs_c, ss_c, hss, hrs = small[:, 4:8], small[:, 8:12], small[:, 16:24], small[:, 24:32]
        qkss, qkrs, acol, fcol = small[:, 32:64], small[:, 64:96], small[:, 96:112], small[:, 112:128]
        smax, ssum, den = small[:, 128:144], small[:, 144:160], small[:, 160:162]

        w0 = 0
        onehot = cols(work, w0, TT, E1 * CAP)
        weighted = cols(work, w0 + 1024, TT, E1 * CAP)
        backT = cols(work, w0 + 2048, 4, S)
        xg = cols(work, w0 + 3072, KD, E1 * CAP)
        w0 += 3072 + KD * E1 * CAP
        xe = [cols(work, w0 + 256 * i, KD, CAP) for i in range(2)]
        back_now = work[:, w0 + 512:w0 + 768]
        gate1 = [work[0:3 * CAP, w0 + 768 + 512 * i:w0 + 1280 + 512 * i] for i in range(2)]
        hid1 = [work[0:3 * CAP, w0 + 1792 + 512 * i:w0 + 2304 + 512 * i] for i in range(2)]
        hid1T = [cols(work, w0 + 2816 + 384 * i, 4, 3, CAP) for i in range(2)]
        y_now = work[:, w0 + 3584:w0 + 4608]
        w0 += 4608
        aff = cols(work, w0, TT, E1)
        slot_t = cols(work, w0 + 32, TT, E1)
        affw, slotrow = work[0:E1, w0 + 64:w0 + 320], work[0:E1, w0 + 320:w0 + 576]
        m8 = work[0:E1, w0 + 576:w0 + 584]
        cact, modc = work[:, w0 + 584:w0 + 592], small[:, 192:224]
        mx1, sm1 = work[:, w0 + 592:w0 + 594], work[:, w0 + 594:w0 + 596]
        assert w0 + 600 <= WORK
        FB1 = FF // P

        turnedT = xnT.rearrange("p k s -> p (k s)")
        z_gate = cols(flat, 0, TT, D)
        o_t = cols(turnedT, 0, TT, D)
        oT2 = cols(flat, 0, KD, S)
        w0 = 0
        pad2 = cols(work, w0, 12, S + CONV2 - 1)
        k_t, v_t = cols(work, w0, TT * GH, P), cols(work, w0 + 1024, TT * GH, P)
        w0 += 12 * (S + CONV2 - 1)
        qkv = cols(work, w0, 12, S)
        w0 += 12 * S
        hq = cols(work, w0, HH * TT, P)
        iB = cols(work, w0 + 1024, TT * HH, P)
        AT = cols(work, w0 + 2048, HH * TT, P)
        w0 += 3072
        s0 = w0
        hsig, hk, hb, hE, hQ, hK = (cols(work, s0 + 1024 * i, HH * TT, P) for i in range(6))
        ATx = hsig[:, 0:4]
        dec, attnT, LT, Ti, Ui, Xi, Lm = (cols(work, s0 + 1024 * i, GH * TT, P) for i in range(7))
        qk_ss = cols(work, s0 + 2048, 8, S)
        grow = [work[0:GH, s0 + 6144 + S * i:s0 + 6144 + S * (i + 1)] for i in range(3)]
        vb, kbe, wT, uu = Ti, Xi[:, 0:4], Xi[:, 4:8], Lm
        S1, vnew, qd, ktail = dec[:, 0:4], dec[:, 4:8], LT[:, 0:4], LT[:, 4:8]
        assert s0 + 7168 <= WORK, s0
        egb = cols(work, 0 + 2048, GH, P)
        lb, oml, scol1 = small[:, 32:36], small[:, 36:40], small[:, 40:48]
        gcol, bcol = small[:, 48:56], small[:, 56:64]
        glast, ecol, tcol = small[:, 64:68], small[:, 68:72], small[:, 72:76]
        nexpa = small[0:GH, 76:77]
        oss, ors = small[:, 80:90], small[:, 90:100]

        hid2 = [[work[:, 512 * i + S * b:512 * i + S * (b + 1)] for b in range(2)] for i in range(2)]
        silu2 = [work[:, 1024 + S * b:1024 + S * (b + 1)] for b in range(2)]
        part2 = [work[:, 1536 + S * b:1536 + S * (b + 1)] for b in range(2)]
        gT = work[0:E2, 2048:2048 + S]
        grow2 = [work[0:E2, 2304 + S * i:2304 + S * (i + 1)] for i in range(2)]
        finw, ytmp = work[:, 3072:4096], [work[:, 4096 + 512 * i:4608 + 512 * i] for i in range(2)]
        r0 = 5120
        score, sel, msel, chosen = (cols(work, r0 + 128 * i, TT, E2) for i in range(4))
        gmax = cols(work, r0 + 512, TT * NG2, 8)
        gsum = cols(work, r0 + 640, TT, NG2)
        cmpa, cmpb = cols(work, r0 + 656, TT, NG2, NG2), cols(work, r0 + 784, TT, NG2, NG2)
        rank = cols(work, r0 + 912, TT, NG2)
        top8 = cols(work, r0 + 928, TT, TOPK)
        wsum = work[:, r0 + 944:r0 + 946]

        block = ctx.enter_context(nc.Block())

        @block.tensor
        def _(pe):
            def piece(name):
                n = len(order)
                order.append(name)
                pe.wait_ge(landed[n % SLOTS], 16 * (n // SLOTS + 1))
                return ring[n % SLOTS].ap()

            def release(ins, name=None):
                ins.then_inc(piece_used, 1)
                if name:
                    products[name] = (products[name][0], piece_used, len(order))

            def fill(name, readers=1):
                b = len(products) % 8
                products[name] = (b, bank_full[b], None)
                if to_empty[b]:
                    pe.wait_ge(bank_emptied[b], to_empty[b])
                to_empty[b] += readers
                turns[name] = to_empty[b]
                return bank[b]

            def complete(ins, name):
                b = products[name][0]
                fills[b] += 1
                products[name] = (b, bank_full[b], fills[b])
                ins.then_inc(bank_full[b], 1)

            def turn(name, blocks, readers=1):
                ps = fill(name, readers)
                for i, (src, n) in enumerate(blocks):
                    m = src.shape[1]
                    last = pe.transpose(ps[0:m, i * n:(i + 1) * n], src, ident[0:n, 0:n])
                complete(last, name)

            def token_major(name, width):
                w = cols(piece(name), 0, KD, S)
                ps = fill(name)
                for t in range(TT):
                    for k in range(KD):
                        last = pe.matmul(ps[:, t * S:t * S + width], xnT[:, k, t * P:(t + 1) * P],
                                         w[:, k, 0:width], start=(k == 0), stop=(k == KD - 1))
                release(last, name)

            def feature_major(name, blocks=2):
                w = cols(piece(name), 0, KD, S)
                ps = fill(name)
                for b in range(blocks):
                    for k in range(KD):
                        last = pe.matmul(ps[:, b * S:(b + 1) * S], w[:, k, b * P:(b + 1) * P],
                                         xnT[:, k, :], start=(k == 0), stop=(k == KD - 1))
                release(last, name)

            def turn_x(name, n):
                pe.wait_ge(sem("x_normed"), n)
                for t in range(TT):
                    for hk in range(2):
                        turn(f"{name}{t}{hk}", [(xn_t[:, t, (4 * hk + i) * P:(4 * hk + i + 1) * P], P)
                                                for i in range(4)])
                pe.wait_ge(sem("xnT_ready"), 4 * n)

            def project(name, src):
                outs = [(t, n, fill(f"{name}{t}{n}")) for t in range(TT) for n in range(2)]
                for q in range(4):
                    w = cols(piece(f"{name}{q}"), 0, 2, 1024)
                    for t, n, ps in outs:
                        for kk in range(2):
                            k = 2 * q + kk
                            last = pe.matmul(ps, src[:, k, t * P:(t + 1) * P],
                                             w[:, kk, n * 512:(n + 1) * 512],
                                             start=(k == 0), stop=(k == KD - 1))
                        if q == 3 and (t, n) != (1, 1):
                            complete(last, f"{name}{t}{n}")
                    release(last, f"{name}11" if q == 3 else None)

            def attend(h):
                pe.wait_ge(sem("probs_ready"), h + 1)
                turn(f"pT{h}", [(prob[h % 2][:, t, kb * P:(kb + 1) * P], P)
                                for kb in range(TT) for t in range(TT)])
                pe.wait_ge(sem("probsT_ready"), h + 1)
                ps = fill(f"o{h // 2}") if h % 2 == 0 else held(f"o{h // 2}")
                r = 64 * (h % 2)
                for kb in range(TT):
                    last = pe.matmul(ps[r:r + 64, 0:S], vc_t[:, kb, h, :], probT[h % 2][:, kb, :],
                                     start=(kb == 0), stop=(kb == TT - 1))
                if h % 2:
                    complete(last, f"o{h // 2}")

            def memory(h):
                pe.wait_ge(sem("weights_ready"), h + 1)
                w = warg[h % 2]
                parts = {0: [[(0, 0)], [(128, 0), (256, 1)]], 1: [[(384, 0), (512, 1)], [(640, 1)]]}
                for d in range(2):
                    ps = fill(f"mem{h}{d}")
                    for t in range(TT):
                        for n, (c, kt) in enumerate(parts[d][t]):
                            last = pe.matmul(ps[:, t * (AD + 1):(t + 1) * (AD + 1)], w[:, c:c + P],
                                             v_ext[:, kt, h, :], start=(n == 0),
                                             stop=(n == len(parts[d][t]) - 1))
                    complete(last, f"mem{h}{d}")

            pe.wait_ge(inputs_landed, 48)
            turn_x("xT", 1)
            w = cols(piece("F0"), 0, KD, S)
            ps = fill("gates_a")
            for half in range(2):
                for k in range(KD):
                    last = pe.matmul(ps[0:64, half * S:(half + 1) * S],
                                     w[:, k, half * 64:half * 64 + 64], xnT[:, k, :],
                                     start=(k == 0), stop=(k == KD - 1))
            release(last, "gates_a")
            for i in range(1, 5):
                feature_major(f"F{i}")
            for i, n in enumerate((256, 256, 160)):
                token_major(f"lat{i}", n)
            for i in range(5, 9):
                feature_major(f"F{i}")
            for i in range(4):
                token_major(f"vo{i}", 256)

            pe.wait_ge(sem("latents_normed"), 1)
            for t in range(TT):
                turn(f"cqT{t}", [(c_t[:, t, i * P:(i + 1) * P], P) for i in range(3)])
                turn(f"ckvT{t}", [(c_t[:, t, CQR + i * P:CQR + (i + 1) * P], P) for i in range(2)])
            pe.wait_ge(sem("latentsT_ready"), 4)
            for half in range(2):
                w = cols(piece(f"uq{half}"), 0, 3, 384)
                for t in range(TT):
                    ps = fill(f"uq{t}{half}")
                    for k in range(3):
                        last = pe.matmul(ps[:, 0:384], cT[:, k, t * P:(t + 1) * P], w[:, k, :],
                                         start=(k == 0), stop=(k == 2))
                    (complete if t == 0 else release)(last, f"uq{t}{half}")
            w = cols(piece("ukv"), 0, 2, 1024)
            for t in range(TT):
                for half in range(2):
                    ps = fill(f"ukv{t}{half}")
                    for k in range(2):
                        last = pe.matmul(ps, cT[:, 3 + k, t * P:(t + 1) * P],
                                         w[:, k, half * 512:(half + 1) * 512],
                                         start=(k == 0), stop=(k == 1))
                    (release if t and half else complete)(last, f"ukv{t}{half}")

            pe.wait_ge(sem("conv_done"), 1)
            ps = fill("conv_sum")
            for j in range(4):
                last = pe.matmul(ps[:, 0:S], ones, uc[:, j, :], start=(j == 0), stop=(j == 3))
            complete(last, "conv_sum")
            pe.wait_ge(sem("conv_squared"), 1)
            ps = fill("conv_var")
            for j in range(4):
                last = pe.matmul(ps[:, 0:S], ones, usq[:, j, :], start=(j == 0), stop=(j == 3))
            complete(last, "conv_var")

            pe.wait_ge(sem("heads_roped"), 1)
            for g in range(4):
                for t in range(TT):
                    turn(f"hT{g}{t}", [(qk_t[:, t, 4 * g + i, :], P) for i in range(4)])
            pe.wait_ge(sem("headsT_ready"), 8)
            for h in range(CH):
                ps = fill(f"sc{h}")
                for t in range(TT):
                    last = pe.matmul(ps[:, t * S:(t + 1) * S], qkT[0:CQK, h, t * P:(t + 1) * P],
                                     qkT[0:CQK, CH + h, :], start=True, stop=True)
                complete(last, f"sc{h}")
                if h:
                    attend(h - 1)
            attend(CH - 1)

            pe.wait_ge(sem("gate_rows"), 1)
            ps = fill("gate_cols")
            for i, r in enumerate((2, 4)):
                for t in range(TT):
                    last = pe.transpose(ps[:, (2 * i + t) * 64:(2 * i + t + 1) * 64],
                                        rows[r][:, t * P:(t + 1) * P], ident[0:64, 0:64])
            complete(last, "gate_cols")
            for h in range(AH):
                ps = fill(f"negA{h}")
                for d in range(2):
                    last = pe.matmul(ps[:, d * S:(d + 1) * S],
                                     ident[0:64, 32 * d + h:32 * d + h + 1].to_broadcast([64, P]),
                                     rows[3], start=True, stop=True)
                complete(last, f"negA{h}")
                ps = fill(f"kq{h}")
                for t in range(TT):
                    last = pe.matmul(ps[:, t * S:(t + 1) * S], fqk[:, 2 * h + 1, t * P:(t + 1) * P],
                                     fqk[:, 2 * h, :], start=True, stop=True)
                complete(last, f"kq{h}")
                if h:
                    memory(h - 1)
            memory(AH - 1)
            pe.wait_ge(sem("memory_normed"), 1)
            for t in range(TT):
                turn(f"memT{t}", [(h_t[:, t, h, :], P) for h in range(AH)])

            for j in range(4):
                for i in range(3):
                    feature_major(f"g{j}{i}")
                if j == 0:
                    pe.wait_ge(sem("conv_out"), 1)
                    pe.wait_ge(sem("memT_ready"), 2)
                    pe.wait_ge(sem("oT_ready"), 4)
                for i in range(3):
                    if i != 1:
                        wy = piece(f"y{j}{i}")
                    w = cols(wy, 1024 * (i % 2), 4, S)
                    src = (hT, uc, oT)[i]
                    ps = fill(f"y{j}{i}_")
                    for b in range(2):
                        for k in range(4):
                            last = pe.matmul(ps[:, b * S:(b + 1) * S], w[:, k, b * P:(b + 1) * P],
                                             src[:, k, :], start=(k == 0), stop=(k == 3))
                    (release if i else complete)(last, f"y{j}{i}_")
            pe.wait_ge(sem("merged_ready"), 4)
            project("wo", merged)

            turn_x("xU", 2)
            ps = fill("router")
            for t in range(TT):
                for k in range(KD):
                    last = pe.matmul(ps[:, t * E1:(t + 1) * E1], xnT[:, k, t * P:(t + 1) * P],
                                     V("router", k * E1, (k + 1) * E1), start=(k == 0), stop=(k == KD - 1))
            complete(last, "router")
            pe.wait_ge(sem("c_ready"), 1)
            ps = fill("mod_cols")
            for n in range(16):
                w = cols(piece(f"ada{n}"), 0, KD, S)
                for b in range(2):
                    for k in range(KD):
                        last = pe.matmul(ps[:, 2 * n + b:2 * n + b + 1], w[:, k, b * P:(b + 1) * P],
                                         cact[:, k:k + 1], start=(k == 0), stop=(k == KD - 1))
                release(last, "mod_cols" if n == 15 else None)
            pe.wait_ge(sem("affinity_ready"), 1)
            turn("affT", [(aff[:, t, :], P) for t in range(TT)])
            for n in range(16, 24):
                w = cols(piece(f"ada{n}"), 0, KD, S)
                ps = fill(f"gmod{n - 16}")
                for k in range(KD):
                    last = pe.matmul(ps[:, 0:S], cact[:, k:k + 1].to_broadcast([P, P]), w[:, k, :],
                                     start=(k == 0), stop=(k == KD - 1))
                release(last, f"gmod{n - 16}")
            pe.wait_ge(sem("slot_rows"), 1)
            turn("slotT", [(slotrow[:, t * P:(t + 1) * P], E1) for t in range(TT)])
            pe.wait_ge(sem("onehot_ready"), 1)
            for k in range(KD):
                ps = fill(f"xg{k}")
                for t in range(TT):
                    last = pe.matmul(ps, xn_t[:, t, k * P:(k + 1) * P], onehot[:, t, :],
                                     start=(t == 0), stop=(t == TT - 1))
                complete(last, f"xg{k}")
            pe.wait_ge(sem("weighted_ready"), 1)
            for t in range(TT):
                turn(f"backT{t}", [(weighted[:, t, g * P:(g + 1) * P], P) for g in range(4)])

            def drain_banks():
                for b in range(8):
                    pe.wait_ge(bank_emptied[b], to_empty[b])

            def piece_in_loop(n, it, rounds):
                pe.wait_ge(landed[n % SLOTS], it * (16 * rounds) + 16 * (n // SLOTS + 1))
                return ring[n % SLOTS].ap()

            drain_banks()
            first1 = len(order)

            pe.nop().then_inc(sem("scattered"), 1)

            def gate_up(n, it, e, i):
                pe.wait_ge(sem("tokens_loaded"), e + 1)
                if i is not None:
                    pe.wait_ge(sem("gated"), e)
                i = i or 0
                for p in range(12):
                    if p == 6 and n != first1:
                        turn_hidden(it, e - 1, i - 1)
                    w = cols(piece_in_loop(n + p, it, 6), 0, 4, 512)
                    for c in range(4):
                        k, m, t = (4 * p + c) // 6, (4 * p + c) // 3 % 2, (4 * p + c) % 3
                        last = pe.matmul(bank[2 * m + i % 2][CAP * t:CAP * (t + 1), :], xe[i % 2][:, k, :],
                                         w[:, c, :], start=(k == 0), stop=(k == KD - 1))
                    last.then_inc(piece_used, 1)

            def turn_hidden(it, e, j):
                pe.wait_ge(sem("gated"), e + 2)
                if j == 0:
                    pe.wait_ge(sem("scatter_read"), it * 4 + 1)
                for c in range(4):
                    last = pe.transpose(bank[7][:, 3 * CAP * c:3 * CAP * (c + 1)],
                                        hid1[j % 2][:, c * P:(c + 1) * P], ident[0:3 * CAP, 0:3 * CAP])
                last.then_inc(sem("hidden_turned"), 1)

            def down(n, it, e, j):
                pe.wait_ge(sem("hiddenT_ready"), e + 1)
                for q in range(6):
                    w = cols(piece_in_loop(n + q, it, 6), 0, 2, 1024)
                    for ff in range(2):
                        f = 2 * q + ff
                        for half in range(2):
                            last = pe.matmul(bank[4 + half][CAP * j:CAP * (j + 1), :],
                                             hid1T[j % 2][:, f % 4, f // 4, :],
                                             w[:, ff, half * 512:(half + 1) * 512],
                                             start=(f == 0), stop=(f == FB1 - 1))
                    last.then_inc(piece_used, 1)

            def group1(it, last_group):
                n = first1 + 12
                for j in range(4):
                    if last_group and j == 3:
                        turn_hidden(it, it * 4 + j, j)
                    else:
                        gate_up(n, it, it * 4 + (j + 1), j + 1)
                        n += 12
                    if j == 0:
                        pe.wait_ge(sem("outputs_read"), it + 1)
                    down(n, it, it * 4 + j, j)
                    n += 6
                pe.wait_ge(sem("outputs_read"), it + 2)
                pe.wait_ge(sem("back_loaded"), it + 1)
                for i in range(4):
                    t, half = divmod(i, 2)
                    pe.wait_ge(sem("scatter_read"), it * 4 + max(i, 1))
                    pe.matmul(bank[6 + i % 2], back_now[:, t * P:(t + 1) * P],
                              y_now[:, half * 512:(half + 1) * 512], start=True,
                              stop=True).then_inc(sem("scattered"), 1)

            for e in range(4 * e1_groups + 1):
                if e < 4 * e1_groups:
                    order.extend(f"e{e}gu{p}" for p in range(12))
                if e:
                    order.extend(f"e{e - 1}d{q}" for q in range(6))
            gate_up(first1, 0, 0, None)
            if e1_groups > 1:
                with pe.Fori(0, e1_groups - 1) as it:
                    group1(it, False)
            group1(e1_groups - 1, True)
            pe.wait_ge(sem("scatter_read"), 4 * e1_groups + 1)

            turn_x("xV", 3)
            w = cols(piece("S0"), 0, KD, S)
            ps = fill("rows2")
            for half in range(2):
                for k in range(KD):
                    last = pe.matmul(ps[0:32, half * S:(half + 1) * S], w[:, k, half * 32:half * 32 + 32],
                                     xnT[:, k, :], start=(k == 0), stop=(k == KD - 1))
            release(last, "rows2")
            for i in range(1, 5):
                feature_major(f"S{i}")
            for i in range(2):
                token_major(f"U{i}", S)

            def weighted_keys(n):
                if n:
                    pe.wait_ge(sem("level_ready"), n)
                kk, qq = (hk, hq) if n == 0 else (hK, hQ)
                if n == 0:
                    pe.wait_ge(sem("hk_ready"), 1)
                if n == 1:
                    ps = fill("hx")
                    for h in range(HH):
                        last = pe.matmul(ps[:, h * P:(h + 1) * P], kk[:, 2 * h, :], qq[:, 2 * h + 1, :],
                                         start=True, stop=True)
                    complete(last, "hx")
                    return
                for half in range(2):
                    ps = fill(f"hl{n}{half}")
                    for i in range(4):
                        last = pe.matmul(ps[:, i * P:(i + 1) * P], kk[:, 4 * half + i, :],
                                         qq[:, 4 * half + i, :], start=True, stop=True)
                    complete(last, f"hl{n}{half}")

            for i in range(5, 11):
                feature_major(f"S{i}")
                if i >= 6:
                    weighted_keys(i - 6)
            for i in range(2, 6):
                token_major(f"U{i}", S)
                weighted_keys(i + 3)
            pe.wait_ge(sem("g_rows"), 1)
            ps = fill("gcols")
            for i, r in enumerate((2, 0)):
                for t in range(TT):
                    last = pe.transpose(ps[:, (2 * i + t) * GH:(2 * i + t + 1) * GH],
                                        grow[r][:, t * P:(t + 1) * P], ident[0:GH, 0:GH])
            complete(last, "gcols")
            pe.wait_ge(sem("AT_ready"), 1)
            for t in range(TT):
                ps = fill(f"oB{t}")
                for h in range(HH):
                    last = pe.matmul(ps[:, h * P:(h + 1) * P], AT[:, 2 * h + t, :], iB[:, 4 * t + h, :],
                                     start=True, stop=(t == 0))
                    if t:
                        last = pe.matmul(ps[:, h * P:(h + 1) * P], ATx[:, h, :], iB[:, h, :],
                                         start=False, stop=True)
                complete(last, f"oB{t}")
            for h in range(GH):
                ps = fill(f"bc{h}")
                for i, r in enumerate((2, 0)):
                    last = pe.matmul(ps[:, i * S:(i + 1) * S], ident[0:GH, h:h + 1].to_broadcast([GH, P]),
                                     grow[r], start=True, stop=True)
                complete(last, f"bc{h}")
            pe.wait_ge(sem("qk_squared"), 1)
            for i in range(4):
                ps = fill(f"l2{i}")
                for b in range(2):
                    last = pe.matmul(ps[:, b * S:(b + 1) * S], ones, qk_ss[:, 2 * i + b, :],
                                     start=True, stop=True)
                complete(last, f"l2{i}")
            pe.wait_ge(sem("qk_unit"), 1)
            for h in range(GH):
                ps = fill(f"kk{h}")
                q, k = qkv[:, h, :], qkv[:, 4 + h, :]
                for t in range(TT):
                    tile = slice(t * P, (t + 1) * P)
                    pe.matmul(ps[:, t * P:(t + 1) * P], k[:, tile], k[:, tile], start=True, stop=True)
                    last = pe.matmul(ps[:, S + t * P:S + (t + 1) * P], k[:, tile], q[:, tile],
                                     start=True, stop=True)
                complete(last, f"kk{h}")
            for t in range(TT):
                for n, b0 in (("kt", 4), ("vt", 8)):
                    turn(f"{n}{t}", [(qkv[:, b0 + h, t * P:(t + 1) * P], P) for h in range(GH)])
            for half in range(2):
                pe.wait_ge(sem("U_ready"), half + 1)
                turn(f"T0{half}", [(Ui[:, 4 * half + i, :], P) for i in range(4)])
            for n in range(1, LEVELS):
                for half in range(2):
                    pe.wait_ge(sem("T_ready"), 2 * (n - 1) + half + 1)
                    pe.wait_ge(sem("Lm_ready"), 2 * (n - 1) + half + 1)
                    ps = fill(f"X{n}{half}")
                    for i in range(4 * half, 4 * half + 4):
                        last = pe.matmul(ps[:, (i % 4) * P:(i % 4 + 1) * P], Lm[:, i, :], Ti[:, i, :],
                                         start=True, stop=True)
                    complete(last, f"X{n}{half}")
                for half in range(2):
                    pe.wait_ge(sem("X_ready"), 2 * (n - 1) + half + 1)
                    pe.wait_ge(sem("U_ready"), 2 * n + half - 1 if n > 1 else half + 1)
                    if n < LEVELS - 1:
                        ps = fill(f"TX{n}{half}")
                        for i in range(4 * half, 4 * half + 4):
                            last = pe.matmul(ps[:, (i % 4) * P:(i % 4 + 1) * P], Ui[:, i, :], Xi[:, i, :],
                                             start=True, stop=True)
                        complete(last, f"TX{n}{half}")
                    ps = fill(f"XU{n}{half}")
                    for i in range(4 * half, 4 * half + 4):
                        last = pe.matmul(ps[:, (i % 4) * P:(i % 4 + 1) * P], Xi[:, i, :], Ui[:, i, :],
                                         start=True, stop=True)
                    complete(last, f"XU{n}{half}")
            pe.wait_ge(sem("U_ready"), 2 * LEVELS)
            pe.wait_ge(sem("vb_ready"), 1)

            def per_head(name, terms):
                ps = fill(name)
                for h in range(GH):
                    pairs = terms(h)
                    for n, (l, r) in enumerate(pairs):
                        last = pe.matmul(ps[:, h * P:(h + 1) * P], l, r, start=(n == 0),
                                         stop=(n == len(pairs) - 1))
                complete(last, name)

            for t in range(TT):
                per_head(f"u{t}", lambda h: [(Ui[:, 2 * h + t, :], vb[:, 4 * t + h, :])])
            per_head("wT", lambda h: [(kbe[:, h, :], Ui[:, 2 * h + 1, :])])
            pe.wait_ge(sem("u_ready"), 2)
            per_head("state", lambda h: [(ktail[:, h, :], uu[:, h, :])])
            per_head("oA0", lambda h: [(attnT[:, 2 * h, :], uu[:, h, :])])
            pe.wait_ge(sem("S1_ready"), 1)
            per_head("wS", lambda h: [(wT[:, h, :], S1[:, h, :])])
            pe.wait_ge(sem("vnew_ready"), 1)
            per_head("oA1", lambda h: [(qd[:, h, :], S1[:, h, :]), (attnT[:, 2 * h + 1, :], vnew[:, h, :])])
            pe.wait_ge(sem("o_ready"), 1)
            for t in range(TT):
                for half in range(2):
                    turn(f"oo{t}{half}", [(o_t[:, t, (4 * half + i) * P:(4 * half + i + 1) * P], P)
                                          for i in range(4)])
            pe.wait_ge(sem("oT2_ready"), 4)
            project("wp", oT2)

            turn_x("xW", 4)
            ps = fill("router2")
            for t in range(TT):
                for k in range(KD):
                    last = pe.matmul(ps[:, t * E2:(t + 1) * E2], xnT[:, k, t * P:(t + 1) * P],
                                     V("router2", k * E2, (k + 1) * E2), start=(k == 0), stop=(k == KD - 1))
            complete(last, "router2")
            pe.wait_ge(sem("gates2_ready"), 1)
            turn("gT", [(chosen[:, t, :], P) for t in range(TT)])
            drain_banks()
            first2 = len(order)
            order.extend(["r64a", "r64b", "r0a", "r64d", "r0b"])
            for e in range(4 * e2_groups):
                if e + 1 < 4 * e2_groups:
                    order.append(f"r{e + 1}a")
                order.append(f"r{e}d")
                if e + 1 < 4 * e2_groups:
                    order.append(f"r{e + 1}b")

            def gate_up2(n, it, b):
                w = cols(piece_in_loop(n, it, 1), 0, KD, S)
                for m in range(2):
                    for k in range(KD):
                        last = pe.matmul(bank[b][:, m * S:(m + 1) * S], w[:, k, m * P:(m + 1) * P],
                                         xnT[:, k, :], start=(k == 0), stop=(k == KD - 1))
                last.then_inc(piece_used, 1)

            pe.nop().then_inc(sem("gate_spread"), 1)

            def spread_gate(e, i):
                pe.wait_ge(sem("gate_row"), e)
                pe.matmul(bank[2 + i % 2][:, 0:S], ones[0:E2], grow2[i % 2], start=True,
                          stop=True).then_inc(sem("gate_spread"), 1)

            def down2(n, it, i, first=False, final=False):
                w = cols(piece_in_loop(n, it, 1), 0, 2, 1024)
                for b in range(2):
                    for t in range(TT):
                        for half in range(2):
                            last = pe.matmul(bank[4 + 2 * t + half], hid2[i % 2][b][:, t * P:(t + 1) * P],
                                             w[:, b, half * 512:(half + 1) * 512],
                                             start=(first and b == 0), stop=(final and b == 1))
                last.then_inc(piece_used, 1)

            def group2(it, last_group):
                n = first2 + 5
                for i in range(1, 5):
                    e = it * 4 + i
                    more = not (last_group and i == 4)
                    if more:
                        pe.wait_ge(sem("hidden2"), e * 2 + 1)
                        spread_gate(e + 1, i + 1)
                        gate_up2(n, it, 0)
                        n += 1
                    pe.wait_ge(sem("hidden2"), e * 2 + 2)
                    down2(n, it, i, final=not more)
                    n += 1
                    if more:
                        gate_up2(n, it, 1)
                        n += 1

            gate_up2(first2, 0, 0)
            gate_up2(first2 + 1, 0, 1)
            pe.wait_ge(sem("hidden2"), 1)
            spread_gate(1, 1)
            gate_up2(first2 + 2, 0, 0)
            pe.wait_ge(sem("hidden2"), 2)
            down2(first2 + 3, 0, 0, first=True)
            gate_up2(first2 + 4, 0, 1)
            if e2_groups > 1:
                with pe.Fori(0, e2_groups - 1) as it:
                    group2(it, False)
            group2(e2_groups - 1, True)

        @block.scalar
        def _(act):
            steps = Steps(act, sem("scalar_steps"))
            act.wait_ge(inputs_landed, 48)

            def inverse_root(out_, in_, n):
                steps.link(act.activation(out_, in_, ACT.Ln, scale=1.0 / n,
                                          bias=C("eps")[0:in_.shape[0]]))
                return act.activation(out_, out_, ACT.Exp, scale=-0.5)

            def square_sums(n):
                for t in range(TT):
                    steps.mark(act.activation(xn_t[:, t, :], x_t[:, t, :], ACT.Square,
                                              accum_out=sq_sum[:, t:t + 1]))
                steps.settle()
                inverse_root(rstd, sq_sum, D).then_inc(sem("rstd_ready"), 1)

            act.preload_act_table_set("natural_log_exp_and_others")
            square_sums(1)
            act.preload_act_table_set("sigmoid_and_others")
            for j in range(4):
                act.wait_ge(*full(f"F{j + 1}"))
                act.activation(sig_u[:, j, :], held(f"F{j + 1}")[:, S:2 * S],
                               ACT.Sigmoid).then_inc(sem("glu_gate"), 1)
            act.wait_ge(sem("xnT_ready"), 4)
            for i, n in enumerate((256, 256, 160)):
                act.wait_ge(*full(f"lat{i}"))
                act.activation(c_t[:, :, 256 * i:256 * i + n], cols(held(f"lat{i}"), 0, TT, S)[:, :, 0:n],
                               ACT.Copy).then_inc(emptied(f"lat{i}"), 1)
            for i in range(3):
                act.wait_ge(*was_emptied(f"lat{i}"))
            for t in range(TT):
                for i, (a, b) in enumerate(((0, CQR), (CQR, CQR + CKR))):
                    steps.mark(act.activation(junk[:, 0:b - a], c_t[:, t, a:b], ACT.Square,
                                              accum_out=ss_c[:, 2 * i + t:2 * i + t + 1]))
                    steps.settle()
            for h in range(AH):
                act.wait_ge(*full(f"F{h + 5}"))
                act.activation(fqk[:, 2 * h:2 * h + 2, :], cols(held(f"F{h + 5}"), 0, 2, S),
                               ACT.Copy).then_inc(emptied(f"F{h + 5}"), 1)
            for i in range(2):
                act.wait_ge(*full(f"vo{i}"))
                for t in range(TT):
                    ins = act.activation(v_ext[:, t, 2 * i:2 * i + 2, 0:AD],
                                         cols(held(f"vo{i}"), t * S, 2, AD), ACT.Copy)
                ins.then_inc(emptied(f"vo{i}"), 1)
            for i in range(2):
                act.wait_ge(*full(f"vo{i + 2}"))
                act.activation(so_t[:, :, S * i:S * (i + 1)], cols(held(f"vo{i + 2}"), 0, TT, S),
                               ACT.Sigmoid).then_inc(emptied(f"vo{i + 2}"), 1)
            act.preload_act_table_set("natural_log_exp_and_others")
            steps.mark(inverse_root(rs_c[:, 0:2], ss_c[:, 0:2], CQR))
            steps.mark(inverse_root(rs_c[:, 2:4], ss_c[:, 2:4], CKR))
            steps.settle()
            for t in range(TT):
                for i, (a, b) in enumerate(((0, CQR), (CQR, CQR + CKR))):
                    n = steps.mark(act.activation(c_t[:, t, a:b], c_t[:, t, a:b], ACT.Copy,
                                                  scale=rs_c[:, 2 * i + t:2 * i + t + 1]))
            steps.settle()
            act.nop().then_inc(sem("latents_normed"), 1)

            act.wait_ge(sem("forget_abs"), 1)
            steps.link(act.activation(rows[4], rows[4], ACT.Exp, scale=-1.0))
            act.activation(rows[4], rows[4], ACT.Ln, bias=1.0).then_inc(sem("forget_log"), 1)

            for half in range(2):
                for t in range(TT):
                    act.wait_ge(*full(f"uq{t}{half}"))
                    act.activation(qk_t[:, t, 4 * half:4 * half + 4, :],
                                   cols(held(f"uq{t}{half}"), 0, 4, CQK),
                                   ACT.Copy).then_inc(emptied(f"uq{t}{half}"), 1)
            for t in range(TT):
                steps.mark(act.activation(
                    qk_t[:, t, CH:2 * CH, CN:CQK],
                    c_t[:, t, CQR + CKR:CQR + CKR + CR].unsqueeze(1).to_broadcast([P, CH, CR]), ACT.Copy))
            for t in range(TT):
                for half in range(2):
                    act.wait_ge(*full(f"ukv{t}{half}"))
                    kv = cols(held(f"ukv{t}{half}"), 0, 4, CN + CV)
                    steps.mark(act.activation(qk_t[:, t, CH + 4 * half:CH + 4 * half + 4, 0:CN],
                                              kv[:, :, 0:CN], ACT.Copy))
                    act.activation(vc_t[:, t, 4 * half:4 * half + 4, :], kv[:, :, CN:CN + CV],
                                   ACT.Copy).then_inc(emptied(f"ukv{t}{half}"), 1)
            steps.settle()
            for half in range(2):
                for t in range(TT):
                    act.wait_ge(*was_emptied(f"uq{t}{half}"))
            act.activation(qk_sq, qk_t, ACT.Square).then_inc(sem("heads_squared"), 1)
            act.wait_ge(sem("head_sums"), 1)
            inverse_root(qkrs, qkss, CQK).then_inc(sem("head_rstd"), 1)
            act.wait_ge(sem("conv_centred"), 1)
            act.activation(usq, uc, ACT.Square).then_inc(sem("conv_squared"), 1)
            act.wait_ge(*full("conv_var"))
            steps.link(act.activation(usq[:, 0, :], held("conv_var")[:, 0:S], ACT.Ln, scale=1.0 / BW,
                                      bias=C("eps")))
            steps.link(act.activation(usq[:, 0, :], usq[:, 0, :], ACT.Exp, scale=-0.5))
            act.nop().then_inc(emptied("conv_var"), 1)
            act.nop().then_inc(sem("conv_rstd"), 1)
            for g in range(4):
                for t in range(TT):
                    act.wait_ge(*full(f"hT{g}{t}"))
                    ins = act.activation(qkT[0:CQK, 4 * g:4 * g + 4, t * P:(t + 1) * P],
                                         cols(held(f"hT{g}{t}"), 0, 4, P)[0:CQK], ACT.Copy)
                    ins.then_inc(emptied(f"hT{g}{t}"), 1)
            for g in range(4):
                for t in range(TT):
                    act.wait_ge(*was_emptied(f"hT{g}{t}"))
            act.nop().then_inc(sem("headsT_ready"), 8)

            def read_attention(h):
                act.wait_ge(*full(f"pT{h}"))
                if h >= 2:
                    act.wait_ge(*full(f"o{h // 2 - 1}"))
                steps.link(act.activation(probT[h % 2].rearrange("p t s -> p (t s)"), held(f"pT{h}"),
                                          ACT.Copy))
                act.nop().then_inc(emptied(f"pT{h}"), 1)
                act.nop().then_inc(sem("probsT_ready"), 1)
                if h % 2:
                    act.wait_ge(*full(f"o{h // 2}"))
                    steps.link(act.activation(oT[:, h // 2, :], held(f"o{h // 2}")[:, 0:S], ACT.Copy))
                    act.nop().then_inc(emptied(f"o{h // 2}"), 1)
                    act.nop().then_inc(sem("oT_ready"), 1)

            for h in range(CH):
                act.wait_ge(sem("score_max"), h + 1)
                for t in range(TT):
                    i = 2 * h + t
                    ins = act.activation(prob[h % 2][:, t, :], held(f"sc{h}")[:, t * S:(t + 1) * S],
                                         ACT.Exp, scale=CQK ** -0.5, bias=smax[:, i:i + 1],
                                         accum_out=ssum[:, i:i + 1])
                    steps.mark(ins)
                steps.settle()
                act.nop().then_inc(emptied(f"sc{h}"), 1)
                act.nop().then_inc(sem("probs_summed"), 1)
                if h:
                    read_attention(h - 1)
            read_attention(CH - 1)

            act.wait_ge(sem("floor_rows"), 1)
            act.activation(rows[4], rows[4], ACT.Exp, scale=-1.0).then_inc(sem("gate_rows"), 1)
            for h in range(AH):
                act.wait_ge(sem("weight_args"), h + 1)
                act.activation(warg[h % 2], warg[h % 2], ACT.Exp).then_inc(sem("weight_exps"), 1)
            act.wait_ge(sem("memory_sums"), 1)
            inverse_root(hrs, hss, AD).then_inc(sem("memory_rstd"), 1)

            act.preload_act_table_set("sigmoid_and_others")
            act.wait_ge(sem("conv_affine"), 1)
            act.activation(usq, uc, ACT.Sigmoid).then_inc(sem("conv_sig"), 1)
            for j in range(4):
                for i in range(3):
                    act.wait_ge(*full(f"g{j}{i}"))
                    if j:
                        act.wait_ge(sem("merged_ready"), j)
                    steps.link(act.activation(gsig[:, i, :], held(f"g{j}{i}"), ACT.Sigmoid))
                    act.nop().then_inc(emptied(f"g{j}{i}"), 1)
                    act.nop().then_inc(sem("branch_gate"), 1)

            act.wait_ge(sem("x_updated"), 1)
            act.dma_start(gmod, gbias_in).then_inc(sem("gate_bias_landed"), 16)
            act.preload_act_table_set("silu_and_others")
            act.activation(cact, V("c"), ACT.Silu).then_inc(sem("c_ready"), 1)
            act.preload_act_table_set("natural_log_exp_and_others")
            square_sums(2)
            act.wait_ge(sem("logits_shifted"), 1)
            act.activation(aff, aff, ACT.Exp).then_inc(sem("affinity_exp"), 1)
            for k in range(1, KD, 2):
                act.wait_ge(*full(f"xg{k}"))
                steps.link(act.activation(xg[:, k, :], held(f"xg{k}"), ACT.Copy,
                                          scale=V("ffn_g", k, k + 1)))
                act.nop().then_inc(emptied(f"xg{k}"), 1)
                act.nop().then_inc(sem("xg_read"), 1)
            for t in range(TT):
                act.wait_ge(*full(f"backT{t}"))
                steps.link(act.activation(backT[:, :, t * P:(t + 1) * P], cols(held(f"backT{t}"), 0, 4, P),
                                          ACT.Copy))
                act.nop().then_inc(emptied(f"backT{t}"), 1)
                act.nop().then_inc(sem("back_ready"), 1)
            act.preload_act_table_set("silu_and_others")
            first1 = order.index("e0gu0")

            act.nop().then_inc(sem("outputs_read"), 1)

            def gate_of(it, j):
                done = first1 + 12 if j == 0 else it * 72 + (first1 + 6 + 18 * j)
                act.wait_ge(piece_used, done)
                if j:
                    act.wait_ge(sem("gated"), it * 4 + j)
                act.activation(gate1[j % 2], bank[j % 2][0:3 * CAP, :],
                               ACT.Silu).then_inc(sem("gate_silu"), 1)

            def outputs_of(it, last_group):
                act.wait_ge(piece_used, it * 72 + (first1 + (72 if last_group else 84)))
                act.wait_ge(sem("scattered"), it * 4 + 1)
                for half in range(2):
                    ins = act.activation(y_now[:, half * 512:(half + 1) * 512], bank[4 + half], ACT.Copy)
                ins.then_inc(sem("outputs_read"), 1)

            gate_of(0, 0)
            if e1_groups > 1:
                with act.Fori(0, e1_groups - 1) as it:
                    for j in range(1, 5):
                        gate_of(it, j)
                    outputs_of(it, False)
            for j in range(1, 4):
                gate_of(e1_groups - 1, j)
            outputs_of(e1_groups - 1, True)

            def read(name, out_, width=512, func=ACT.Copy, **kw):
                act.wait_ge(*full(name))
                n = out_.shape[0]
                act.activation(out_, held(name)[0:n, 0:width], func, **kw).then_inc(emptied(name), 1)

            def put(name, out_, **kw):
                read(name, out_, **kw)
                act.wait_ge(*was_emptied(name))

            def wide(v):
                return v.rearrange("p a b -> p (a b)")

            act.wait_ge(sem("scatter_read"), 4 * e1_groups + 1)
            act.preload_act_table_set("natural_log_exp_and_others")
            square_sums(3)
            act.activation(nexpa, V("a_log")[0:GH], ACT.Exp).then_inc(sem("decay_rate"), 1)
            act.preload_act_table_set("sigmoid_and_others")
            act.wait_ge(sem("lb_diff"), 1)
            act.activation(lb, lb, ACT.Sigmoid).then_inc(sem("lb_ready"), 1)
            act.wait_ge(*full("rows2"))
            act.activation(grow[0], held("rows2")[0:GH, 0:S], ACT.Sigmoid)
            act.activation(grow[1], held("rows2")[0:GH, S:2 * S], ACT.Identity,
                           bias=V("dt")[0:GH]).then_inc(emptied("rows2"), 1)
            for i in range(2):
                act.wait_ge(*full(f"S{i + 1}"))
                steps.mark(act.activation(wide(hsig)[:, 512 * i:512 * (i + 1)], held(f"S{i + 1}"), ACT.Sigmoid))
                read(f"S{i + 1}", wide(hk)[:, 512 * i:512 * (i + 1)], func=ACT.Sigmoid, scale=-1.0)
            for i in range(2):
                act.wait_ge(*was_emptied(f"S{i + 1}"))
            act.nop().then_inc(sem("keep_sig"), 1)
            act.preload_act_table_set("silu_and_others")
            for i in range(2):
                put(f"S{i + 3}", wide(hq)[:, 512 * i:512 * (i + 1)], func=ACT.Silu)
            act.nop().then_inc(sem("hq_ready"), 1)
            for i in range(2):
                act.wait_ge(*full(f"U{i}"))
                for t in range(TT):
                    ins = act.activation(iB[:, 4 * t + 2 * i:4 * t + 2 * i + 2, :],
                                         cols(held(f"U{i}"), t * S, 2, P), ACT.Copy)
                ins.then_inc(emptied(f"U{i}"), 1)
            act.preload_act_table_set("natural_log_exp_and_others")
            steps.settle()
            act.wait_ge(sem("oml_ready"), 1)
            for h in range(HH):
                steps.mark(act.activation(hb[:, 2 * h:2 * h + 2, :], hsig[:, 2 * h:2 * h + 2, :], ACT.Ln,
                                          scale=oml[:, h:h + 1], bias=lb[:, h:h + 1]))
            steps.settle()
            act.nop().then_inc(sem("logf_ready"), 1)
            act.wait_ge(sem("decay_abs"), 1)
            steps.link(act.activation(grow[2], grow[2], ACT.Exp, scale=-1.0))
            act.activation(grow[2], grow[2], ACT.Ln, bias=1.0).then_inc(sem("decay_log"), 1)
            for n in range(1, 9):
                act.wait_ge(sem("level_args"), n)
                act.activation(hE, hE, ACT.Exp).then_inc(sem("level_exps"), 1)
                if n <= 6:
                    name = f"S{n + 4}"
                    act.wait_ge(*full(name))
                    act.activation(pad2[:, 2 * (n - 1):2 * n, CONV2 - 1:], cols(held(name), 0, 2, S),
                                   ACT.Copy).then_inc(emptied(name), 1)
                if n == 2:
                    put("hx", wide(ATx))
            for n in range(1, 7):
                act.wait_ge(*was_emptied(f"S{n + 4}"))
            act.nop().then_inc(sem("pad2_ready"), 1)
            act.preload_act_table_set("silu_and_others")
            for i in range(4):
                act.wait_ge(*full(f"U{i + 2}"))
                act.activation(z_gate[:, :, S * i:S * (i + 1)], cols(held(f"U{i + 2}"), 0, TT, S),
                               ACT.Silu).then_inc(emptied(f"U{i + 2}"), 1)
            for t in range(TT):
                put(f"oB{t}", o_t[:, t, 512:1024])
            act.wait_ge(sem("conv2_done"), 1)
            steps.link(act.activation(wide(qkv), wide(qkv), ACT.Silu))
            act.nop().then_inc(sem("qkv_ready"), 1)
            act.wait_ge(sem("AT_ready"), 1)
            act.activation(wide(qk_ss), wide(qkv)[:, 0:8 * S], ACT.Square).then_inc(sem("qk_squared"), 1)
            act.preload_act_table_set("natural_log_exp_and_others")
            for h in range(GH):
                act.wait_ge(*full(f"bc{h}"))
                steps.mark(act.activation(egb[:, h, :], held(f"bc{h}")[:, P:2 * P], ACT.Exp))
                steps.mark(act.activation(dec[:, 2 * h:2 * h + 2, :], cols(held(f"bc{h}"), 0, 2, P), ACT.Copy))
                act.activation(attnT[:, 2 * h:2 * h + 2, :], cols(held(f"bc{h}"), S, 2, P),
                               ACT.Copy).then_inc(emptied(f"bc{h}"), 1)
            steps.settle()
            act.nop().then_inc(sem("bc_read"), 1)
            act.wait_ge(sem("dec_args"), 1)
            steps.link(act.activation(wide(dec), wide(dec), ACT.Exp))
            act.nop().then_inc(sem("dec_exps"), 1)
            for i in range(4):
                act.wait_ge(*full(f"l2{i}"))
            for i in range(4):
                v = wide(qk_ss)[:, 512 * i:512 * (i + 1)]
                put(f"l2{i}", v, func=ACT.Ln, bias=C("eps"))
                steps.mark(act.activation(v, v, ACT.Exp, scale=-0.5))
            steps.settle()
            act.nop().then_inc(sem("unit_ready"), 1)
            act.wait_ge(sem("col_args"), 1)
            steps.link(act.activation(small[:, 68:76], small[:, 68:76], ACT.Exp))
            act.nop().then_inc(sem("col_exps"), 1)
            for t in range(TT):
                put(f"kt{t}", wide(k_t)[:, 512 * t:512 * (t + 1)])
                put(f"vt{t}", wide(v_t)[:, 512 * t:512 * (t + 1)])
            act.nop().then_inc(sem("kv_turned"), 1)
            for half in range(2):
                put(f"T0{half}", wide(Ti)[:, 512 * half:512 * (half + 1)])
                act.nop().then_inc(sem("T_ready"), 1)
            for n in range(1, LEVELS):
                for half in range(2):
                    if n > 1:
                        act.wait_ge(*full(f"XU{n - 1}{half}"))
                    put(f"X{n}{half}", wide(Xi)[:, 512 * half:512 * (half + 1)])
                    act.nop().then_inc(sem("X_ready"), 1)
            for t in range(TT):
                put(f"u{t}", wide(uu)[:, 512 * t:512 * (t + 1)])
                act.nop().then_inc(sem("u_ready"), 1)
            put("wT", wide(wT))
            act.wait_ge(*full("oA0"))
            put("state", wide(S1))
            act.nop().then_inc(sem("S1_ready"), 1)
            put("oA0", o_t[:, 0, 0:512])
            put("oA1", o_t[:, 1, 0:512])
            act.wait_ge(sem("vnew_ready"), 1)
            for t in range(TT):
                for h in range(GH):
                    steps.mark(act.activation(work[:, s0 + 6144:s0 + 6272], o_t[:, t, h * P:(h + 1) * P],
                                              ACT.Square, accum_out=oss[:, 4 * t + h:4 * t + h + 1]))
                    steps.settle()
                steps.mark(act.activation(work[:, s0 + 6144:s0 + 6656], o_t[:, t, 512:1024], ACT.Square,
                                          accum_out=oss[:, 8 + t:9 + t]))
                steps.settle()
            steps.mark(inverse_root(ors[:, 0:8], oss[:, 0:8], P))
            steps.mark(inverse_root(ors[:, 8:10], oss[:, 8:10], HH * P))
            steps.settle()
            act.nop().then_inc(sem("o_rstd"), 1)

            act.wait_ge(sem("x_updated2"), 1)
            act.dma_start(finw, finw_in).then_inc(sem("final_w_landed"), 16)
            square_sums(4)
            act.preload_act_table_set("sigmoid_and_others")
            act.wait_ge(*full("router2"))
            act.activation(wide(score), held("router2")[:, 0:TT * E2],
                           ACT.Sigmoid).then_inc(emptied("router2"), 1)
            act.wait_ge(*was_emptied("router2"))
            act.nop().then_inc(sem("scores_ready"), 1)
            act.preload_act_table_set("silu_and_others")
            first2 = order.index("r64a")

            def gate_of2(done, b):
                act.wait_ge(piece_used, done)
                act.activation(silu2[b], bank[b][:, 0:S], ACT.Silu).then_inc(sem("silu2"), 1)

            def silu_group(it, n_experts):
                n = first2 + 5
                for i in range(n_experts):
                    gate_of2(it * 12 + (n + 1), 0)
                    gate_of2(it * 12 + (n + 3), 1)
                    n += 3

            for n, b in ((1, 0), (2, 1), (3, 0), (5, 1)):
                gate_of2(first2 + n, b)
            if e2_groups > 1:
                with act.Fori(0, e2_groups - 1) as it:
                    silu_group(it, 4)
            silu_group(e2_groups - 1, 3)
            act.preload_act_table_set("natural_log_exp_and_others")
            act.wait_ge(sem("x_updated3"), 1)
            square_sums(5)

        @block.vector
        def _(dve):
            steps = Steps(dve, sem("vector_steps"))
            tt, ts, stt = dve.tensor_tensor, dve.tensor_scalar, dve.scalar_tensor_tensor
            steps.mark(dve.memset(u_pad, 0.0))
            steps.mark(dve.memset(v_ext[:, :, :, AD:AD + 1], 1.0))
            for r in (1, 2, 3, 4, 5):
                steps.mark(dve.memset(rows[r], 0.0))
            steps.settle()
            dve.wait_ge(inputs_landed, 48)

            def scale_x(n):
                dve.wait_ge(sem("rstd_ready"), n)
                for t in range(TT):
                    steps.mark(ts(xn_t[:, t, :], x_t[:, t, :], rstd[:, t:t + 1], None, ALU.mult))
                steps.settle()
                dve.nop().then_inc(sem("x_normed"), 1)

            def read_turned(name, gain):
                for t in range(TT):
                    for hk in range(2):
                        dve.wait_ge(*full(f"{name}{t}{hk}"))
                        steps.link(tt(xnT[:, 4 * hk:4 * hk + 4, t * P:(t + 1) * P],
                                      cols(held(f"{name}{t}{hk}"), 0, 4, P),
                                      spread(gain[:, 4 * hk:4 * hk + 4], P), ALU.mult))
                        dve.nop().then_inc(emptied(f"{name}{t}{hk}"), 1)
                        dve.nop().then_inc(sem("xnT_ready"), 1)

            scale_x(1)
            read_turned("xT", V("mix_g"))

            dve.wait_ge(*full("gates_a"))
            ga = held("gates_a")
            steps.mark(ts(rows[0], ga[0:64, 0:S], V("b_i")[0:64], None, ALU.add))
            steps.link(ts(rows[1], ga[0:64, S:2 * S], V("b_f")[0:64], None, ALU.add))
            dve.nop().then_inc(emptied("gates_a"), 1)
            stt(rows[4], rows[1], -1.0, rows[1], ALU.mult, ALU.max).then_inc(sem("forget_abs"), 1)

            for j in range(4):
                dve.wait_ge(sem("glu_gate"), j + 1)
                steps.link(tt(u_pad[:, j, BK // 2:BK // 2 + S], held(f"F{j + 1}")[:, 0:S],
                              sig_u[:, j, :], ALU.mult))
                dve.nop().then_inc(emptied(f"F{j + 1}"), 1)
            taps = [0] * 4
            for k in range(BK):
                for j in range(4):
                    tap = V("conv_w", 31 * j + k, 31 * j + k + 1)
                    if k == 0:
                        ins = ts(uc[:, j, :], u_pad[:, j, 0:S], tap, V("conv_b", j, j + 1), ALU.mult, ALU.add)
                    else:
                        steps.settle(taps[j])
                        ins = stt(uc[:, j, :], u_pad[:, j, k:k + S], tap, uc[:, j, :], ALU.mult, ALU.add)
                    taps[j] = steps.mark(ins)
            steps.settle()
            dve.nop().then_inc(sem("conv_done"), 1)

            for t in range(TT):
                for name, a, n, gain in ((f"cqT{t}", 0, 3, V("cq_g")), (f"ckvT{t}", 3, 2, V("ckv_g"))):
                    dve.wait_ge(*full(name))
                    steps.link(tt(cT[:, a:a + n, t * P:(t + 1) * P], cols(held(name), 0, n, P),
                                  spread(gain, P), ALU.mult))
                    dve.nop().then_inc(emptied(name), 1)
                    dve.nop().then_inc(sem("latentsT_ready"), 1)

            dve.wait_ge(sem("forget_log"), 1)
            steps.link(stt(rows[1], rows[1], 0.0, rows[4], ALU.min, ALU.subtract))
            for d in range(2):
                r = slice(32 * d, 32 * d + AH)
                flow = slice(None, None, -1) if d else slice(None)
                one = ones_row[r]
                steps.link(dve.tensor_tensor_scan(rows[5][r, flow], one, rows[1][r, flow], 0.0,
                                                  ALU.mult, ALU.add))
            steps.link(tt(rows[2], rows[0], rows[5], ALU.subtract))
            for d in range(2):
                r = slice(32 * d, 32 * d + AH)
                flow = slice(None, None, -1) if d else slice(None)
                one = ones_row[r]
                steps.link(dve.tensor_tensor_scan(rows[3][r, flow], one, rows[2][r, flow], 0.0,
                                                  ALU.mult, ALU.max))
            steps.link(tt(rows[4], rows[5], rows[3], ALU.add))
            steps.link(ts(rows[3], rows[3], -1.0, None, ALU.mult))
            dve.nop().then_inc(sem("floor_rows"), 1)

            dve.wait_ge(sem("heads_squared"), 1)
            dve.tensor_reduce(qkss, qk_sq.rearrange("p t h d -> p (t h) d"), AX.X,
                              ALU.add).then_inc(sem("head_sums"), 1)
            dve.wait_ge(sem("head_rstd"), 1)
            steps.link(tt(qk_t.rearrange("p t h d -> p (t h) d"), qk_t.rearrange("p t h d -> p (t h) d"),
                          spread(qkrs, CQK), ALU.mult))
            for t in range(TT):
                for i, g in enumerate(("qn_g", "kn_g")):
                    v = qk_t[:, t, CH * i:CH * (i + 1), :]
                    steps.mark(tt(v, v, repeated(V(g), CH), ALU.mult))
            steps.settle()
            for t in range(TT):
                r1, r2 = qk_t[:, t, :, CN:CN + 16], qk_t[:, t, :, CN + 16:CQK]
                cos, sin = (repeated(C(n, 16 * t, 16 * t + 16), 2 * CH) for n in ("cos", "sin"))
                parts = [cols(qk_sq.rearrange("p t h d -> p (t h d)"), 256 * i, 2 * CH, 16) for i in range(4)]
                for o, (a, b) in zip(parts, ((r1, cos), (r2, sin), (r2, cos), (r1, sin))):
                    steps.mark(tt(o, a, b, ALU.mult))
                steps.settle()
                steps.mark(tt(r1, parts[0], parts[1], ALU.subtract))
                steps.mark(tt(r2, parts[2], parts[3], ALU.add))
                steps.settle()
            dve.nop().then_inc(sem("heads_roped"), 1)

            dve.wait_ge(*full("conv_sum"))
            for j in range(4):
                steps.mark(stt(uc[:, j, :], held("conv_sum")[:, 0:S], -1.0 / BW, uc[:, j, :],
                               ALU.mult, ALU.add))
            steps.settle()
            dve.nop().then_inc(emptied("conv_sum"), 1)
            dve.nop().then_inc(sem("conv_centred"), 1)
            dve.wait_ge(sem("conv_rstd"), 1)
            steps.link(tt(uc, uc, usq[:, 0:1, :].to_broadcast([P, 4, S]), ALU.mult))
            for j in range(4):
                steps.mark(ts(uc[:, j, :], uc[:, j, :], V("ln_g", j, j + 1), V("ln_b", j, j + 1),
                              ALU.mult, ALU.add))
            steps.settle()
            dve.nop().then_inc(sem("conv_affine"), 1)

            for h in range(CH + 1):
                if h < CH:
                    dve.wait_ge(*full(f"sc{h}"))
                    steps.link(dve.tensor_reduce(smax[:, 2 * h:2 * h + 2], cols(held(f"sc{h}"), 0, TT, S),
                                                 AX.X, ALU.max))
                    ts(smax[:, 2 * h:2 * h + 2], smax[:, 2 * h:2 * h + 2], -CQK ** -0.5, None,
                       ALU.mult).then_inc(sem("score_max"), 1)
                if h:
                    g = h - 1
                    dve.wait_ge(sem("probs_summed"), g + 1)
                    steps.link(dve.reciprocal(ssum[:, 2 * g:2 * g + 2], ssum[:, 2 * g:2 * g + 2]))
                    steps.link(tt(prob[g % 2], prob[g % 2], spread(ssum[:, 2 * g:2 * g + 2], S), ALU.mult))
                    dve.nop().then_inc(sem("probs_ready"), 1)

            dve.wait_ge(*full("gate_cols"))
            gc = held("gate_cols")[:, 0:256].rearrange("p (i t r) -> p i t r", i=2, t=TT)
            for i, o in enumerate((acol, fcol)):
                for d in range(2):
                    steps.mark(dve.tensor_copy(
                        o.rearrange("p (t d h) -> p t d h", t=TT, d=2)[:, :, d, :],
                        gc[:, i, :, 32 * d:32 * d + AH]))
            steps.settle()
            dve.nop().then_inc(emptied("gate_cols"), 1)
            areas = ((0, 0, 0, 0, 256), (0, 1, 128, 256, 384), (1, 0, 0, 384, 512), (1, 1, 0, 512, 768))

            def combine(h):
                for d in range(2):
                    dve.wait_ge(*full(f"mem{h}{d}"))
                    m = cols(held(f"mem{h}{d}"), 0, TT, AD + 1)
                    dn = den[:, 0:TT].unsqueeze(2)
                    steps.link(dve.tensor_copy(dn, m[:, :, AD:AD + 1]))
                    steps.link(stt(den[:, 0:TT], den[:, 0:TT], -1.0, den[:, 0:TT], ALU.mult, ALU.max))
                    floor = fcol.rearrange("p (t d h) -> p t d h", t=TT, d=2)[:, :, d, h:h + 1]
                    steps.link(tt(dn, dn, floor, ALU.max))
                    steps.link(dve.reciprocal(den[:, 0:TT], den[:, 0:TT]))
                    for t in range(TT):
                        if d == 0:
                            ins = ts(h_t[:, t, h, :], m[:, t, 0:AD], den[:, t:t + 1], None, ALU.mult)
                        else:
                            ins = stt(h_t[:, t, h, :], m[:, t, 0:AD], den[:, t:t + 1], h_t[:, t, h, :],
                                      ALU.mult, ALU.add)
                        steps.mark(ins)
                    steps.settle()
                    dve.nop().then_inc(emptied(f"mem{h}{d}"), 1)

            for h in range(AH + 1):
                if h < AH:
                    dve.wait_ge(*full(f"negA{h}"))
                    if h >= 2:
                        dve.wait_ge(*full(f"mem{h - 2}1"))
                    for d, kt, q, a, b in areas:
                        steps.mark(ts(warg[h % 2][:, a:b], held(f"negA{h}")[:, d * S + q:d * S + q + b - a],
                                      acol[:, (2 * kt + d) * AH + h:(2 * kt + d) * AH + h + 1], 0.0,
                                      ALU.add, ALU.min))
                    steps.settle()
                    dve.nop().then_inc(emptied(f"negA{h}"), 1)
                    dve.nop().then_inc(sem("weight_args"), 1)
                    dve.wait_ge(sem("weight_exps"), h + 1)
                    steps.link(tt(warg[h % 2], warg[h % 2], C("mmask"), ALU.mult))
                    dve.wait_ge(*full(f"kq{h}"))
                    for d, kt, q, a, b in areas:
                        steps.mark(tt(warg[h % 2][:, a:b], warg[h % 2][:, a:b],
                                      held(f"kq{h}")[:, kt * S + q:kt * S + q + b - a], ALU.mult))
                    steps.settle()
                    dve.nop().then_inc(emptied(f"kq{h}"), 1)
                    dve.nop().then_inc(sem("weights_ready"), 1)
                if h:
                    combine(h - 1)
            hv = h_t.rearrange("p t h d -> p (t h) d")
            h_sq = cols(warg[0], 0, 6, AD), cols(warg[1], 0, 2, AD)
            steps.mark(tt(h_sq[0], hv[:, 0:6, :], hv[:, 0:6, :], ALU.mult))
            steps.mark(tt(h_sq[1], hv[:, 6:8, :], hv[:, 6:8, :], ALU.mult))
            steps.settle()
            steps.mark(dve.tensor_reduce(hss[:, 0:6], h_sq[0], AX.X, ALU.add))
            steps.mark(dve.tensor_reduce(hss[:, 6:8], h_sq[1], AX.X, ALU.add))
            steps.settle()
            dve.nop().then_inc(sem("memory_sums"), 1)
            dve.wait_ge(sem("memory_rstd"), 1)
            steps.link(tt(hv, hv, spread(hrs, AD), ALU.mult))
            for i in range(2):
                dve.wait_ge(*was_emptied(f"vo{i + 2}"))
            steps.link(tt(h_t.rearrange("p t h d -> p (t h d)"), h_t.rearrange("p t h d -> p (t h d)"),
                          so_t.rearrange("p t d -> p (t d)"), ALU.mult))
            dve.nop().then_inc(sem("memory_normed"), 1)
            dve.wait_ge(sem("conv_sig"), 1)
            tt(uc, uc, usq, ALU.mult).then_inc(sem("conv_out"), 1)
            for t in range(TT):
                dve.wait_ge(*full(f"memT{t}"))
                steps.link(tt(hT[:, :, t * P:(t + 1) * P], cols(held(f"memT{t}"), 0, 4, P),
                              spread(V("a_g"), P), ALU.mult))
                dve.nop().then_inc(emptied(f"memT{t}"), 1)
                dve.nop().then_inc(sem("memT_ready"), 1)
            for j in range(4):
                for i in range(3):
                    dve.wait_ge(*full(f"y{j}{i}_"))
                    dve.wait_ge(sem("branch_gate"), 3 * j + i + 1)
                    mj = merged[:, 2 * j:2 * j + 2, :].rearrange("p b s -> p (b s)")
                    steps.link(tt(mj if i == 0 else gtmp[:, i - 1, :], gsig[:, i, :], held(f"y{j}{i}_"),
                                  ALU.mult))
                    dve.nop().then_inc(emptied(f"y{j}{i}_"), 1)
                    if i:
                        steps.link(tt(mj, mj, gtmp[:, i - 1, :], ALU.add))
                dve.nop().then_inc(sem("merged_ready"), 1)
            for t in range(TT):
                for n in range(2):
                    dve.wait_ge(*full(f"wo{t}{n}"))
                    v = x_t[:, t, n * 512:(n + 1) * 512]
                    steps.link(tt(v, v, held(f"wo{t}{n}"), ALU.add))
                    dve.nop().then_inc(emptied(f"wo{t}{n}"), 1)
            dve.nop().then_inc(sem("x_updated"), 1)

            scale_x(2)
            read_turned("xU", V("ffn_g"))
            dve.wait_ge(*full("router"))
            lg = held("router")[:, 0:TT * E1].rearrange("p (t e) -> p t e", t=TT)
            steps.link(dve.tensor_reduce(mx1, lg, AX.X, ALU.max))
            steps.link(tt(aff, lg, spread(mx1, E1), ALU.subtract))
            dve.nop().then_inc(emptied("router"), 1)
            dve.nop().then_inc(sem("logits_shifted"), 1)
            dve.wait_ge(sem("affinity_exp"), 1)
            steps.link(dve.tensor_reduce(sm1, aff, AX.X, ALU.add))
            steps.link(dve.reciprocal(sm1, sm1))
            tt(aff, aff, spread(sm1, E1), ALU.mult).then_inc(sem("affinity_ready"), 1)
            dve.wait_ge(*full("affT"))
            steps.link(dve.tensor_copy(affw, held("affT")[0:E1, 0:S]))
            dve.nop().then_inc(emptied("affT"), 1)
            for _ in range(CAP // 8):
                steps.link(dve.max(m8, affw))
                steps.link(dve.match_replace(affw, m8, affw, -1.0))
            steps.link(ts(affw, affw, 0.0, None, ALU.is_lt))
            steps.link(dve.tensor_tensor_scan(slotrow, ones_row[0:E1], affw, 0.0, ALU.mult, ALU.add))
            tt(slotrow, slotrow, affw, ALU.mult).then_inc(sem("slot_rows"), 1)
            dve.wait_ge(*full("mod_cols"))
            steps.link(tt(modc, held("mod_cols")[:, 0:32], V("b_ada"), ALU.add))
            dve.nop().then_inc(emptied("mod_cols"), 1)
            dve.wait_ge(sem("gate_bias_landed"), 16)
            for n in range(8):
                dve.wait_ge(*full(f"gmod{n}"))
                v = gmod[:, n * S:(n + 1) * S]
                steps.link(tt(v, v, held(f"gmod{n}")[:, 0:S], ALU.add))
                dve.nop().then_inc(emptied(f"gmod{n}"), 1)
            dve.wait_ge(*full("slotT"))
            steps.link(dve.tensor_copy(slot_t.rearrange("p t e -> p (t e)"), held("slotT")[:, 0:TT * E1]))
            dve.nop().then_inc(emptied("slotT"), 1)
            for t in range(TT):
                oh = onehot[:, t, :].rearrange("p (e c) -> p e c", e=E1)
                steps.mark(tt(oh, repeated(C("iota"), E1), spread(slot_t[:, t, :], CAP), ALU.is_equal))
            steps.settle()
            dve.nop().then_inc(sem("onehot_ready"), 1)
            for t in range(TT):
                oh, wt = (v[:, t, :].rearrange("p (e c) -> p e c", e=E1) for v in (onehot, weighted))
                steps.mark(tt(wt, oh, spread(aff[:, t, :], CAP), ALU.mult))
            steps.settle()
            dve.nop().then_inc(sem("weighted_ready"), 1)
            for k in range(0, KD, 2):
                dve.wait_ge(*full(f"xg{k}"))
                steps.link(ts(xg[:, k, :], held(f"xg{k}"), V("ffn_g", k, k + 1), None, ALU.mult))
                dve.nop().then_inc(emptied(f"xg{k}"), 1)
                dve.nop().then_inc(sem("xg_read"), 1)
            first1 = order.index("e0gu0")

            dve.nop().then_inc(sem("gated"), 1)
            dve.nop().then_inc(sem("scatter_read"), 1)

            def hidden_of(it, j):
                dve.wait_ge(sem("gate_silu"), it * 4 + (j + 1))
                dve.tensor_tensor(hid1[j % 2], gate1[j % 2], bank[2 + j % 2][0:3 * CAP, :],
                                  ALU.mult).then_inc(sem("gated"), 1)

            def hiddenT_of(it, j):
                dve.wait_ge(sem("hidden_turned"), it * 4 + (j + 1))
                dve.wait_ge(piece_used, it * 72 + (first1 + 12 + 18 * (j - 1)))
                dve.tensor_copy(hid1T[j % 2], cols(bank[7], 0, 4, 3, CAP)).then_inc(sem("hiddenT_ready"), 1)

            def add_back(it):
                for i in range(4):
                    t, half = divmod(i, 2)
                    dve.wait_ge(sem("scattered"), it * 4 + (i + 2))
                    v = x_t[:, t, half * 512:(half + 1) * 512]
                    tt(v, v, bank[6 + i % 2], ALU.add).then_inc(sem("scatter_read"), 1)

            hidden_of(0, 0)
            if e1_groups > 1:
                with dve.Fori(0, e1_groups - 1) as it:
                    for j in range(4):
                        hiddenT_of(it, j)
                        hidden_of(it, j + 1)
                    add_back(it)
            for j in range(4):
                hiddenT_of(e1_groups - 1, j)
                if j < 3:
                    hidden_of(e1_groups - 1, j + 1)
            add_back(e1_groups - 1)
            dve.wait_ge(sem("scatter_read"), 4 * e1_groups + 1)

            def read_modulated(name, weight, shift, scale):
                steps.link(stt(scol1, scale, 1.0, weight, ALU.add, ALU.mult))
                for t in range(TT):
                    for hk2 in range(2):
                        b4 = slice(4 * hk2, 4 * hk2 + 4)
                        out_ = xnT[:, b4, t * P:(t + 1) * P]
                        dve.wait_ge(*full(f"{name}{t}{hk2}"))
                        steps.link(tt(out_, cols(held(f"{name}{t}{hk2}"), 0, 4, P), spread(scol1[:, b4], P),
                                      ALU.mult))
                        dve.nop().then_inc(emptied(f"{name}{t}{hk2}"), 1)
                        steps.link(tt(out_, out_, spread(shift[:, b4], P), ALU.add))
                        dve.nop().then_inc(sem("xnT_ready"), 1)

            def wide(v):
                return v.rearrange("p a b -> p (a b)")

            tt(lb, V("lb0"), V("lb1"), ALU.subtract).then_inc(sem("lb_diff"), 1)
            steps.mark(dve.memset(pad2[:, :, 0:CONV2 - 1], 0.0))
            scale_x(3)
            read_modulated("xV", V("n1w"), modc[:, 0:8], modc[:, 8:16])
            steps.mark(dve.memset(wide(hQ), 0.0))
            steps.mark(dve.memset(wide(hK), 0.0))
            dve.wait_ge(sem("lb_ready"), 1)
            ts(oml, lb, -1.0, 1.0, ALU.mult, ALU.add).then_inc(sem("oml_ready"), 1)
            dve.wait_ge(*was_emptied("rows2"))
            stt(grow[2], grow[1], -1.0, grow[1], ALU.mult, ALU.max).then_inc(sem("decay_abs"), 1)
            dve.wait_ge(sem("oml_ready"), 1)
            dve.wait_ge(sem("keep_sig"), 1)
            for h in range(HH):
                v = hk[:, 2 * h:2 * h + 2, :]
                steps.mark(ts(v, v, oml[:, h:h + 1], None, ALU.mult))
            steps.settle()
            dve.wait_ge(sem("hq_ready"), 1)
            dve.nop().then_inc(sem("hk_ready"), 1)
            dve.wait_ge(sem("logf_ready"), 1)
            for i in range(HH * TT):
                steps.mark(dve.tensor_tensor_scan(hb[:, i, :], ones_row[:, 0:P], hb[:, i, :], 0.0,
                                                  ALU.mult, ALU.add))
            dve.wait_ge(sem("decay_log"), 1)
            dve.wait_ge(sem("decay_rate"), 1)
            steps.link(stt(grow[1], grow[1], 0.0, grow[2], ALU.max, ALU.add))
            steps.link(ts(grow[1], grow[1], nexpa, -1.0, ALU.mult, ALU.mult))
            for t in range(TT):
                c = slice(t * P, (t + 1) * P)
                steps.mark(dve.tensor_tensor_scan(grow[2][:, c], ones_row[0:GH, 0:P], grow[1][:, c], 0.0,
                                                  ALU.mult, ALU.add))
            steps.settle()
            dve.nop().then_inc(sem("g_rows"), 1)

            def level_views(n):
                if n == 1:
                    half = lambda v, i: v.rearrange("p (h t) s -> p h t s", t=TT)[:, :, i, :]
                    return half, P
                hs = 1 << (n - 2)
                return (lambda v, i: wide(v).rearrange("p (b two s) -> p b two s", two=2, s=hs)[:, :, i, :]), hs

            def level_args(n):
                half, hs = level_views(n)
                b0, b1 = half(hb, 0), half(hb, 1)
                mid = b0[:, :, hs - 1:hs].to_broadcast(list(b0.shape))
                steps.mark(tt(half(hE, 0), mid, b0, ALU.subtract))
                if n == 1:
                    steps.mark(dve.tensor_copy(half(hE, 1), b1))
                else:
                    steps.mark(tt(half(hE, 1), b1, mid, ALU.subtract))
                steps.settle()
                dve.nop().then_inc(sem("level_args"), 1)

            def add_level(n):
                for i in range(2):
                    dve.wait_ge(*full(f"hl{n}{i}"))
                    at = AT[:, 4 * i:4 * i + 4, :]
                    mask = ident if n == 0 else C("levels", (n - 2) * P, (n - 1) * P)
                    o = at if n == 0 else hsig[:, 4:8, :]
                    steps.link(tt(o, cols(held(f"hl{n}{i}"), 0, 4, P), repeated(mask, 4), ALU.mult))
                    dve.nop().then_inc(emptied(f"hl{n}{i}"), 1)
                    if n:
                        steps.link(tt(at, at, o, ALU.add))

            level_args(1)
            for n in range(1, 9):
                half, hs = level_views(n)
                dve.wait_ge(sem("level_exps"), n)
                if n >= 2:
                    dve.wait_ge(*full("hx" if n == 2 else f"hl{n - 1}1"))
                steps.mark(tt(half(hK, 0), half(hk, 0), half(hE, 0), ALU.mult))
                steps.mark(tt(half(hQ, 1), half(hq, 1), half(hE, 1), ALU.mult))
                steps.settle()
                dve.nop().then_inc(sem("level_ready"), 1)
                if n < 8:
                    level_args(n + 1)
                if n == 1:
                    add_level(0)
                elif n > 2:
                    add_level(n - 1)
            add_level(8)
            dve.nop().then_inc(sem("AT_ready"), 1)
            dve.wait_ge(sem("pad2_ready"), 1)
            marks = [0] * 12
            for k in range(CONV2):
                for j in range(12):
                    tap = V("conv2_w", CONV2 * j + k, CONV2 * j + k + 1)
                    if k == 0:
                        ins = ts(qkv[:, j, :], pad2[:, j, 0:S], tap, None, ALU.mult)
                    else:
                        steps.settle(marks[j])
                        ins = stt(qkv[:, j, :], pad2[:, j, k:k + S], tap, qkv[:, j, :], ALU.mult, ALU.add)
                    marks[j] = steps.mark(ins)
            steps.settle()
            dve.nop().then_inc(sem("conv2_done"), 1)
            dve.wait_ge(*full("gcols"))
            steps.link(dve.tensor_copy(small[:, 48:64], held("gcols")[:, 0:16]))
            dve.nop().then_inc(emptied("gcols"), 1)
            dve.wait_ge(sem("bc_read"), 1)
            for h in range(GH):
                steps.link(dve.tensor_copy(glast[:, h:h + 1], dec[:, 2 * h, P - 1:P]))
                for t in range(TT):
                    v = dec[:, 2 * h + t, :]
                    steps.mark(ts(v, v, gcol[:, 4 * t + h:4 * t + h + 1], 0.0, ALU.subtract, ALU.min))
            steps.settle()
            dve.nop().then_inc(sem("dec_args"), 1)
            steps.mark(dve.tensor_copy(ecol, gcol[:, 4:8]))
            steps.mark(tt(tcol, glast, gcol[:, 0:4], ALU.subtract))
            steps.settle()
            dve.nop().then_inc(sem("col_args"), 1)
            dve.wait_ge(sem("dec_exps"), 1)
            steps.link(tt(dec, dec, repeated(tri, 8), ALU.mult))
            dve.wait_ge(sem("unit_ready"), 1)
            q, k = wide(qkv)[:, 0:4 * S], wide(qkv)[:, 4 * S:8 * S]
            r = wide(qk_ss)
            steps.mark(stt(q, q, P ** -0.5, r[:, 0:4 * S], ALU.mult, ALU.mult))
            steps.mark(tt(k, k, r[:, 4 * S:8 * S], ALU.mult))
            steps.settle()
            dve.nop().then_inc(sem("qk_unit"), 1)
            steps.link(tt(LT, attnT, dec, ALU.mult))
            for h in range(GH):
                dve.wait_ge(*full(f"kk{h}"))
                v = slice(2 * h, 2 * h + 2)
                steps.mark(tt(LT[:, v, :], LT[:, v, :], cols(held(f"kk{h}"), 0, 2, P), ALU.mult))
                steps.mark(tt(attnT[:, v, :], dec[:, v, :], cols(held(f"kk{h}"), S, 2, P), ALU.mult))
                steps.settle()
                dve.nop().then_inc(emptied(f"kk{h}"), 1)

            def level_of_L(n):
                for i in range(2):
                    if n > 1:
                        dve.wait_ge(*full(f"X{n - 1}{i}"))
                    h4 = slice(4 * i, 4 * i + 4)
                    steps.link(tt(Lm[:, h4, :], LT[:, h4, :],
                                  repeated(C("levels", n * P, (n + 1) * P), 4), ALU.mult))
                    if n:
                        dve.nop().then_inc(sem("Lm_ready"), 1)

            for h in range(GH):
                dve.wait_ge(*was_emptied(f"bc{h}"))
            level_of_L(0)
            for i in range(2):
                h4 = slice(4 * i, 4 * i + 4)
                tt(Ui[:, h4, :], repeated(ident, 4), Lm[:, h4, :], ALU.subtract).then_inc(sem("U_ready"), 1)
            dve.wait_ge(sem("U_ready"), 2)
            level_of_L(1)
            for n in range(1, LEVELS):
                for i in range(2):
                    h4 = slice(4 * i, 4 * i + 4)
                    if n < LEVELS - 1:
                        dve.wait_ge(*full(f"TX{n}{i}"))
                        steps.link(tt(Ti[:, h4, :], Ti[:, h4, :], cols(held(f"TX{n}{i}"), 0, 4, P),
                                      ALU.subtract))
                        dve.nop().then_inc(emptied(f"TX{n}{i}"), 1)
                        dve.nop().then_inc(sem("T_ready"), 1)
                    dve.wait_ge(*full(f"XU{n}{i}"))
                    steps.link(tt(Ui[:, h4, :], Ui[:, h4, :], cols(held(f"XU{n}{i}"), 0, 4, P),
                                  ALU.subtract))
                    dve.nop().then_inc(emptied(f"XU{n}{i}"), 1)
                    dve.nop().then_inc(sem("U_ready"), 1)
                if n < LEVELS - 1:
                    level_of_L(n + 1)
            dve.wait_ge(sem("kv_turned"), 1)
            dve.wait_ge(sem("col_exps"), 1)
            steps.mark(tt(vb, v_t, spread(bcol, P), ALU.mult))
            steps.link(tt(ecol, ecol, bcol[:, 4:8], ALU.mult))
            steps.mark(tt(kbe, k_t[:, 4:8, :], spread(ecol, P), ALU.mult))
            steps.mark(tt(ktail, k_t[:, 0:4, :], spread(tcol, P), ALU.mult))
            q1 = qkv[:, 0:4, P:2 * P]
            steps.mark(tt(qd, q1, egb, ALU.mult))
            steps.settle()
            dve.nop().then_inc(sem("vb_ready"), 1)
            dve.wait_ge(*full("wS"))
            steps.link(tt(vnew, uu[:, 4:8, :], cols(held("wS"), 0, 4, P), ALU.subtract))
            dve.nop().then_inc(emptied("wS"), 1)
            dve.nop().then_inc(sem("vnew_ready"), 1)
            dve.wait_ge(sem("o_rstd"), 1)
            for t in range(TT):
                a = o_t[:, t, 0:512].rearrange("p (h d) -> p h d", h=GH)
                steps.mark(tt(a, a, spread(ors[:, 4 * t:4 * t + 4], P), ALU.mult))
                steps.mark(ts(o_t[:, t, 512:1024], o_t[:, t, 512:1024], ors[:, 8 + t:9 + t], None, ALU.mult))
            steps.settle()
            for i in range(4):
                dve.wait_ge(*was_emptied(f"U{i + 2}"))
            steps.link(tt(wide(o_t), wide(o_t), wide(z_gate), ALU.mult))
            dve.nop().then_inc(sem("o_ready"), 1)
            for t in range(TT):
                for half in range(2):
                    dve.wait_ge(*full(f"oo{t}{half}"))
                    steps.link(tt(oT2[:, 4 * half:4 * half + 4, t * P:(t + 1) * P],
                                  cols(held(f"oo{t}{half}"), 0, 4, P),
                                  spread(V("og", 4 * half, 4 * half + 4), P), ALU.mult))
                    dve.nop().then_inc(emptied(f"oo{t}{half}"), 1)
                    dve.nop().then_inc(sem("oT2_ready"), 1)
            for t in range(TT):
                for n in range(2):
                    dve.wait_ge(*full(f"wp{t}{n}"))
                    v, tmp = x_t[:, t, n * 512:(n + 1) * 512], work[:, n * 512:(n + 1) * 512]
                    steps.link(tt(tmp, held(f"wp{t}{n}"), gmod[:, n * 512:(n + 1) * 512], ALU.mult))
                    dve.nop().then_inc(emptied(f"wp{t}{n}"), 1)
                    steps.link(tt(v, v, tmp, ALU.add))
            dve.nop().then_inc(sem("x_updated2"), 1)

            scale_x(4)
            read_modulated("xW", V("n2w"), modc[:, 16:24], modc[:, 24:32])
            dve.wait_ge(sem("scores_ready"), 1)
            steps.link(tt(sel, score, repeated(V("rbias"), TT), ALU.add))
            for i in range(TT * NG2):
                steps.mark(dve.max(gmax[:, i, :], wide(sel)[:, 8 * i:8 * i + 8]))
            steps.settle()
            gs = wide(gsum).unsqueeze(2)
            steps.link(tt(gs, gmax[:, :, 0:1], gmax[:, :, 1:2], ALU.add))
            other = gsum.unsqueeze(2).to_broadcast([P, TT, NG2, NG2])
            own = gsum.unsqueeze(3).to_broadcast([P, TT, NG2, NG2])
            steps.mark(tt(cmpa, other, own, ALU.is_gt))
            steps.link(tt(cmpb, other, own, ALU.is_equal))
            before = C("gbefore").rearrange("p (a b) -> p a b", a=NG2)
            for t in range(TT):
                steps.mark(tt(cmpb[:, t], cmpb[:, t], before, ALU.mult))
            steps.settle()
            steps.link(tt(cmpa, cmpa, cmpb, ALU.add))
            steps.link(dve.tensor_reduce(rank, cmpa, AX.X, ALU.add))
            steps.link(ts(rank, rank, TOPG - 0.5, None, ALU.is_lt))
            in_group = wide(rank).unsqueeze(2).to_broadcast([P, TT * NG2, 8])
            by_group = lambda v: wide(v).rearrange("p (g e) -> p g e", e=8)
            steps.link(tt(by_group(msel), by_group(sel), in_group, ALU.mult))
            steps.link(ts(rank, rank, -1.0, 1e30, ALU.add, ALU.mult))
            steps.link(tt(by_group(msel), by_group(msel), in_group, ALU.add))
            for t in range(TT):
                steps.link(dve.max(top8[:, t, :], msel[:, t, :]))
                steps.link(dve.match_replace(chosen[:, t, :], top8[:, t, :], msel[:, t, :], -3e30))
            steps.link(ts(wide(chosen), wide(chosen), -2e30, None, ALU.is_lt))
            steps.link(tt(chosen, chosen, score, ALU.mult))
            steps.link(dve.tensor_reduce(wsum, chosen, AX.X, ALU.add))
            steps.link(dve.reciprocal(wsum, wsum))
            for t in range(TT):
                steps.mark(ts(chosen[:, t, :], chosen[:, t, :], wsum[:, t:t + 1], ROUTE_SCALE, ALU.mult,
                              ALU.mult))
            steps.settle()
            dve.nop().then_inc(sem("gates2_ready"), 1)
            dve.wait_ge(*full("gT"))
            steps.link(dve.tensor_copy(gT, held("gT")[0:E2, 0:S]))
            dve.nop().then_inc(emptied("gT"), 1)
            dve.nop().then_inc(sem("gT_ready"), 1)
            first2 = order.index("r64a")

            def hidden_of2(e, i, b, used):
                dve.wait_ge(sem("silu2"), e * 2 + (b + 1))
                if b == 0 and used is not None:
                    dve.wait_ge(piece_used, used)
                steps_in_loop(tt(part2[b], silu2[b], bank[b][:, S:2 * S], ALU.mult), e * 2 + (b + 1))
                dve.wait_ge(sem("gate_spread"), e + 1)
                tt(hid2[i % 2][b], part2[b], bank[2 + i % 2][:, 0:S], ALU.mult).then_inc(sem("hidden2"), 1)

            def steps_in_loop(ins, n):
                ins.then_inc(sem("part2_ready"), 1)
                dve.wait_ge(sem("part2_ready"), n - 2)

            for b in range(2):
                dve.wait_ge(sem("silu2"), b + 1)
                tt(hid2[0][b], silu2[b], bank[b][:, S:2 * S], ALU.mult).then_inc(sem("hidden2"), 1)
            for b in range(2):
                hidden_of2(1, 1, b, None)

            def hidden_group(it, n_experts):
                for i in range(2, 2 + n_experts):
                    for b in range(2):
                        hidden_of2(it * 4 + i, i, b, it * 12 + (first2 + 5 + 3 * (i - 2) - 1))

            if e2_groups > 1:
                with dve.Fori(0, e2_groups - 1) as it:
                    hidden_group(it, 4)
            hidden_group(e2_groups - 1, 3)
            dve.wait_ge(piece_used, first2 + 4 + 12 * e2_groups - 1)
            for t in range(TT):
                for n in range(2):
                    v, y = x_t[:, t, n * 512:(n + 1) * 512], ytmp[n]
                    steps.link(tt(y, bank[4 + 2 * t + n], gmod[:, D + n * 512:D + (n + 1) * 512], ALU.mult))
                    steps.link(tt(v, v, y, ALU.add))
            dve.nop().then_inc(sem("x_updated3"), 1)
            scale_x(5)
            dve.wait_ge(sem("final_w_landed"), 16)
            for t in range(TT):
                steps.mark(tt(xn_t[:, t, :], xn_t[:, t, :], finw, ALU.mult))
            steps.settle()
            dve.nop().then_inc(sem("out_ready"), 1)

        @block.gpsimd
        def _(pool):
            pool.wait_ge(sem("xg_read"), KD)
            first1 = order.index("e0gu0")

            def load_tokens(it, j):
                pool.wait_ge(piece_used, it * 72 + max(first1 + 6 + 18 * (j - 2), first1 + 12 if j == 2 else 1))
                nc.gpsimd.tensor_copy(xe[j % 2], xg[:, :, bass.ds((it * 4 + j) * CAP, CAP)]
                                      ).then_inc(sem("tokens_loaded"), 1)

            def load_back(it):
                pool.wait_ge(sem("scattered"), it * 4 + 1)
                nc.gpsimd.tensor_copy(back_now.unsqueeze(1), backT[:, bass.ds(it, 1), :]
                                      ).then_inc(sem("back_loaded"), 1)

            load_tokens(0, 0)
            pool.wait_ge(sem("back_ready"), 2)
            if e1_groups > 1:
                with pool.Fori(0, e1_groups - 1) as it:
                    for j in range(1, 5):
                        load_tokens(it, j)
                        if j == 1:
                            load_back(it)
            for j in range(1, 4):
                load_tokens(e1_groups - 1, j)
                if j == 1:
                    load_back(e1_groups - 1)
            pool.wait_ge(sem("gT_ready"), 1)

            def gate_row(e, i):
                if i is not None:
                    pool.wait_ge(sem("gate_spread"), e - 1)
                own = ident[0:E2, bass.ds(e - 1, 1)].to_broadcast([E2, S])
                nc.gpsimd.tensor_tensor(grow2[(i or 1) % 2], gT, own, ALU.mult).then_inc(sem("gate_row"), 1)

            gate_row(1, None)
            if e2_groups > 1:
                with pool.Fori(0, e2_groups - 1) as it:
                    for i in range(2, 6):
                        gate_row(it * 4 + i, i)
            for i in range(2, 5):
                gate_row((e2_groups - 1) * 4 + i, i)

        @block.sync
        def _(sp):
            sp.dma_start(x_t, x_in.rearrange("o (t p) d -> p (o t) d", p=P)).then_inc(inputs_landed, 16)
            sp.dma_start(cst, cst_in).then_inc(inputs_landed, 16)
            sp.dma_start(vec, vec_in).then_inc(inputs_landed, 16)
            n_pieces = len(order)
            for n in range(min(SLOTS, n_pieces)):
                sp.dma_start(ring[n % SLOTS].ap(), stream_in[n]).then_inc(landed[n % SLOTS], 16)
            full_rounds = n_pieces // SLOTS
            if full_rounds > 1:
                with sp.Fori(1, full_rounds) as i:
                    for s in range(SLOTS):
                        sp.wait_ge(piece_used, i * SLOTS + (s + 1 - SLOTS))
                        sp.dma_start(ring[s].ap(), stream_in[i * SLOTS + s]).then_inc(landed[s], 16)
            for n in range(max(full_rounds, 1) * SLOTS, n_pieces):
                sp.wait_ge(piece_used, n + 1 - SLOTS)
                sp.dma_start(ring[n % SLOTS].ap(), stream_in[n]).then_inc(landed[n % SLOTS], 16)
            sp.wait_ge(sem("out_ready"), 1)
            sp.dma_start(out.rearrange("o (t p) d -> p (o t) d", p=P), xn_t).then_inc(sem("stored"), 16)
            sp.wait_ge(sem("stored"), 16)


def k_major(w):
    return w.reshape(w.shape[0] // P, P, w.shape[1]).transpose(1, 0, 2)


def layout(a):
    f = np.float32
    z = {}
    at = 0
    for name, n in (("q", 512), ("k", 512), ("v", 512), ("o", 512), ("g", 16), ("glu", 1024),
                    ("cq", CQR), ("ckv", CKR), ("kr", CR), ("gts", 3 * D)):
        z[name] = a["w_in"][0][:, at:at + n]
        at += n
    pieces = {}

    def put_k(name, w, width=S):
        full_w = np.zeros((w.shape[0], width), f)
        full_w[:, :w.shape[1]] = w
        pieces[name] = k_major(full_w).reshape(P, -1)

    gate = np.zeros((D, S), f)
    for at, kind in ((0, 0), (32, 2), (64, 1), (96, 3)):
        gate[:, at:at + AH] = z["g"][:, AH * kind:AH * (kind + 1)]
    put_k("F0", gate)
    for j in range(4):
        c = slice(j * P, (j + 1) * P)
        c2 = slice(BW + j * P, BW + (j + 1) * P)
        put_k(f"F{j + 1}", np.concatenate([z["glu"][:, c], z["glu"][:, c2]], 1))
        put_k(f"F{j + 5}", np.concatenate([z["q"][:, c], z["k"][:, c]], 1))
    lat = np.concatenate([z["cq"], z["ckv"], z["kr"]], 1)
    vo = np.concatenate([z["v"], z["o"]], 1)
    for i in range(3):
        put_k(f"lat{i}", lat[:, S * i:S * (i + 1)])
    for i in range(4):
        put_k(f"vo{i}", vo[:, S * i:S * (i + 1)])
    for half in range(2):
        pieces[f"uq{half}"] = k_major(a["w_uq"][0][:, 384 * half:384 * (half + 1)]).reshape(P, -1)
    pieces["ukv"] = k_major(a["w_ukv"][0]).reshape(P, -1)
    for j in range(4):
        ys = []
        for i in range(3):
            put_k(f"g{j}{i}", z["gts"][:, D * i + S * j:D * i + S * (j + 1)])
            w = (a["w_a_out"], a["w_b_out"], a["w_c_out"])[i][0]
            ys.append(k_major(w[:, S * j:S * (j + 1)]).reshape(P, -1))
        pieces[f"y{j}0"] = np.concatenate(ys[0:2], 1)
        pieces[f"y{j}2"] = ys[2]
    for q in range(4):
        pieces[f"wo{q}"] = k_major(a["w_out"][0][S * q:S * (q + 1)]).reshape(P, -1)
        pieces[f"wp{q}"] = k_major(a["w_out_2"][0][S * q:S * (q + 1)]).reshape(P, -1)
    ada = a["w_ada_2"][0]
    for i, kind in enumerate((0, 1, 3, 4, 2, 5)):
        for q in range(4):
            put_k(f"ada{4 * i + q}", ada[:, D * kind + S * q:D * kind + S * (q + 1)])
    z2, at = {}, 0
    for name, n in (("q", 512), ("k", 512), ("v", 512), ("gateA", 512), ("beta", 4), ("a", 4), ("f", 512),
                    ("i", 512), ("qB", 512), ("gateB", 512)):
        z2[name] = a["w_in_2"][0][:, at:at + n]
        at += n
    ab = np.zeros((D, S), f)
    ab[:, 0:GH], ab[:, 32:32 + GH] = z2["beta"], z2["a"]
    put_k("S0", ab)
    f2 = np.concatenate([z2["f"], z2["qB"], z2["q"], z2["k"], z2["v"]], 1)
    for i in range(10):
        put_k(f"S{i + 1}", f2[:, S * i:S * (i + 1)])
    t2 = np.concatenate([z2["i"], z2["gateA"], z2["gateB"]], 1)
    for i in range(6):
        put_k(f"U{i}", t2[:, S * i:S * (i + 1)])
    for e in range(E1):
        g, u, d = k_major(a["w_e_gate"][0, e]), k_major(a["w_e_up"][0, e]), k_major(a["w_e_down"][0, e])
        gu = np.concatenate([g, u], 2).reshape(P, -1)
        for p in range(12):
            pieces[f"e{e}gu{p}"] = gu[:, PC * p:PC * (p + 1)]
        for q in range(6):
            pieces[f"e{e}d{q}"] = d[:, 2 * q:2 * q + 2].reshape(P, -1)
    for e in range(E2 + 1):
        g, u, d = ((a["w_gate_2"][0, e], a["w_up_2"][0, e], a["w_down_2"][0, e]) if e < E2 else
                   (a["ws_gate_2"][0], a["ws_up_2"][0], a["ws_down_2"][0]))
        g, u = k_major(g), k_major(u)
        for b, n in enumerate("ab"):
            c = slice(b * P, (b + 1) * P)
            pieces[f"r{e}{n}"] = np.concatenate([g[:, :, c], u[:, :, c]], 2).reshape(P, -1)
        pieces[f"r{e}d"] = k_major(d).reshape(P, -1)

    def column(v):
        return v.reshape(-1, P).T

    def everywhere(v):
        return np.broadcast_to(v.reshape(1, -1), (P, v.size))

    def gate_column(fw, bw):
        v = np.zeros((P, 1), f)
        v[0:AH, 0], v[32:32 + AH, 0] = fw, bw
        return v

    b = a["b_if"][0].reshape(4, AH)
    vals = dict(
        mix_g=column(a["mix_norm_g"][0]),
        conv_w=a["conv_w"][0].T.reshape(4, P, BK).transpose(1, 0, 2).reshape(P, -1),
        conv_b=column(a["conv_b"][0]), ln_g=column(a["conv_ln_g"][0]), ln_b=column(a["conv_ln_b"][0]),
        a_g=a["a_norm_g"][0].T, cq_g=column(a["cq_norm_g"][0]), ckv_g=column(a["ckv_norm_g"][0]),
        qn_g=everywhere(a["q_norm_g"][0]), kn_g=everywhere(a["k_norm_g"][0]),
        b_i=gate_column(b[0], b[2]), b_f=gate_column(b[1], b[3]),
        ffn_g=column(a["ffn_norm_g"][0]), router=k_major(a["w_router"][0]).reshape(P, -1),
        c=column(a["c_2"][0]),
        b_ada=np.concatenate([column(a["b_ada_2"][0][D * i:D * (i + 1)]) for i in (0, 1, 3, 4)], 1),
        n1w=column(a["norm1_w_2"][0]),
        conv2_w=a["conv_w_2"][0].T.reshape(12, P, CONV2).transpose(1, 0, 2).reshape(P, -1),
        a_log=np.pad(a["gdn_a_log_2"][0].reshape(GH, 1), ((0, P - GH), (0, 0))),
        dt=np.pad(a["gdn_dt_bias_2"][0].reshape(GH, 1), ((0, P - GH), (0, 0))),
        og=np.concatenate([np.repeat(a["gdn_norm_w_2"][0].reshape(P, 1), GH, 1),
                           column(a["hg_norm_w_2"][0])], 1),
        lb0=column(a["hg_lb_2"][0]), lb1=column(a["hg_lb_2"][1]), n2w=column(a["norm2_w_2"][0]),
        router2=k_major(a["w_router_2"][0]).reshape(P, -1), rbias=everywhere(a["router_bias_2"][0]))
    vec = np.concatenate([vals[n].reshape(P, w) for n, w in VEC.items()], 1)
    return pieces, np.ascontiguousarray(vec)


def constants():
    f = np.float32
    i = np.arange(P)
    s, t = i[:, None], i[None, :]
    tri = (s <= t).astype(f)
    one = np.ones((P, P), f)
    mask = np.concatenate([tri, one, tri, tri.T, one, tri.T], 1) * f(AD ** -0.5)
    levels = [((s < t) & ((s ^ t) >= 2 ** n) & ((s ^ t) < 2 ** (n + 1))).astype(f) for n in range(LEVELS)]
    g = np.arange(NG2)
    inv = (np.float32(10000.0) ** (-np.arange(0, CR, 2, dtype=f) / f(CR))).astype(f)
    ang = np.arange(S, dtype=f)[:, None] * inv[None, :]
    by_tile = lambda v: v.reshape(TT, P, -1).transpose(1, 0, 2).reshape(P, -1)
    vals = dict(ident=np.eye(P, dtype=f), ones=one, tri=tri, mmask=mask, levels=np.concatenate(levels, 1),
                iota=np.tile(np.arange(1, CAP + 1, dtype=f), (P, 1)),
                gbefore=np.tile((g[None, :] < g[:, None]).astype(f).reshape(1, -1), (P, 1)),
                cos=by_tile(np.cos(ang)), sin=by_tile(np.sin(ang)), eps=np.full((P, 1), EPS, f))
    return np.concatenate([vals[n].astype(f).reshape(P, w) for n, w in CST.items()], 1)


def make(nc, **kw):
    order = []
    n_pieces = kw.pop("n_pieces")
    dram = lambda n, s, k: nc.dram_tensor(n, s, F32, kind=k).ap()
    build(nc, dram("x", (1, S, D), "ExternalInput"), dram("stream", (n_pieces, P, PC), "ExternalInput"),
          dram("vec_pack", (P, VN), "ExternalInput"), dram("const_pack", (P, CN_ALL), "ExternalInput"),
          dram("gate_bias", (P, 2 * D), "ExternalInput"), dram("final_w", (P, D), "ExternalInput"),
          dram("result", (1, S, D), "ExternalOutput"), order, **kw)
    return order


def arrays(inputs, order):
    a = {k: np.asarray(v) for k, v in inputs.items()}
    pieces, vec = layout(a)
    stream = np.zeros((len(order), P, PC), np.float32)
    for n, name in enumerate(order):
        p = pieces[name]
        stream[n, :, :p.shape[1]] = p
    bias = a["b_ada_2"][0]
    return {"x": a["x"], "stream": stream, "vec_pack": vec, "const_pack": constants(),
            "gate_bias": np.tile(np.concatenate([bias[2 * D:3 * D], bias[5 * D:6 * D]]), (P, 1)),
            "final_w": np.tile(a["final_norm_w_2"], (P, 1))}


def kernel(**inputs):
    from concourse import bacc
    from concourse.bass_utils import run_bass_kernel_spmd

    nc = bacc.Bacc("TRN2", target_bir_lowering=False, num_devices=1)
    order = make(nc, n_pieces=N_PIECES)
    assert len(order) == N_PIECES, len(order)
    r = run_bass_kernel_spmd(nc, [arrays(inputs, order)], core_ids=[0])
    return r.results[0]["result"]
```

```python
from contextlib import ExitStack

import numpy as np

import concourse.bass as bass
from concourse import mybir
from concourse.alu_op_type import AluOpType as ALU

F32 = mybir.dt.float32
F32R = mybir.dt.float32r
ACT = mybir.ActivationFunctionType
AX = mybir.AxisListType

P = 128
S = 256
TT = S // P
D = 1024
KD = D // P
EPS = 1e-6

PC = 2048
SLOTS = 12

AH, AD = 4, 128
BW, BK = 512, 31
CH, CQK, CN, CR, CV = 8, 96, 64, 32, 64
CQR, CKR = 384, 256
E1, FF, CAP = 16, 1536, 32
GH, HH = 4, 4
CONV2 = 4
E2, DE, NG2, TOPG, TOPK = 64, 256, 8, 4, 8
ROUTE_SCALE = 2.5
LEVELS = 7

HIGHS, AHEAD = 4, 3
N_PIECES = 43 + 24 + 18 * E1 + 21 + 3 * (E2 + 1)

VEC = dict(mix_g=8, conv_w=124, conv_b=4, ln_g=4, ln_b=4, a_g=4, cq_g=3, ckv_g=2, qn_g=96, kn_g=96,
           b_i=1, b_f=1, ffn_g=8, router=128, c=8, b_ada=48, n1w=8, conv2_w=48, a_log=1, dt=1, og=8,
           lb0=4, lb1=4, n2w=8, router2=512, rbias=64)
CST = dict(ident=128, ones=128, tri=128, mmask=768, levels=LEVELS * 128, iota=32, gbefore=64,
           cos=32, sin=32, eps=1)


def offsets(widths):
    at, out = 0, {}
    for name, n in widths.items():
        out[name] = (at, at + n)
        at += n
    return out, at


VOFF, VN = offsets(VEC)
COFF, CN_ALL = offsets(CST)


def build(nc, x_in, stream_in, vec_in, cst_in, finw_in, out, order, e1_groups=E1 // 4,
          e2_groups=E2 // 4):
    ctx = ExitStack()
    with ctx:
        def sb(name, cols):
            return ctx.enter_context(nc.sbuf_tensor(name, [P, cols], F32))

        sems = {}

        def sem(name):
            if name not in sems:
                sems[name] = ctx.enter_context(nc.semaphore(name))
            return sems[name]

        def twice(name, cols):
            with nc.sbuf_tensor(name, [P, cols], F32) as plain:
                pass
            return plain, ctx.enter_context(nc.sbuf_tensor(f"{name}_r", [P, cols], F32R))

        ring, ring_r = zip(*(twice(f"piece{i}", PC) for i in range(SLOTS)))
        x_t = sb("x_t", TT * D).ap().rearrange("p (t d) -> p t d", t=TT)
        xn_t = sb("xn_t", TT * D).ap().rearrange("p (t d) -> p t d", t=TT)
        xnT = sb("xnT", KD * S).ap().rearrange("p (k s) -> p k s", k=KD)
        vec = sb("vec", VN).ap()
        cst = sb("cst", CN_ALL).ap()
        gmod = sb("gmod", 2 * D).ap()
        small = sb("small", 256).ap()
        WORK = 16500
        work, work_r = (v.ap() for v in twice("work", WORK))
        bank = [ctx.enter_context(nc.psum_tensor(f"bank{i}", [P, 512], F32)).ap() for i in range(8)]

        def V(name, a=0, b=None):
            lo, hi = VOFF[name]
            return vec[:, lo + a:(hi if b is None else lo + b)]

        def C(name, a=0, b=None):
            lo, hi = COFF[name]
            return cst[:, lo + a:(hi if b is None else lo + b)]

        ident, ones, tri = C("ident"), C("ones"), C("tri")

        def cols(base, at, *dims):
            n = int(np.prod(dims))
            v = base[:, at:at + n]
            if len(dims) == 2:
                v = v.rearrange("p (a b) -> p a b", a=dims[0])
            if len(dims) == 3:
                v = v.rearrange("p (a b c) -> p a b c", a=dims[0], b=dims[1])
            if len(dims) == 4:
                v = v.rearrange("p (a b c d) -> p a b c d", a=dims[0], b=dims[1], c=dims[2])
            return v

        def spread(v, n):
            return v.unsqueeze(2).to_broadcast([v.shape[0], v.shape[1], n])

        def repeated(v, n):
            return v.unsqueeze(1).to_broadcast([v.shape[0], n, v.shape[1]])

        modc, cact = small[:, 192:240], small[:, 240:248]
        diagonal = cols(sb("diagonal", 2 * P).ap(), 0, 2, P)
        sq_sum = small[:, 0:2]
        rstd = small[:, 2:4]

        products = {}
        to_empty = [0] * 8
        bank_full = [sem(f"bank_full{i}") for i in range(8)]
        bank_emptied = [sem(f"bank_emptied{i}") for i in range(8)]

        fills = [0] * 8
        turns = {}

        def full(name):
            return products[name][1:]

        def was_emptied(name):
            return bank_emptied[products[name][0]], turns[name]

        def emptied(name):
            return bank_emptied[products[name][0]]

        def held(name):
            return bank[products[name][0]]

        class Steps:

            def __init__(self, eng, s):
                self.eng, self.s, self.n = eng, s, 0

            def mark(self, ins):
                ins.then_inc(self.s, 1)
                self.n += 1
                return self.n

            def settle(self, n=None):
                self.eng.wait_ge(self.s, self.n if n is None else n)

            def link(self, ins):
                self.mark(ins)
                self.settle()

        landed = [sem(f"landed{i}") for i in range(SLOTS)]
        piece_used = sem("piece_used")
        inputs_landed = sem("inputs_landed")

        flat = xn_t.rearrange("p t d -> p (t d)")
        c_t = cols(flat, 0, TT, CQR + CKR + CR)
        usq = cols(flat, 0, 4, S)
        uc = cols(gmod, 0, 4, S)
        oT = cols(gmod, 4 * S, 4, S)
        w0 = 0
        cT = cols(work, w0, 5, S)
        hT = cols(work, w0, 4, S)
        w0 += 5 * S
        fqk = cols(work, w0, 8, S)
        merged = cols(work, w0, 8, S)
        w0 += 8 * S
        v_ext = cols(work, w0, TT, AH, AD + 1)
        w0 += TT * AH * (AD + 1)
        so_t = cols(work, w0, TT, AH * AD)
        w0 += TT * AH * AD
        gsig, gtmp = cols(work, w0, 3, 512), cols(work, w0 + 1536, 2, 512)
        u_pad = cols(work, w0, 4, S + BK - 1)
        w0 += 4 * (S + BK - 1)
        sig_u = cols(work, w0, 4, S)
        qk_t = cols(work, w0, TT, 2 * CH, CQK)
        prob = [cols(work, w0 + 512 * i, TT, S) for i in range(2)]
        probT = [cols(work, w0 + 1024 + 512 * i, TT, S) for i in range(2)]
        w0 += TT * 2 * CH * CQK
        vc_t = cols(work, w0, TT, CH, CV)
        w0 += TT * CH * CV
        qkT = cols(work, w0, 2 * CH, S)
        qk_sq = cols(work, w0, TT, 2 * CH, CQK)
        junk = work[:, w0:w0 + CQR]
        warg = [work[:, w0 + 768 * i:w0 + 768 * (i + 1)] for i in range(2)]
        h_t = cols(work, w0 + 1536, TT, AH, AD)
        w0 += 2 * CH * S
        rows = {r: work[0:64, w0 + S * i:w0 + S * (i + 1)] for i, r in enumerate((0, 1, 3, 4, 5))}
        rows[2] = rows[0]
        w0 += 5 * S
        assert w0 <= WORK, w0
        at_gates = 5 * S + 8 * S + TT * (AH * (AD + 1) + AH * AD) + 5 * 512
        gate_high = [work_r[:, a:a + PC] for a in (at_gates, at_gates + PC, 13 * S)]
        gx_high, gx_low = (cols(work_r, at_gates + PC * (2 + i), KD, S) for i in range(2))
        assert at_gates + 4 * PC <= WORK
        ones_row = C("ones", 0, 1).to_broadcast([P, S])
        rs_c, ss_c, hss, hrs = small[:, 4:8], small[:, 8:12], small[:, 16:24], small[:, 24:32]
        qkss, qkrs, acol, fcol = small[:, 32:64], small[:, 64:96], small[:, 96:112], small[:, 112:128]
        smax, ssum, den = small[:, 128:144], small[:, 144:160], small[:, 160:162]

        w0 = 0
        onehot = cols(work_r, w0, TT, E1 * CAP)
        weighted = cols(work, w0 + 1024, TT, E1 * CAP)
        backT = cols(work, w0 + 2048, 4, S)
        xg = cols(work, w0 + 3072, KD, E1 * CAP)
        w0 += 3072 + KD * E1 * CAP
        xe = [cols(work, w0 + 256 * i, KD, CAP) for i in range(2)]
        back_now = work[:, w0 + 512:w0 + 768]
        gate1 = [work[0:3 * CAP, w0 + 768 + 512 * i:w0 + 1280 + 512 * i] for i in range(2)]
        hid1 = [work[0:3 * CAP, w0 + 1792 + 512 * i:w0 + 2304 + 512 * i] for i in range(2)]
        hid1T = [cols(work, w0 + 2816 + 384 * i, 4, 3, CAP) for i in range(2)]
        y_now = work[:, w0 + 3584:w0 + 4608]
        w0 += 4608
        aff = cols(work, w0, TT, E1)
        slot_t = cols(work, w0 + 32, TT, E1)
        affw, slotrow = work[0:E1, w0 + 64:w0 + 320], work[0:E1, w0 + 320:w0 + 576]
        m8 = work[0:E1, w0 + 576:w0 + 584]
        mx1, sm1 = work[:, w0 + 592:w0 + 594], work[:, w0 + 594:w0 + 596]
        xn_high, xn_low = (cols(work_r, w0 + 600 + TT * D * i, TT, D) for i in range(2))
        assert w0 + 600 + 2 * TT * D <= WORK
        FB1 = FF // P

        turnedT = xnT.rearrange("p k s -> p (k s)")
        z_gate = cols(flat, 0, TT, D)
        o_t = cols(turnedT, 0, TT, D)
        oT2 = cols(flat, 0, KD, S)
        w0 = 0
        pad2 = cols(work, w0, 12, S + CONV2 - 1)
        k_t, v_t = cols(work, w0, TT * GH, P), cols(work, w0 + 1024, TT * GH, P)
        w0 += 12 * (S + CONV2 - 1)
        qkv = cols(work, w0, 12, S)
        w0 += 12 * S
        hq = cols(work, w0, HH * TT, P)
        iB = cols(work, w0 + 1024, TT * HH, P)
        AT = cols(work, w0 + 2048, HH * TT, P)
        w0 += 3072
        s0 = w0
        hsig, hk, hb, hE, hQ, hK = (cols(work, s0 + 1024 * i, HH * TT, P) for i in range(6))
        ATx = hsig[:, 0:4]
        dec, attnT, LT, Ti, Ui, Xi, Lm = (cols(work, s0 + 1024 * i, GH * TT, P) for i in range(7))
        qk_ss = cols(work, s0 + 2048, 8, S)
        grow = [work[0:GH, s0 + 6144 + S * i:s0 + 6144 + S * (i + 1)] for i in range(3)]
        vb, kbe, wT, uu = Ti, Xi[:, 0:4], Xi[:, 4:8], Lm
        S1, vnew, qd, ktail = dec[:, 0:4], dec[:, 4:8], LT[:, 0:4], LT[:, 4:8]
        assert s0 + 7168 <= WORK, s0
        egb = cols(work, 0 + 2048, GH, P)
        lb, oml, scol1 = small[:, 32:36], small[:, 36:40], small[:, 40:48]
        gcol, bcol = small[:, 48:56], small[:, 56:64]
        glast, ecol, tcol = small[:, 64:68], small[:, 68:72], small[:, 72:76]
        nexpa = small[0:GH, 76:77]
        oss, ors = small[:, 80:90], small[:, 90:100]

        w_high = [work_r[:, PC * i:PC * (i + 1)] for i in range(HIGHS)]
        w0 = HIGHS * PC
        x_high, x_low = (cols(work_r, w0 + KD * S * i, KD, S) for i in range(2))
        w0 += 2 * KD * S
        r0 = w0 + 4 * S
        hid2 = [[[work_r[:, w0 + S * (4 * i + 2 * part + b):w0 + S * (4 * i + 2 * part + b + 1)]
                  for b in range(2)] for part in range(2)] for i in range(2)]
        w0 += 8 * S
        gT = work_r[0:E2, w0:w0 + 2 * S]
        grow2 = [work_r[0:E2, w0 + 2 * S * (i + 1):w0 + 2 * S * (i + 2)] for i in range(2)]
        w0 += 6 * S
        ones_r = work_r[0:E2, w0:w0 + P]
        w0 += P
        ytmp = [turnedT[:, 512 * i:512 * (i + 1)] for i in range(2)]
        silu2 = [turnedT[:, S * b:S * (b + 1)] for b in range(2)]
        part2 = [turnedT[:, 512 + S * b:512 + S * (b + 1)] for b in range(2)]
        assert w0 <= WORK
        finw = gmod[:, 0:D]
        score, sel, msel, chosen = (cols(work, r0 + 128 * i, TT, E2) for i in range(4))
        gmax = cols(work, r0 + 512, TT * NG2, 8)
        gsum = cols(work, r0 + 640, TT, NG2)
        cmpa, cmpb = cols(work, r0 + 656, TT, NG2, NG2), cols(work, r0 + 784, TT, NG2, NG2)
        rank = cols(work, r0 + 912, TT, NG2)
        top8 = cols(work, r0 + 928, TT, TOPK)
        wsum = work[:, r0 + 944:r0 + 946]

        block = ctx.enter_context(nc.Block())

        @block.tensor
        def _(pe):
            def piece(name):
                n = len(order)
                order.append(name)
                pe.wait_ge(landed[n % SLOTS], 16 * (n // SLOTS + 1))
                return ring[n % SLOTS].ap()

            def release(ins, name=None):
                ins.then_inc(piece_used, 1)
                if name:
                    products[name] = (products[name][0], piece_used, len(order))

            def fill(name, readers=1):
                b = len(products) % 8
                products[name] = (b, bank_full[b], None)
                if to_empty[b]:
                    pe.wait_ge(bank_emptied[b], to_empty[b])
                to_empty[b] += readers
                turns[name] = to_empty[b]
                return bank[b]

            def complete(ins, name):
                b = products[name][0]
                fills[b] += 1
                products[name] = (b, bank_full[b], fills[b])
                ins.then_inc(bank_full[b], 1)

            def turn(name, blocks, readers=1):
                ps = fill(name, readers)
                for i, (src, n) in enumerate(blocks):
                    m = src.shape[1]
                    last = pe.transpose(ps[0:m, i * n:(i + 1) * n], src, ident[0:n, 0:n])
                complete(last, name)

            def token_major(name, width):
                w = cols(piece(name), 0, KD, S)
                ps = fill(name)
                for t in range(TT):
                    for k in range(KD):
                        last = pe.matmul(ps[:, t * S:t * S + width], xnT[:, k, t * P:(t + 1) * P],
                                         w[:, k, 0:width], start=(k == 0), stop=(k == KD - 1))
                release(last, name)

            def feature_major(name, blocks=2):
                w = cols(piece(name), 0, KD, S)
                ps = fill(name)
                for b in range(blocks):
                    for k in range(KD):
                        last = pe.matmul(ps[:, b * S:(b + 1) * S], w[:, k, b * P:(b + 1) * P],
                                         xnT[:, k, :], start=(k == 0), stop=(k == KD - 1))
                release(last, name)

            def feature_major_by_parts(name, n, w_high):
                piece(name)
                pe.wait_ge(sem("gate_rest"), n)
                wh, wl = cols(w_high, 0, KD, S), cols(ring_r[(len(order) - 1) % SLOTS].ap(), 0, KD, S)
                ps = fill(name)
                for b in range(2):
                    for k in range(KD):
                        for i, (w, x) in enumerate(((wh, gx_high), (wh, gx_low), (wl, gx_high))):
                            last = pe.matmul(ps[:, b * S:(b + 1) * S], w[:, k, b * P:(b + 1) * P], x[:, k, :],
                                             start=(k == 0 and i == 0), stop=(k == KD - 1 and i == 2))
                release(last, name)

            def turn_x(name, n):
                pe.wait_ge(sem("x_normed"), n)
                for t in range(TT):
                    for hk in range(2):
                        turn(f"{name}{t}{hk}", [(xn_t[:, t, (4 * hk + i) * P:(4 * hk + i + 1) * P], P)
                                                for i in range(4)])
                pe.wait_ge(sem("xnT_ready"), 4 * n)

            def project(name, src):
                outs = [(t, n, fill(f"{name}{t}{n}")) for t in range(TT) for n in range(2)]
                for q in range(4):
                    w = cols(piece(f"{name}{q}"), 0, 2, 1024)
                    for t, n, ps in outs:
                        for kk in range(2):
                            k = 2 * q + kk
                            last = pe.matmul(ps, src[:, k, t * P:(t + 1) * P],
                                             w[:, kk, n * 512:(n + 1) * 512],
                                             start=(k == 0), stop=(k == KD - 1))
                        if q == 3 and (t, n) != (1, 1):
                            complete(last, f"{name}{t}{n}")
                    release(last, f"{name}11" if q == 3 else None)

            def attend(h):
                pe.wait_ge(sem("probs_ready"), h + 1)
                turn(f"pT{h}", [(prob[h % 2][:, t, kb * P:(kb + 1) * P], P)
                                for kb in range(TT) for t in range(TT)])
                pe.wait_ge(sem("probsT_ready"), h + 1)
                ps = fill(f"o{h // 2}") if h % 2 == 0 else held(f"o{h // 2}")
                r = 64 * (h % 2)
                for kb in range(TT):
                    last = pe.matmul(ps[r:r + 64, 0:S], vc_t[:, kb, h, :], probT[h % 2][:, kb, :],
                                     start=(kb == 0), stop=(kb == TT - 1))
                if h % 2:
                    complete(last, f"o{h // 2}")

            def memory(h):
                pe.wait_ge(sem("weights_ready"), h + 1)
                w = warg[h % 2]
                parts = {0: [[(0, 0)], [(128, 0), (256, 1)]], 1: [[(384, 0), (512, 1)], [(640, 1)]]}
                for d in range(2):
                    ps = fill(f"mem{h}{d}")
                    for t in range(TT):
                        for n, (c, kt) in enumerate(parts[d][t]):
                            last = pe.matmul(ps[:, t * (AD + 1):(t + 1) * (AD + 1)], w[:, c:c + P],
                                             v_ext[:, kt, h, :], start=(n == 0),
                                             stop=(n == len(parts[d][t]) - 1))
                    complete(last, f"mem{h}{d}")

            modulated = [0]

            def modulate(count):
                for _ in range(count):
                    name = f"ada{modulated[0]}"
                    modulated[0] += 1
                    w = cols(piece(name), 0, KD, S)
                    ps = fill(name)
                    for k in range(KD):
                        last = pe.matmul(ps[:, 0:S], cact[:, k:k + 1].to_broadcast([P, P]), w[:, k, :],
                                         start=(k == 0), stop=(k == KD - 1))
                    release(last, name)

            pe.wait_ge(inputs_landed, 48)
            turn_x("xT", 1)
            w = cols(piece("F0"), 0, KD, S)
            ps = fill("gates_a")
            for half in range(2):
                for k in range(KD):
                    last = pe.matmul(ps[0:64, half * S:(half + 1) * S],
                                     w[:, k, half * 64:half * 64 + 64], xnT[:, k, :],
                                     start=(k == 0), stop=(k == KD - 1))
            release(last, "gates_a")
            for i in range(1, 5):
                feature_major(f"F{i}")
            for i, n in enumerate((256, 256, 160)):
                token_major(f"lat{i}", n)
            for i in range(5, 9):
                feature_major(f"F{i}")
            for i in range(4):
                token_major(f"vo{i}", 256)

            pe.wait_ge(sem("latents_normed"), 1)
            for t in range(TT):
                turn(f"cqT{t}", [(c_t[:, t, i * P:(i + 1) * P], P) for i in range(3)])
                turn(f"ckvT{t}", [(c_t[:, t, CQR + i * P:CQR + (i + 1) * P], P) for i in range(2)])
            pe.wait_ge(sem("latentsT_ready"), 4)
            for half in range(2):
                w = cols(piece(f"uq{half}"), 0, 3, 384)
                for t in range(TT):
                    ps = fill(f"uq{t}{half}")
                    for k in range(3):
                        last = pe.matmul(ps[:, 0:384], cT[:, k, t * P:(t + 1) * P], w[:, k, :],
                                         start=(k == 0), stop=(k == 2))
                    (complete if t == 0 else release)(last, f"uq{t}{half}")
            w = cols(piece("ukv"), 0, 2, 1024)
            for t in range(TT):
                for half in range(2):
                    ps = fill(f"ukv{t}{half}")
                    for k in range(2):
                        last = pe.matmul(ps, cT[:, 3 + k, t * P:(t + 1) * P],
                                         w[:, k, half * 512:(half + 1) * 512],
                                         start=(k == 0), stop=(k == 1))
                    (release if t and half else complete)(last, f"ukv{t}{half}")

            pe.wait_ge(sem("conv_done"), 1)
            ps = fill("conv_sum")
            for j in range(4):
                last = pe.matmul(ps[:, 0:S], ones, uc[:, j, :], start=(j == 0), stop=(j == 3))
            complete(last, "conv_sum")
            pe.wait_ge(sem("c_ready"), 1)
            modulate(6)
            pe.wait_ge(sem("conv_squared"), 1)
            ps = fill("conv_var")
            for j in range(4):
                last = pe.matmul(ps[:, 0:S], ones, usq[:, j, :], start=(j == 0), stop=(j == 3))
            complete(last, "conv_var")

            pe.wait_ge(sem("heads_roped"), 1)
            for g in range(4):
                for t in range(TT):
                    turn(f"hT{g}{t}", [(qk_t[:, t, 4 * g + i, :], P) for i in range(4)])
            pe.wait_ge(sem("headsT_ready"), 8)
            for h in range(CH):
                ps = fill(f"sc{h}")
                for t in range(TT):
                    last = pe.matmul(ps[:, t * S:(t + 1) * S], qkT[0:CQK, h, t * P:(t + 1) * P],
                                     qkT[0:CQK, CH + h, :], start=True, stop=True)
                complete(last, f"sc{h}")
                if h % 2:
                    modulate(1)
                if h:
                    attend(h - 1)
            attend(CH - 1)

            pe.wait_ge(sem("gate_rows"), 1)
            ps = fill("gate_cols")
            for i, r in enumerate((2, 4)):
                for t in range(TT):
                    last = pe.transpose(ps[:, (2 * i + t) * 64:(2 * i + t + 1) * 64],
                                        rows[r][:, t * P:(t + 1) * P], ident[0:64, 0:64])
            complete(last, "gate_cols")
            for h in range(AH):
                ps = fill(f"negA{h}")
                for d in range(2):
                    last = pe.matmul(ps[:, d * S:(d + 1) * S],
                                     ident[0:64, 32 * d + h:32 * d + h + 1].to_broadcast([64, P]),
                                     rows[3], start=True, stop=True)
                complete(last, f"negA{h}")
                ps = fill(f"kq{h}")
                for t in range(TT):
                    last = pe.matmul(ps[:, t * S:(t + 1) * S], fqk[:, 2 * h + 1, t * P:(t + 1) * P],
                                     fqk[:, 2 * h, :], start=True, stop=True)
                complete(last, f"kq{h}")
                if h:
                    modulate(1)
                    memory(h - 1)
            modulate(1)
            memory(AH - 1)
            modulate(2)
            pe.wait_ge(sem("memory_normed"), 1)
            for t in range(TT):
                turn(f"memT{t}", [(h_t[:, t, h, :], P) for h in range(AH)])

            for j in range(4):
                for i in range(3):
                    if j == 0:
                        feature_major(f"g{j}{i}")
                    else:
                        feature_major_by_parts(f"g{j}{i}", 3 * (j - 1) + i + 1, gate_high[i])
                if j == 0:
                    pe.wait_ge(sem("gx_low"), 1)
                    pe.wait_ge(sem("conv_out"), 1)
                    pe.wait_ge(sem("memT_ready"), 2)
                    pe.wait_ge(sem("oT_ready"), 4)
                for i in range(3):
                    if i != 1:
                        wy = piece(f"y{j}{i}")
                    w = cols(wy, 1024 * (i % 2), 4, S)
                    src = (hT, uc, oT)[i]
                    ps = fill(f"y{j}{i}_")
                    for b in range(2):
                        for k in range(4):
                            last = pe.matmul(ps[:, b * S:(b + 1) * S], w[:, k, b * P:(b + 1) * P],
                                             src[:, k, :], start=(k == 0), stop=(k == 3))
                    (release if i else complete)(last, f"y{j}{i}_")
            pe.wait_ge(sem("merged_ready"), 4)
            project("wo", merged)

            turn_x("xU", 2)
            ps = fill("router")
            for t in range(TT):
                for k in range(KD):
                    last = pe.matmul(ps[:, t * E1:(t + 1) * E1], xnT[:, k, t * P:(t + 1) * P],
                                     V("router", k * E1, (k + 1) * E1), start=(k == 0), stop=(k == KD - 1))
            complete(last, "router")
            pe.wait_ge(sem("affinity_ready"), 1)
            turn("affT", [(aff[:, t, :], P) for t in range(TT)])
            pe.wait_ge(sem("slot_rows"), 1)
            turn("slotT", [(slotrow[:, t * P:(t + 1) * P], E1) for t in range(TT)])
            pe.wait_ge(sem("xn_low_ready"), 1)
            pe.wait_ge(sem("onehot_ready"), 1)
            for k in range(KD):
                ps = fill(f"xg{k}")
                for t in range(TT):
                    for part in (xn_high, xn_low):
                        last = pe.matmul(ps, part[:, t, k * P:(k + 1) * P], onehot[:, t, :],
                                         start=(t == 0 and part is xn_high),
                                         stop=(t == TT - 1 and part is xn_low))
                complete(last, f"xg{k}")
            pe.wait_ge(sem("weighted_ready"), 1)
            for t in range(TT):
                turn(f"backT{t}", [(weighted[:, t, g * P:(g + 1) * P], P) for g in range(4)])

            def drain_banks():
                for b in range(8):
                    pe.wait_ge(bank_emptied[b], to_empty[b])

            def piece_in_loop(n, it, rounds):
                pe.wait_ge(landed[n % SLOTS], it * (16 * rounds) + 16 * (n // SLOTS + 1))
                return ring[n % SLOTS].ap()

            drain_banks()
            first1 = len(order)

            pe.nop().then_inc(sem("scattered"), 1)

            def gate_up(n, it, e, i):
                pe.wait_ge(sem("tokens_loaded"), e + 1)
                if i is not None:
                    pe.wait_ge(sem("gated"), e)
                i = i or 0
                for p in range(12):
                    if p == 6 and n != first1:
                        turn_hidden(it, e - 1, i - 1)
                    w = cols(piece_in_loop(n + p, it, 6), 0, 4, 512)
                    for c in range(4):
                        k, m, t = (4 * p + c) // 6, (4 * p + c) // 3 % 2, (4 * p + c) % 3
                        last = pe.matmul(bank[2 * m + i % 2][CAP * t:CAP * (t + 1), :], xe[i % 2][:, k, :],
                                         w[:, c, :], start=(k == 0), stop=(k == KD - 1))
                    last.then_inc(piece_used, 1)

            def turn_hidden(it, e, j):
                pe.wait_ge(sem("gated"), e + 2)
                if j == 0:
                    pe.wait_ge(sem("scatter_read"), it * 4 + 1)
                for c in range(4):
                    last = pe.transpose(bank[7][:, 3 * CAP * c:3 * CAP * (c + 1)],
                                        hid1[j % 2][:, c * P:(c + 1) * P], ident[0:3 * CAP, 0:3 * CAP])
                last.then_inc(sem("hidden_turned"), 1)

            def down(n, it, e, j):
                pe.wait_ge(sem("hiddenT_ready"), e + 1)
                for q in range(6):
                    w = cols(piece_in_loop(n + q, it, 6), 0, 2, 1024)
                    for ff in range(2):
                        f = 2 * q + ff
                        for half in range(2):
                            last = pe.matmul(bank[4 + half][CAP * j:CAP * (j + 1), :],
                                             hid1T[j % 2][:, f % 4, f // 4, :],
                                             w[:, ff, half * 512:(half + 1) * 512],
                                             start=(f == 0), stop=(f == FB1 - 1))
                    last.then_inc(piece_used, 1)

            def group1(it, last_group):
                n = first1 + 12
                for j in range(4):
                    if last_group and j == 3:
                        turn_hidden(it, it * 4 + j, j)
                    else:
                        gate_up(n, it, it * 4 + (j + 1), j + 1)
                        n += 12
                    if j == 0:
                        pe.wait_ge(sem("outputs_read"), it + 1)
                    down(n, it, it * 4 + j, j)
                    n += 6
                pe.wait_ge(sem("outputs_read"), it + 2)
                pe.wait_ge(sem("back_loaded"), it + 1)
                for i in range(4):
                    t, half = divmod(i, 2)
                    pe.wait_ge(sem("scatter_read"), it * 4 + max(i, 1))
                    pe.matmul(bank[6 + i % 2], back_now[:, t * P:(t + 1) * P],
                              y_now[:, half * 512:(half + 1) * 512], start=True,
                              stop=True).then_inc(sem("scattered"), 1)

            for e in range(4 * e1_groups + 1):
                if e < 4 * e1_groups:
                    order.extend(f"e{e}gu{p}" for p in range(12))
                if e:
                    order.extend(f"e{e - 1}d{q}" for q in range(6))
            gate_up(first1, 0, 0, None)
            if e1_groups > 1:
                with pe.Fori(0, e1_groups - 1) as it:
                    group1(it, False)
            group1(e1_groups - 1, True)
            pe.wait_ge(sem("scatter_read"), 4 * e1_groups + 1)

            modulate(2)
            turn_x("xV", 3)
            w = cols(piece("S0"), 0, KD, S)
            ps = fill("rows2")
            for half in range(2):
                for k in range(KD):
                    last = pe.matmul(ps[0:32, half * S:(half + 1) * S], w[:, k, half * 32:half * 32 + 32],
                                     xnT[:, k, :], start=(k == 0), stop=(k == KD - 1))
            release(last, "rows2")
            for i in range(1, 5):
                feature_major(f"S{i}")
            for i in range(2):
                token_major(f"U{i}", S)

            def weighted_keys(n):
                if n:
                    pe.wait_ge(sem("level_ready"), n)
                kk, qq = (hk, hq) if n == 0 else (hK, hQ)
                if n == 0:
                    pe.wait_ge(sem("hk_ready"), 1)
                if n == 1:
                    ps = fill("hx")
                    for h in range(HH):
                        last = pe.matmul(ps[:, h * P:(h + 1) * P], kk[:, 2 * h, :], qq[:, 2 * h + 1, :],
                                         start=True, stop=True)
                    complete(last, "hx")
                    return
                for half in range(2):
                    ps = fill(f"hl{n}{half}")
                    for i in range(4):
                        last = pe.matmul(ps[:, i * P:(i + 1) * P], kk[:, 4 * half + i, :],
                                         qq[:, 4 * half + i, :], start=True, stop=True)
                    complete(last, f"hl{n}{half}")

            for i in range(5, 11):
                feature_major(f"S{i}")
                if i >= 6:
                    weighted_keys(i - 6)
            for i in range(2, 6):
                token_major(f"U{i}", S)
                weighted_keys(i + 3)
            pe.wait_ge(sem("g_rows"), 1)
            ps = fill("gcols")
            for i, r in enumerate((2, 0)):
                for t in range(TT):
                    last = pe.transpose(ps[:, (2 * i + t) * GH:(2 * i + t + 1) * GH],
                                        grow[r][:, t * P:(t + 1) * P], ident[0:GH, 0:GH])
            complete(last, "gcols")
            pe.wait_ge(sem("AT_ready"), 1)
            for t in range(TT):
                ps = fill(f"oB{t}")
                for h in range(HH):
                    last = pe.matmul(ps[:, h * P:(h + 1) * P], AT[:, 2 * h + t, :], iB[:, 4 * t + h, :],
                                     start=True, stop=(t == 0))
                    if t:
                        last = pe.matmul(ps[:, h * P:(h + 1) * P], ATx[:, h, :], iB[:, h, :],
                                         start=False, stop=True)
                complete(last, f"oB{t}")
            for h in range(GH):
                ps = fill(f"bc{h}")
                for i, r in enumerate((2, 0)):
                    last = pe.matmul(ps[:, i * S:(i + 1) * S], ident[0:GH, h:h + 1].to_broadcast([GH, P]),
                                     grow[r], start=True, stop=True)
                complete(last, f"bc{h}")
            pe.wait_ge(sem("qk_squared"), 1)
            for i in range(4):
                ps = fill(f"l2{i}")
                for b in range(2):
                    last = pe.matmul(ps[:, b * S:(b + 1) * S], ones, qk_ss[:, 2 * i + b, :],
                                     start=True, stop=True)
                complete(last, f"l2{i}")
            modulate(3)
            pe.wait_ge(sem("qk_unit"), 1)
            for h in range(GH):
                ps = fill(f"kk{h}")
                q, k = qkv[:, h, :], qkv[:, 4 + h, :]
                for t in range(TT):
                    tile = slice(t * P, (t + 1) * P)
                    pe.matmul(ps[:, t * P:(t + 1) * P], k[:, tile], k[:, tile], start=True, stop=True)
                    last = pe.matmul(ps[:, S + t * P:S + (t + 1) * P], k[:, tile], q[:, tile],
                                     start=True, stop=True)
                complete(last, f"kk{h}")
            for t in range(TT):
                for n, b0 in (("kt", 4), ("vt", 8)):
                    turn(f"{n}{t}", [(qkv[:, b0 + h, t * P:(t + 1) * P], P) for h in range(GH)])
            for half in range(2):
                pe.wait_ge(sem("U_ready"), half + 1)
                turn(f"T0{half}", [(Ui[:, 4 * half + i, :], P) for i in range(4)])
            for n in range(1, LEVELS):
                for half in range(2):
                    if n == 1:
                        pe.wait_ge(sem("T_ready"), half + 1)
                    else:
                        pe.wait_ge(*was_emptied(f"TX{n - 1}{half}"))
                    pe.wait_ge(sem("Lm_ready"), 2 * (n - 1) + half + 1)
                    ps = fill(f"X{n}{half}")
                    for i in range(4 * half, 4 * half + 4):
                        last = pe.matmul(ps[:, (i % 4) * P:(i % 4 + 1) * P], Lm[:, i, :], Ti[:, i, :],
                                         start=True, stop=True)
                    complete(last, f"X{n}{half}")
                for half in range(2):
                    pe.wait_ge(sem("X_ready"), 2 * (n - 1) + half + 1)
                    pe.wait_ge(sem("U_ready"), 2 * n + half - 1 if n > 1 else half + 1)
                    if n < LEVELS - 1:
                        ps = fill(f"TX{n}{half}")
                        for i in range(4 * half, 4 * half + 4):
                            last = pe.matmul(ps[:, (i % 4) * P:(i % 4 + 1) * P], Ui[:, i, :], Xi[:, i, :],
                                             start=True, stop=True)
                        complete(last, f"TX{n}{half}")
                for half in range(2):
                    ps = fill(f"XU{n}{half}")
                    for i in range(4 * half, 4 * half + 4):
                        last = pe.matmul(ps[:, (i % 4) * P:(i % 4 + 1) * P], Xi[:, i, :], Ui[:, i, :],
                                         start=True, stop=True)
                    complete(last, f"XU{n}{half}")
            pe.wait_ge(sem("U_ready"), 2 * LEVELS)
            modulate(1)
            pe.wait_ge(sem("vb_ready"), 1)

            def per_head(name, terms):
                ps = fill(name)
                for h in range(GH):
                    pairs = terms(h)
                    for n, (l, r) in enumerate(pairs):
                        last = pe.matmul(ps[:, h * P:(h + 1) * P], l, r, start=(n == 0),
                                         stop=(n == len(pairs) - 1))
                complete(last, name)

            for t in range(TT):
                per_head(f"u{t}", lambda h: [(Ui[:, 2 * h + t, :], vb[:, 4 * t + h, :])])
            per_head("wT", lambda h: [(kbe[:, h, :], Ui[:, 2 * h + 1, :])])
            pe.wait_ge(sem("u_ready"), 2)
            per_head("state", lambda h: [(ktail[:, h, :], uu[:, h, :])])
            per_head("oA0", lambda h: [(attnT[:, 2 * h, :], uu[:, h, :])])
            pe.wait_ge(sem("S1_ready"), 1)
            per_head("wS", lambda h: [(wT[:, h, :], S1[:, h, :])])
            pe.wait_ge(sem("vnew_ready"), 1)
            per_head("oA1", lambda h: [(qd[:, h, :], S1[:, h, :]), (attnT[:, 2 * h + 1, :], vnew[:, h, :])])
            modulate(2)
            pe.wait_ge(sem("o_ready"), 1)
            for t in range(TT):
                for half in range(2):
                    turn(f"oo{t}{half}", [(o_t[:, t, (4 * half + i) * P:(4 * half + i + 1) * P], P)
                                          for i in range(4)])
            pe.wait_ge(sem("mod_ready"), 1)
            for g in range(4):
                ps = fill(f"gate_rows{g}")
                for i in range(4):
                    j = 32 + 4 * g + i
                    last = pe.matmul(ps[:, i * P:(i + 1) * P], modc[:, j:j + 1].to_broadcast([P, P]), ident,
                                     start=True, stop=True)
                complete(last, f"gate_rows{g}")

            pe.wait_ge(sem("oT2_ready"), 4)
            project("wp", oT2)

            turn_x("xW", 4)
            ps = fill("router2")
            for t in range(TT):
                for k in range(KD):
                    last = pe.matmul(ps[:, t * E2:(t + 1) * E2], xnT[:, k, t * P:(t + 1) * P],
                                     V("router2", k * E2, (k + 1) * E2), start=(k == 0), stop=(k == KD - 1))
            complete(last, "router2")
            drain_banks()
            first2 = len(order)
            order.extend(["r64a", "r64b", "r0a", "r64d", "r0b"])
            for e in range(4 * e2_groups):
                if e + 1 < 4 * e2_groups:
                    order.append(f"r{e + 1}a")
                order.append(f"r{e}d")
                if e + 1 < 4 * e2_groups:
                    order.append(f"r{e + 1}b")

            def parts_of(n, it, *dims):
                pe.wait_ge(sem("rest_ready"), it * SLOTS + (n - first2 + 1))
                return (cols(w_high[(n - first2) % HIGHS], 0, *dims), cols(ring_r[n % SLOTS].ap(), 0, *dims))

            def gate_up2(n, it, b):
                wh, wl = parts_of(n, it, KD, S)
                for m in range(2):
                    for k in range(KD):
                        for i, (w, x) in enumerate(((wh, x_high), (wh, x_low), (wl, x_high))):
                            last = pe.matmul(bank[b][:, m * S:(m + 1) * S], w[:, k, m * P:(m + 1) * P],
                                             x[:, k, :], start=(k == 0 and i == 0),
                                             stop=(k == KD - 1 and i == 2))
                last.then_inc(piece_used, 1)

            pe.nop().then_inc(sem("gate_spread"), 1)

            def spread_gate(e, i):
                pe.wait_ge(sem("gate_row"), e)
                for part in range(2):
                    last = pe.matmul(bank[2 + i % 2][:, 0:S], ones_r, grow2[i % 2][:, part * S:(part + 1) * S],
                                     start=(part == 0), stop=(part == 1))
                last.then_inc(sem("gate_spread"), 1)

            def down2(n, it, i, first=False, final=False):
                wh, wl = parts_of(n, it, 2, 1024)
                high, low = hid2[i % 2]
                for b in range(2):
                    for t in range(TT):
                        tile = slice(t * P, (t + 1) * P)
                        for half in range(2):
                            c = slice(half * 512, (half + 1) * 512)
                            for j, (h, w) in enumerate(((high, wh), (high, wl), (low, wh))):
                                last = pe.matmul(bank[4 + 2 * t + half], h[b][:, tile], w[:, b, c],
                                                 start=(first and b == 0 and j == 0),
                                                 stop=(final and b == 1 and j == 2))
                last.then_inc(piece_used, 1)

            def group2(it, last_group):
                n = first2 + 5
                for i in range(1, 5):
                    e = it * 4 + i
                    more = not (last_group and i == 4)
                    if more:
                        pe.wait_ge(sem("hidden2"), e * 2 + 1)
                        spread_gate(e + 1, i + 1)
                        gate_up2(n, it, 0)
                        n += 1
                    pe.wait_ge(sem("hidden2"), e * 2 + 2)
                    down2(n, it, i, final=not more)
                    n += 1
                    if more:
                        gate_up2(n, it, 1)
                        n += 1

            pe.wait_ge(sem("x_low_ready"), 1)
            pe.wait_ge(sem("x_high_ready"), 1)
            gate_up2(first2, 0, 0)
            gate_up2(first2 + 1, 0, 1)
            pe.wait_ge(sem("hidden2"), 1)
            gate_up2(first2 + 2, 0, 0)
            pe.wait_ge(sem("gates2_ready"), 1)
            for t in range(TT):
                last = pe.transpose(bank[7][0:E2, t * P:(t + 1) * P], chosen[:, t, :], ident)
            last.then_inc(sem("gates_turned"), 1)
            spread_gate(1, 1)
            pe.wait_ge(sem("hidden2"), 2)
            pe.wait_ge(sem("gT_ready"), 1)
            down2(first2 + 3, 0, 0, first=True)
            gate_up2(first2 + 4, 0, 1)
            if e2_groups > 1:
                with pe.Fori(0, e2_groups - 1) as it:
                    group2(it, False)
            group2(e2_groups - 1, True)

        @block.scalar
        def _(act):
            steps = Steps(act, sem("scalar_steps"))
            act.wait_ge(inputs_landed, 48)

            def inverse_root(out_, in_, n):
                steps.link(act.activation(out_, in_, ACT.Ln, scale=1.0 / n,
                                          bias=C("eps")[0:in_.shape[0]]))
                return act.activation(out_, out_, ACT.Exp, scale=-0.5)

            def square_sums(n, updated=None):
                for t in range(TT):
                    if updated:
                        act.wait_ge(updated, t + 1)
                    steps.mark(act.activation(xn_t[:, t, :], x_t[:, t, :], ACT.Square,
                                              accum_out=sq_sum[:, t:t + 1]))
                steps.settle()
                inverse_root(rstd, sq_sum, D).then_inc(sem("rstd_ready"), 1)

            act.preload_act_table_set("natural_log_exp_and_others")
            square_sums(1)
            act.preload_act_table_set("sigmoid_and_others")
            act.activation(cact, V("c"), ACT.Sigmoid).then_inc(sem("c_sig"), 1)
            for j in range(4):
                act.wait_ge(*full(f"F{j + 1}"))
                act.activation(sig_u[:, j, :], held(f"F{j + 1}")[:, S:2 * S],
                               ACT.Sigmoid).then_inc(sem("glu_gate"), 1)
            act.wait_ge(sem("xnT_ready"), 4)
            for i, n in enumerate((256, 256, 160)):
                act.wait_ge(*full(f"lat{i}"))
                act.activation(c_t[:, :, 256 * i:256 * i + n], cols(held(f"lat{i}"), 0, TT, S)[:, :, 0:n],
                               ACT.Copy).then_inc(emptied(f"lat{i}"), 1)
            for i in range(3):
                act.wait_ge(*was_emptied(f"lat{i}"))
            for t in range(TT):
                for i, (a, b) in enumerate(((0, CQR), (CQR, CQR + CKR))):
                    steps.mark(act.activation(junk[:, 0:b - a], c_t[:, t, a:b], ACT.Square,
                                              accum_out=ss_c[:, 2 * i + t:2 * i + t + 1]))
                    steps.settle()
            for h in range(AH):
                act.wait_ge(*full(f"F{h + 5}"))
                act.activation(fqk[:, 2 * h:2 * h + 2, :], cols(held(f"F{h + 5}"), 0, 2, S),
                               ACT.Copy).then_inc(emptied(f"F{h + 5}"), 1)
            for i in range(2):
                act.wait_ge(*full(f"vo{i}"))
                for t in range(TT):
                    ins = act.activation(v_ext[:, t, 2 * i:2 * i + 2, 0:AD],
                                         cols(held(f"vo{i}"), t * S, 2, AD), ACT.Copy)
                ins.then_inc(emptied(f"vo{i}"), 1)
            for i in range(2):
                act.wait_ge(*full(f"vo{i + 2}"))
                act.activation(so_t[:, :, S * i:S * (i + 1)], cols(held(f"vo{i + 2}"), 0, TT, S),
                               ACT.Sigmoid).then_inc(emptied(f"vo{i + 2}"), 1)
            act.preload_act_table_set("natural_log_exp_and_others")
            steps.mark(inverse_root(rs_c[:, 0:2], ss_c[:, 0:2], CQR))
            steps.mark(inverse_root(rs_c[:, 2:4], ss_c[:, 2:4], CKR))
            steps.settle()
            for t in range(TT):
                for i, (a, b) in enumerate(((0, CQR), (CQR, CQR + CKR))):
                    n = steps.mark(act.activation(c_t[:, t, a:b], c_t[:, t, a:b], ACT.Copy,
                                                  scale=rs_c[:, 2 * i + t:2 * i + t + 1]))
            steps.settle()
            act.nop().then_inc(sem("latents_normed"), 1)

            act.wait_ge(sem("forget_abs"), 1)
            steps.link(act.activation(rows[4], rows[4], ACT.Exp, scale=-1.0))
            act.activation(rows[4], rows[4], ACT.Ln, bias=1.0).then_inc(sem("forget_log"), 1)

            for half in range(2):
                for t in range(TT):
                    act.wait_ge(*full(f"uq{t}{half}"))
                    act.activation(qk_t[:, t, 4 * half:4 * half + 4, :],
                                   cols(held(f"uq{t}{half}"), 0, 4, CQK),
                                   ACT.Copy).then_inc(emptied(f"uq{t}{half}"), 1)
            for t in range(TT):
                steps.mark(act.activation(
                    qk_t[:, t, CH:2 * CH, CN:CQK],
                    c_t[:, t, CQR + CKR:CQR + CKR + CR].unsqueeze(1).to_broadcast([P, CH, CR]), ACT.Copy))
            for t in range(TT):
                for half in range(2):
                    act.wait_ge(*full(f"ukv{t}{half}"))
                    kv = cols(held(f"ukv{t}{half}"), 0, 4, CN + CV)
                    steps.mark(act.activation(qk_t[:, t, CH + 4 * half:CH + 4 * half + 4, 0:CN],
                                              kv[:, :, 0:CN], ACT.Copy))
                    act.activation(vc_t[:, t, 4 * half:4 * half + 4, :], kv[:, :, CN:CN + CV],
                                   ACT.Copy).then_inc(emptied(f"ukv{t}{half}"), 1)
            steps.settle()
            for half in range(2):
                for t in range(TT):
                    act.wait_ge(*was_emptied(f"uq{t}{half}"))
            act.activation(qk_sq, qk_t, ACT.Square).then_inc(sem("heads_squared"), 1)
            act.wait_ge(sem("head_sums"), 1)
            inverse_root(qkrs, qkss, CQK).then_inc(sem("head_rstd"), 1)
            act.wait_ge(sem("conv_centred"), 1)
            act.activation(usq, uc, ACT.Square).then_inc(sem("conv_squared"), 1)
            act.wait_ge(*full("conv_var"))
            steps.link(act.activation(usq[:, 0, :], held("conv_var")[:, 0:S], ACT.Ln, scale=1.0 / BW,
                                      bias=C("eps")))
            steps.link(act.activation(usq[:, 0, :], usq[:, 0, :], ACT.Exp, scale=-0.5))
            act.nop().then_inc(emptied("conv_var"), 1)
            act.nop().then_inc(sem("conv_rstd"), 1)
            for g in range(4):
                for t in range(TT):
                    act.wait_ge(*full(f"hT{g}{t}"))
                    ins = act.activation(qkT[0:CQK, 4 * g:4 * g + 4, t * P:(t + 1) * P],
                                         cols(held(f"hT{g}{t}"), 0, 4, P)[0:CQK], ACT.Copy)
                    ins.then_inc(emptied(f"hT{g}{t}"), 1)
            for g in range(4):
                for t in range(TT):
                    act.wait_ge(*was_emptied(f"hT{g}{t}"))
            act.nop().then_inc(sem("headsT_ready"), 8)

            def read_attention(h):
                act.wait_ge(*full(f"pT{h}"))
                if h >= 2:
                    act.wait_ge(*full(f"o{h // 2 - 1}"))
                steps.link(act.activation(probT[h % 2].rearrange("p t s -> p (t s)"), held(f"pT{h}"),
                                          ACT.Copy))
                act.nop().then_inc(emptied(f"pT{h}"), 1)
                act.nop().then_inc(sem("probsT_ready"), 1)
                if h % 2:
                    act.wait_ge(*full(f"o{h // 2}"))
                    steps.link(act.activation(oT[:, h // 2, :], held(f"o{h // 2}")[:, 0:S], ACT.Copy))
                    act.nop().then_inc(emptied(f"o{h // 2}"), 1)
                    act.nop().then_inc(sem("oT_ready"), 1)

            for h in range(CH):
                act.wait_ge(sem("score_max"), h + 1)
                for t in range(TT):
                    i = 2 * h + t
                    ins = act.activation(prob[h % 2][:, t, :], held(f"sc{h}")[:, t * S:(t + 1) * S],
                                         ACT.Exp, scale=CQK ** -0.5, bias=smax[:, i:i + 1],
                                         accum_out=ssum[:, i:i + 1])
                    steps.mark(ins)
                steps.settle()
                act.nop().then_inc(emptied(f"sc{h}"), 1)
                act.nop().then_inc(sem("probs_summed"), 1)
                if h:
                    read_attention(h - 1)
            read_attention(CH - 1)

            act.wait_ge(sem("floor_rows"), 1)
            act.activation(rows[4], rows[4], ACT.Exp, scale=-1.0).then_inc(sem("gate_rows"), 1)
            for h in range(AH):
                act.wait_ge(sem("weight_args"), h + 1)
                act.activation(warg[h % 2], warg[h % 2], ACT.Exp).then_inc(sem("weight_exps"), 1)
            act.wait_ge(sem("memory_sums"), 1)
            inverse_root(hrs, hss, AD).then_inc(sem("memory_rstd"), 1)

            act.preload_act_table_set("sigmoid_and_others")
            act.wait_ge(sem("conv_affine"), 1)
            act.activation(usq, uc, ACT.Sigmoid).then_inc(sem("conv_sig"), 1)
            act.wait_ge(*full("memT1"))
            act.activation(gx_high, xnT, ACT.Copy).then_inc(sem("gx_high"), 1)
            for j in range(4):
                for i in range(3):
                    act.wait_ge(*full(f"g{j}{i}"))
                    if j:
                        act.wait_ge(sem("merged_ready"), j)
                    steps.link(act.activation(gsig[:, i, :], held(f"g{j}{i}"), ACT.Sigmoid))
                    act.nop().then_inc(emptied(f"g{j}{i}"), 1)
                    act.nop().then_inc(sem("branch_gate"), 1)
                    if j < 3:
                        n = order.index(f"g{j + 1}{i}")
                        act.wait_ge(landed[n % SLOTS], 16 * (n // SLOTS + 1))
                        act.activation(gate_high[i], ring[n % SLOTS].ap(), ACT.Copy).then_inc(sem("gate_high"), 1)

            act.preload_act_table_set("natural_log_exp_and_others")
            square_sums(2, sem("x_updated"))
            act.wait_ge(sem("logits_shifted"), 1)
            act.activation(aff, aff, ACT.Exp).then_inc(sem("affinity_exp"), 1)
            act.wait_ge(sem("x_normed"), 2)
            act.activation(xn_high, xn_t, ACT.Copy).then_inc(sem("xn_high_ready"), 1)
            for k in range(1, KD, 2):
                act.wait_ge(*full(f"xg{k}"))
                steps.link(act.activation(xg[:, k, :], held(f"xg{k}"), ACT.Copy,
                                          scale=V("ffn_g", k, k + 1)))
                act.nop().then_inc(emptied(f"xg{k}"), 1)
                act.nop().then_inc(sem("xg_read"), 1)
            for t in range(TT):
                act.wait_ge(*full(f"backT{t}"))
                steps.link(act.activation(backT[:, :, t * P:(t + 1) * P], cols(held(f"backT{t}"), 0, 4, P),
                                          ACT.Copy))
                act.nop().then_inc(emptied(f"backT{t}"), 1)
                act.nop().then_inc(sem("back_ready"), 1)
            act.preload_act_table_set("silu_and_others")
            first1 = order.index("e0gu0")

            act.nop().then_inc(sem("outputs_read"), 1)

            def gate_of(it, j):
                done = first1 + 12 if j == 0 else it * 72 + (first1 + 6 + 18 * j)
                act.wait_ge(piece_used, done)
                if j:
                    act.wait_ge(sem("gated"), it * 4 + j)
                act.activation(gate1[j % 2], bank[j % 2][0:3 * CAP, :],
                               ACT.Silu).then_inc(sem("gate_silu"), 1)

            def outputs_of(it, last_group):
                act.wait_ge(piece_used, it * 72 + (first1 + (72 if last_group else 84)))
                act.wait_ge(sem("scattered"), it * 4 + 1)
                for half in range(2):
                    ins = act.activation(y_now[:, half * 512:(half + 1) * 512], bank[4 + half], ACT.Copy)
                ins.then_inc(sem("outputs_read"), 1)

            gate_of(0, 0)
            if e1_groups > 1:
                with act.Fori(0, e1_groups - 1) as it:
                    for j in range(1, 5):
                        gate_of(it, j)
                    outputs_of(it, False)
            for j in range(1, 4):
                gate_of(e1_groups - 1, j)
            outputs_of(e1_groups - 1, True)

            def read(name, out_, width=512, func=ACT.Copy, **kw):
                act.wait_ge(*full(name))
                n = out_.shape[0]
                act.activation(out_, held(name)[0:n, 0:width], func, **kw).then_inc(emptied(name), 1)

            def put(name, out_, **kw):
                read(name, out_, **kw)
                act.wait_ge(*was_emptied(name))

            def wide(v):
                return v.rearrange("p a b -> p (a b)")

            def modulated_rest(name):
                shift = modc[:, 0:8] if name == "xV" else modc[:, 16:24]
                act.wait_ge(sem("scales_ready"), 1 if name == "xV" else 2)
                for t in range(TT):
                    act.wait_ge(*full(f"{name}{t}1"))
                    for i in range(4):
                        k = 4 + i
                        ins = act.activation(xnT[:, k, t * P:(t + 1) * P],
                                             held(f"{name}{t}1")[:, i * P:(i + 1) * P], ACT.Identity,
                                             scale=scol1[:, k:k + 1], bias=shift[:, k:k + 1])
                    ins.then_inc(emptied(f"{name}{t}1"), 1)
                    act.wait_ge(*was_emptied(f"{name}{t}1"))
                    act.nop().then_inc(sem("xnT_ready"), 1)

            act.wait_ge(sem("scatter_read"), 4 * e1_groups + 1)
            act.preload_act_table_set("natural_log_exp_and_others")
            square_sums(3)
            modulated_rest("xV")
            act.activation(nexpa, V("a_log")[0:GH], ACT.Exp).then_inc(sem("decay_rate"), 1)
            act.preload_act_table_set("sigmoid_and_others")
            act.wait_ge(sem("lb_diff"), 1)
            act.activation(lb, lb, ACT.Sigmoid).then_inc(sem("lb_ready"), 1)
            act.wait_ge(*full("rows2"))
            act.activation(grow[0], held("rows2")[0:GH, 0:S], ACT.Sigmoid)
            act.activation(grow[1], held("rows2")[0:GH, S:2 * S], ACT.Identity,
                           bias=V("dt")[0:GH]).then_inc(emptied("rows2"), 1)
            for i in range(2):
                act.wait_ge(*full(f"S{i + 1}"))
                steps.mark(act.activation(wide(hsig)[:, 512 * i:512 * (i + 1)], held(f"S{i + 1}"), ACT.Sigmoid))
                read(f"S{i + 1}", wide(hk)[:, 512 * i:512 * (i + 1)], func=ACT.Sigmoid, scale=-1.0)
            for i in range(2):
                act.wait_ge(*was_emptied(f"S{i + 1}"))
            act.nop().then_inc(sem("keep_sig"), 1)
            act.preload_act_table_set("silu_and_others")
            for i in range(2):
                put(f"S{i + 3}", wide(hq)[:, 512 * i:512 * (i + 1)], func=ACT.Silu)
            act.nop().then_inc(sem("hq_ready"), 1)
            for i in range(2):
                act.wait_ge(*full(f"U{i}"))
                for t in range(TT):
                    ins = act.activation(iB[:, 4 * t + 2 * i:4 * t + 2 * i + 2, :],
                                         cols(held(f"U{i}"), t * S, 2, P), ACT.Copy)
                ins.then_inc(emptied(f"U{i}"), 1)
            act.preload_act_table_set("natural_log_exp_and_others")
            steps.settle()
            act.wait_ge(sem("oml_ready"), 1)
            for h in range(HH):
                steps.mark(act.activation(hb[:, 2 * h:2 * h + 2, :], hsig[:, 2 * h:2 * h + 2, :], ACT.Ln,
                                          scale=oml[:, h:h + 1], bias=lb[:, h:h + 1]))
            steps.settle()
            act.nop().then_inc(sem("logf_ready"), 1)
            act.wait_ge(sem("decay_abs"), 1)
            steps.link(act.activation(grow[2], grow[2], ACT.Exp, scale=-1.0))
            act.activation(grow[2], grow[2], ACT.Ln, bias=1.0).then_inc(sem("decay_log"), 1)
            for n in range(1, 9):
                act.wait_ge(sem("level_args"), n)
                act.activation(hE, hE, ACT.Exp).then_inc(sem("level_exps"), 1)
                if n <= 6:
                    name = f"S{n + 4}"
                    act.wait_ge(*full(name))
                    act.activation(pad2[:, 2 * (n - 1):2 * n, CONV2 - 1:], cols(held(name), 0, 2, S),
                                   ACT.Copy).then_inc(emptied(name), 1)
                if n == 2:
                    put("hx", wide(ATx))
            act.preload_act_table_set("silu_and_others")
            for i in range(4):
                act.wait_ge(*full(f"U{i + 2}"))
                act.activation(z_gate[:, :, S * i:S * (i + 1)], cols(held(f"U{i + 2}"), 0, TT, S),
                               ACT.Silu).then_inc(emptied(f"U{i + 2}"), 1)
            for t in range(TT):
                put(f"oB{t}", o_t[:, t, 512:1024])
            act.wait_ge(sem("conv2_done"), 1)
            steps.link(act.activation(wide(qkv), wide(qkv), ACT.Silu))
            act.wait_ge(sem("AT_ready"), 1)
            act.activation(wide(qk_ss), wide(qkv)[:, 0:8 * S], ACT.Square).then_inc(sem("qk_squared"), 1)
            act.preload_act_table_set("natural_log_exp_and_others")
            for h in range(GH):
                act.wait_ge(*full(f"bc{h}"))
                steps.mark(act.activation(egb[:, h, :], held(f"bc{h}")[:, P:2 * P], ACT.Exp))
                steps.mark(act.activation(dec[:, 2 * h:2 * h + 2, :], cols(held(f"bc{h}"), 0, 2, P), ACT.Copy))
                act.activation(attnT[:, 2 * h:2 * h + 2, :], cols(held(f"bc{h}"), S, 2, P),
                               ACT.Copy).then_inc(emptied(f"bc{h}"), 1)
            steps.settle()
            act.nop().then_inc(sem("bc_read"), 1)
            act.wait_ge(sem("dec_args"), 1)
            steps.link(act.activation(wide(dec), wide(dec), ACT.Exp))
            act.nop().then_inc(sem("dec_exps"), 1)
            for i in range(4):
                act.wait_ge(*full(f"l2{i}"))
            for i in range(4):
                v = wide(qk_ss)[:, 512 * i:512 * (i + 1)]
                put(f"l2{i}", v, func=ACT.Ln, bias=C("eps"))
                steps.mark(act.activation(v, v, ACT.Exp, scale=-0.5))
            steps.settle()
            act.nop().then_inc(sem("unit_ready"), 1)
            act.wait_ge(sem("col_args"), 1)
            steps.link(act.activation(small[:, 68:76], small[:, 68:76], ACT.Exp))
            act.nop().then_inc(sem("col_exps"), 1)
            for t in range(TT):
                put(f"kt{t}", wide(k_t)[:, 512 * t:512 * (t + 1)])
                put(f"vt{t}", wide(v_t)[:, 512 * t:512 * (t + 1)])
            act.nop().then_inc(sem("kv_turned"), 1)
            for half in range(2):
                put(f"T0{half}", wide(Ti)[:, 512 * half:512 * (half + 1)])
                act.nop().then_inc(sem("T_ready"), 1)
            for n in range(1, LEVELS):
                for half in range(2):
                    if n > 1:
                        act.wait_ge(*full(f"XU{n - 1}{half}"))
                    put(f"X{n}{half}", wide(Xi)[:, 512 * half:512 * (half + 1)])
                    act.nop().then_inc(sem("X_ready"), 1)
                if n <= TT:
                    steps.link(act.activation(wide(hq)[:, 0:512], o_t[:, n - 1, 512:1024], ACT.Square,
                                              accum_out=oss[:, 7 + n:8 + n]))
            for t in range(TT):
                put(f"u{t}", wide(uu)[:, 512 * t:512 * (t + 1)])
                act.nop().then_inc(sem("u_ready"), 1)
            put("wT", wide(wT))
            act.wait_ge(*full("oA0"))
            put("state", wide(S1))
            act.nop().then_inc(sem("S1_ready"), 1)
            for t in range(TT):
                put(f"oA{t}", o_t[:, t, 0:512])
                for h in range(GH):
                    steps.link(act.activation(wide(hq)[:, 0:P], o_t[:, t, h * P:(h + 1) * P],
                                              ACT.Square, accum_out=oss[:, 4 * t + h:4 * t + h + 1]))
            steps.mark(inverse_root(ors[:, 0:8], oss[:, 0:8], P))
            steps.mark(inverse_root(ors[:, 8:10], oss[:, 8:10], HH * P))
            steps.settle()
            act.nop().then_inc(sem("o_rstd"), 1)

            first2 = order.index("r64a")

            def high_part(p, it=0):
                n = first2 + p
                act.wait_ge(landed[n % SLOTS], it * 16 + 16 * (n // SLOTS + 1))
                if p >= HIGHS:
                    act.wait_ge(piece_used, it * SLOTS + (n - HIGHS + 1))
                act.activation(w_high[p % HIGHS], ring[n % SLOTS].ap(), ACT.Copy).then_inc(sem("high_ready"), 1)

            act.wait_ge(sem("o_ready"), 1)
            for g in range(4):
                act.wait_ge(*full(f"gate_rows{g}"))
                act.activation(gmod[:, 512 * g:512 * (g + 1)], held(f"gate_rows{g}"),
                               ACT.Copy).then_inc(emptied(f"gate_rows{g}"), 1)
            for p in range(AHEAD + 1):
                high_part(p)
            square_sums(4, sem("x_updated2"))
            act.dma_start(finw, finw_in).then_inc(sem("final_w_landed"), 16)
            modulated_rest("xW")
            act.wait_ge(sem("xnT_ready"), 16)
            act.activation(ones_r, ones[0:E2], ACT.Copy)
            act.activation(x_high, xnT, ACT.Copy).then_inc(sem("x_high_ready"), 1)
            act.preload_act_table_set("sigmoid_and_others")
            act.wait_ge(*full("router2"))
            act.activation(wide(score), held("router2")[:, 0:TT * E2],
                           ACT.Sigmoid).then_inc(emptied("router2"), 1)
            act.wait_ge(*was_emptied("router2"))
            act.nop().then_inc(sem("scores_ready"), 1)
            act.preload_act_table_set("silu_and_others")

            def gate_of2(p, it, b):
                act.wait_ge(piece_used, it * SLOTS + (first2 + p + 1))
                act.activation(silu2[b], bank[b][:, 0:S], ACT.Silu).then_inc(sem("silu2"), 1)

            gate_of2(0, 0, 0)
            for p in range(1, 5):
                high_part(p + AHEAD)
                if p != 3:
                    gate_of2(p, 0, (0, 1, 0, 1, 1)[p])

            def parts_group(it, n_pieces):
                for q in range(n_pieces):
                    if q + AHEAD < n_pieces or n_pieces == SLOTS:
                        high_part(5 + q + AHEAD, it)
                    if q % 3 != 1 and (q < 9 or n_pieces == SLOTS):
                        gate_of2(5 + q, it, q % 3 // 2)

            if e2_groups > 1:
                with act.Fori(0, e2_groups - 1) as it:
                    parts_group(it, SLOTS)
            parts_group(e2_groups - 1, SLOTS - 2)
            act.preload_act_table_set("natural_log_exp_and_others")
            for t in range(TT):
                act.wait_ge(sem("x_updated3"), t + 1)
                steps.link(act.activation(xn_t[:, t, :], x_t[:, t, :], ACT.Square,
                                          accum_out=sq_sum[:, t:t + 1]))
                inverse_root(rstd[:, t:t + 1], sq_sum[:, t:t + 1], D).then_inc(sem("rstd_ready"), 1)

        @block.vector
        def _(dve):
            steps = Steps(dve, sem("vector_steps"))
            tt, ts, stt = dve.tensor_tensor, dve.tensor_scalar, dve.scalar_tensor_tensor
            steps.mark(dve.memset(u_pad, 0.0))
            steps.mark(dve.memset(v_ext[:, :, :, AD:AD + 1], 1.0))
            for r in (1, 2, 3, 4, 5):
                steps.mark(dve.memset(rows[r], 0.0))
            steps.settle()
            dve.wait_ge(inputs_landed, 48)

            def scale_x(n):
                dve.wait_ge(sem("rstd_ready"), n)
                for t in range(TT):
                    steps.mark(ts(xn_t[:, t, :], x_t[:, t, :], rstd[:, t:t + 1], None, ALU.mult))
                steps.settle()
                dve.nop().then_inc(sem("x_normed"), 1)

            def read_turned(name, gain):
                for t in range(TT):
                    for hk in range(2):
                        dve.wait_ge(*full(f"{name}{t}{hk}"))
                        steps.link(tt(xnT[:, 4 * hk:4 * hk + 4, t * P:(t + 1) * P],
                                      cols(held(f"{name}{t}{hk}"), 0, 4, P),
                                      spread(gain[:, 4 * hk:4 * hk + 4], P), ALU.mult))
                        dve.nop().then_inc(emptied(f"{name}{t}{hk}"), 1)
                        dve.nop().then_inc(sem("xnT_ready"), 1)

            read_parts = [0]

            def read_modulation(count):
                for _ in range(count):
                    i = read_parts[0]
                    read_parts[0] += 1
                    dve.wait_ge(*full(f"ada{i}"))
                    tt(diagonal, cols(held(f"ada{i}"), 0, 2, P), repeated(ident, 2),
                       ALU.mult).then_inc(emptied(f"ada{i}"), 1)
                    dve.wait_ge(*was_emptied(f"ada{i}"))
                    steps.link(dve.tensor_reduce(modc[:, 2 * i:2 * i + 2], diagonal, AX.X, ALU.add))

            scale_x(1)
            read_turned("xT", V("mix_g"))
            dve.wait_ge(sem("c_sig"), 1)
            tt(cact, cact, V("c"), ALU.mult).then_inc(sem("c_ready"), 1)

            dve.wait_ge(*full("gates_a"))
            ga = held("gates_a")
            steps.mark(ts(rows[0], ga[0:64, 0:S], V("b_i")[0:64], None, ALU.add))
            steps.link(ts(rows[1], ga[0:64, S:2 * S], V("b_f")[0:64], None, ALU.add))
            dve.nop().then_inc(emptied("gates_a"), 1)
            stt(rows[4], rows[1], -1.0, rows[1], ALU.mult, ALU.max).then_inc(sem("forget_abs"), 1)

            for j in range(4):
                dve.wait_ge(sem("glu_gate"), j + 1)
                steps.link(tt(u_pad[:, j, BK // 2:BK // 2 + S], held(f"F{j + 1}")[:, 0:S],
                              sig_u[:, j, :], ALU.mult))
                dve.nop().then_inc(emptied(f"F{j + 1}"), 1)
            taps = [0] * 4
            for k in range(BK):
                for j in range(4):
                    tap = V("conv_w", 31 * j + k, 31 * j + k + 1)
                    if k == 0:
                        ins = ts(uc[:, j, :], u_pad[:, j, 0:S], tap, V("conv_b", j, j + 1), ALU.mult, ALU.add)
                    else:
                        steps.settle(taps[j])
                        ins = stt(uc[:, j, :], u_pad[:, j, k:k + S], tap, uc[:, j, :], ALU.mult, ALU.add)
                    taps[j] = steps.mark(ins)
            steps.settle()
            dve.nop().then_inc(sem("conv_done"), 1)

            for t in range(TT):
                for name, a, n, gain in ((f"cqT{t}", 0, 3, V("cq_g")), (f"ckvT{t}", 3, 2, V("ckv_g"))):
                    dve.wait_ge(*full(name))
                    steps.link(tt(cT[:, a:a + n, t * P:(t + 1) * P], cols(held(name), 0, n, P),
                                  spread(gain, P), ALU.mult))
                    dve.nop().then_inc(emptied(name), 1)
                    dve.nop().then_inc(sem("latentsT_ready"), 1)

            dve.wait_ge(sem("forget_log"), 1)
            steps.link(stt(rows[1], rows[1], 0.0, rows[4], ALU.min, ALU.subtract))
            for d in range(2):
                r = slice(32 * d, 32 * d + AH)
                flow = slice(None, None, -1) if d else slice(None)
                one = ones_row[r]
                steps.link(dve.tensor_tensor_scan(rows[5][r, flow], one, rows[1][r, flow], 0.0,
                                                  ALU.mult, ALU.add))
            steps.link(tt(rows[2], rows[0], rows[5], ALU.subtract))
            for d in range(2):
                r = slice(32 * d, 32 * d + AH)
                flow = slice(None, None, -1) if d else slice(None)
                one = ones_row[r]
                steps.link(dve.tensor_tensor_scan(rows[3][r, flow], one, rows[2][r, flow], 0.0,
                                                  ALU.mult, ALU.max))
            steps.link(tt(rows[4], rows[5], rows[3], ALU.add))
            steps.link(ts(rows[3], rows[3], -1.0, None, ALU.mult))
            dve.nop().then_inc(sem("floor_rows"), 1)

            dve.wait_ge(sem("heads_squared"), 1)
            dve.tensor_reduce(qkss, qk_sq.rearrange("p t h d -> p (t h) d"), AX.X,
                              ALU.add).then_inc(sem("head_sums"), 1)
            dve.wait_ge(sem("head_rstd"), 1)
            steps.link(tt(qk_t.rearrange("p t h d -> p (t h) d"), qk_t.rearrange("p t h d -> p (t h) d"),
                          spread(qkrs, CQK), ALU.mult))
            for t in range(TT):
                for i, g in enumerate(("qn_g", "kn_g")):
                    v = qk_t[:, t, CH * i:CH * (i + 1), :]
                    steps.mark(tt(v, v, repeated(V(g), CH), ALU.mult))
            steps.settle()
            for t in range(TT):
                r1, r2 = qk_t[:, t, :, CN:CN + 16], qk_t[:, t, :, CN + 16:CQK]
                cos, sin = (repeated(C(n, 16 * t, 16 * t + 16), 2 * CH) for n in ("cos", "sin"))
                parts = [cols(qk_sq.rearrange("p t h d -> p (t h d)"), 256 * i, 2 * CH, 16) for i in range(4)]
                for o, (a, b) in zip(parts, ((r1, cos), (r2, sin), (r2, cos), (r1, sin))):
                    steps.mark(tt(o, a, b, ALU.mult))
                steps.settle()
                steps.mark(tt(r1, parts[0], parts[1], ALU.subtract))
                steps.mark(tt(r2, parts[2], parts[3], ALU.add))
                steps.settle()
            dve.nop().then_inc(sem("heads_roped"), 1)

            dve.wait_ge(*full("conv_sum"))
            for j in range(4):
                steps.mark(stt(uc[:, j, :], held("conv_sum")[:, 0:S], -1.0 / BW, uc[:, j, :],
                               ALU.mult, ALU.add))
            steps.settle()
            dve.nop().then_inc(emptied("conv_sum"), 1)
            dve.nop().then_inc(sem("conv_centred"), 1)
            read_modulation(6)
            dve.wait_ge(sem("conv_rstd"), 1)
            steps.link(tt(uc, uc, usq[:, 0:1, :].to_broadcast([P, 4, S]), ALU.mult))
            for j in range(4):
                steps.mark(ts(uc[:, j, :], uc[:, j, :], V("ln_g", j, j + 1), V("ln_b", j, j + 1),
                              ALU.mult, ALU.add))
            steps.settle()
            dve.nop().then_inc(sem("conv_affine"), 1)

            for h in range(CH + 1):
                if h < CH:
                    dve.wait_ge(*full(f"sc{h}"))
                    steps.link(dve.tensor_reduce(smax[:, 2 * h:2 * h + 2], cols(held(f"sc{h}"), 0, TT, S),
                                                 AX.X, ALU.max))
                    ts(smax[:, 2 * h:2 * h + 2], smax[:, 2 * h:2 * h + 2], -CQK ** -0.5, None,
                       ALU.mult).then_inc(sem("score_max"), 1)
                if h:
                    g = h - 1
                    dve.wait_ge(sem("probs_summed"), g + 1)
                    steps.link(dve.reciprocal(ssum[:, 2 * g:2 * g + 2], ssum[:, 2 * g:2 * g + 2]))
                    steps.link(tt(prob[g % 2], prob[g % 2], spread(ssum[:, 2 * g:2 * g + 2], S), ALU.mult))
                    dve.nop().then_inc(sem("probs_ready"), 1)
                if h < CH and h % 2:
                    read_modulation(1)

            dve.wait_ge(*full("gate_cols"))
            gc = held("gate_cols")[:, 0:256].rearrange("p (i t r) -> p i t r", i=2, t=TT)
            for i, o in enumerate((acol, fcol)):
                for d in range(2):
                    steps.mark(dve.tensor_copy(
                        o.rearrange("p (t d h) -> p t d h", t=TT, d=2)[:, :, d, :],
                        gc[:, i, :, 32 * d:32 * d + AH]))
            steps.settle()
            dve.nop().then_inc(emptied("gate_cols"), 1)
            areas = ((0, 0, 0, 0, 256), (0, 1, 128, 256, 384), (1, 0, 0, 384, 512), (1, 1, 0, 512, 768))

            def combine(h):
                for d in range(2):
                    dve.wait_ge(*full(f"mem{h}{d}"))
                    m = cols(held(f"mem{h}{d}"), 0, TT, AD + 1)
                    dn = den[:, 0:TT].unsqueeze(2)
                    steps.link(dve.tensor_copy(dn, m[:, :, AD:AD + 1]))
                    steps.link(stt(den[:, 0:TT], den[:, 0:TT], -1.0, den[:, 0:TT], ALU.mult, ALU.max))
                    floor = fcol.rearrange("p (t d h) -> p t d h", t=TT, d=2)[:, :, d, h:h + 1]
                    steps.link(tt(dn, dn, floor, ALU.max))
                    steps.link(dve.reciprocal(den[:, 0:TT], den[:, 0:TT]))
                    for t in range(TT):
                        if d == 0:
                            ins = ts(h_t[:, t, h, :], m[:, t, 0:AD], den[:, t:t + 1], None, ALU.mult)
                        else:
                            ins = stt(h_t[:, t, h, :], m[:, t, 0:AD], den[:, t:t + 1], h_t[:, t, h, :],
                                      ALU.mult, ALU.add)
                        steps.mark(ins)
                    steps.settle()
                    dve.nop().then_inc(emptied(f"mem{h}{d}"), 1)

            for h in range(AH + 1):
                if h < AH:
                    dve.wait_ge(*full(f"negA{h}"))
                    if h >= 2:
                        dve.wait_ge(*full(f"mem{h - 2}1"))
                    for d, kt, q, a, b in areas:
                        steps.mark(ts(warg[h % 2][:, a:b], held(f"negA{h}")[:, d * S + q:d * S + q + b - a],
                                      acol[:, (2 * kt + d) * AH + h:(2 * kt + d) * AH + h + 1], 0.0,
                                      ALU.add, ALU.min))
                    steps.settle()
                    dve.nop().then_inc(emptied(f"negA{h}"), 1)
                    dve.nop().then_inc(sem("weight_args"), 1)
                    dve.wait_ge(sem("weight_exps"), h + 1)
                    steps.link(tt(warg[h % 2], warg[h % 2], C("mmask"), ALU.mult))
                    dve.wait_ge(*full(f"kq{h}"))
                    for d, kt, q, a, b in areas:
                        steps.mark(tt(warg[h % 2][:, a:b], warg[h % 2][:, a:b],
                                      held(f"kq{h}")[:, kt * S + q:kt * S + q + b - a], ALU.mult))
                    steps.settle()
                    dve.nop().then_inc(emptied(f"kq{h}"), 1)
                    dve.nop().then_inc(sem("weights_ready"), 1)
                if h:
                    combine(h - 1)
                    read_modulation(1)
            hv = h_t.rearrange("p t h d -> p (t h) d")
            h_sq = cols(warg[0], 0, 6, AD), cols(warg[1], 0, 2, AD)
            steps.mark(tt(h_sq[0], hv[:, 0:6, :], hv[:, 0:6, :], ALU.mult))
            steps.mark(tt(h_sq[1], hv[:, 6:8, :], hv[:, 6:8, :], ALU.mult))
            steps.settle()
            steps.mark(dve.tensor_reduce(hss[:, 0:6], h_sq[0], AX.X, ALU.add))
            steps.mark(dve.tensor_reduce(hss[:, 6:8], h_sq[1], AX.X, ALU.add))
            steps.settle()
            dve.nop().then_inc(sem("memory_sums"), 1)
            dve.wait_ge(sem("memory_rstd"), 1)
            steps.link(tt(hv, hv, spread(hrs, AD), ALU.mult))
            for i in range(2):
                dve.wait_ge(*was_emptied(f"vo{i + 2}"))
            steps.link(tt(h_t.rearrange("p t h d -> p (t h d)"), h_t.rearrange("p t h d -> p (t h d)"),
                          so_t.rearrange("p t d -> p (t d)"), ALU.mult))
            dve.nop().then_inc(sem("memory_normed"), 1)
            read_modulation(2)
            dve.wait_ge(sem("conv_sig"), 1)
            tt(uc, uc, usq, ALU.mult).then_inc(sem("conv_out"), 1)
            for t in range(TT):
                dve.wait_ge(*full(f"memT{t}"))
                steps.link(tt(hT[:, :, t * P:(t + 1) * P], cols(held(f"memT{t}"), 0, 4, P),
                              spread(V("a_g"), P), ALU.mult))
                dve.nop().then_inc(emptied(f"memT{t}"), 1)
                dve.nop().then_inc(sem("memT_ready"), 1)
            dve.wait_ge(sem("gx_high"), 1)
            tt(gx_low, xnT, gx_high, ALU.subtract).then_inc(sem("gx_low"), 1)
            for j in range(4):
                for i in range(3):
                    dve.wait_ge(*full(f"y{j}{i}_"))
                    dve.wait_ge(sem("branch_gate"), 3 * j + i + 1)
                    mj = merged[:, 2 * j:2 * j + 2, :].rearrange("p b s -> p (b s)")
                    steps.link(tt(mj if i == 0 else gtmp[:, i - 1, :], gsig[:, i, :], held(f"y{j}{i}_"),
                                  ALU.mult))
                    dve.nop().then_inc(emptied(f"y{j}{i}_"), 1)
                    if i:
                        steps.link(tt(mj, mj, gtmp[:, i - 1, :], ALU.add))
                    if j < 3:
                        n = order.index(f"g{j + 1}{i}")
                        dve.wait_ge(sem("gate_high"), 3 * j + i + 1)
                        tt(ring_r[n % SLOTS].ap(), ring[n % SLOTS].ap(), gate_high[i],
                           ALU.subtract).then_inc(sem("gate_rest"), 1)
                dve.nop().then_inc(sem("merged_ready"), 1)
            for t in range(TT):
                for n in range(2):
                    dve.wait_ge(*full(f"wo{t}{n}"))
                    v = x_t[:, t, n * 512:(n + 1) * 512]
                    steps.link(tt(v, v, held(f"wo{t}{n}"), ALU.add))
                    dve.nop().then_inc(emptied(f"wo{t}{n}"), 1)
                dve.nop().then_inc(sem("x_updated"), 1)

            scale_x(2)
            read_turned("xU", V("ffn_g"))
            dve.wait_ge(*full("router"))
            lg = held("router")[:, 0:TT * E1].rearrange("p (t e) -> p t e", t=TT)
            steps.link(dve.tensor_reduce(mx1, lg, AX.X, ALU.max))
            steps.link(tt(aff, lg, spread(mx1, E1), ALU.subtract))
            dve.nop().then_inc(emptied("router"), 1)
            dve.nop().then_inc(sem("logits_shifted"), 1)
            dve.wait_ge(sem("affinity_exp"), 1)
            steps.link(dve.tensor_reduce(sm1, aff, AX.X, ALU.add))
            steps.link(dve.reciprocal(sm1, sm1))
            tt(aff, aff, spread(sm1, E1), ALU.mult).then_inc(sem("affinity_ready"), 1)
            dve.wait_ge(sem("xn_high_ready"), 1)
            tt(xn_low, xn_t, xn_high, ALU.subtract).then_inc(sem("xn_low_ready"), 1)
            dve.wait_ge(*full("affT"))
            steps.link(dve.tensor_copy(affw, held("affT")[0:E1, 0:S]))
            dve.nop().then_inc(emptied("affT"), 1)
            for _ in range(CAP // 8):
                steps.link(dve.max(m8, affw))
                steps.link(dve.match_replace(affw, m8, affw, -1.0))
            steps.link(ts(affw, affw, 0.0, None, ALU.is_lt))
            steps.link(dve.tensor_tensor_scan(slotrow, ones_row[0:E1], affw, 0.0, ALU.mult, ALU.add))
            tt(slotrow, slotrow, affw, ALU.mult).then_inc(sem("slot_rows"), 1)
            dve.wait_ge(*full("slotT"))
            steps.link(dve.tensor_copy(slot_t.rearrange("p t e -> p (t e)"), held("slotT")[:, 0:TT * E1]))
            dve.nop().then_inc(emptied("slotT"), 1)
            for t in range(TT):
                oh = onehot[:, t, :].rearrange("p (e c) -> p e c", e=E1)
                steps.mark(tt(oh, repeated(C("iota"), E1), spread(slot_t[:, t, :], CAP), ALU.is_equal))
            steps.settle()
            dve.nop().then_inc(sem("onehot_ready"), 1)
            for t in range(TT):
                oh, wt = (v[:, t, :].rearrange("p (e c) -> p e c", e=E1) for v in (onehot, weighted))
                steps.mark(tt(wt, oh, spread(aff[:, t, :], CAP), ALU.mult))
            steps.settle()
            dve.nop().then_inc(sem("weighted_ready"), 1)
            for k in range(0, KD, 2):
                dve.wait_ge(*full(f"xg{k}"))
                steps.link(ts(xg[:, k, :], held(f"xg{k}"), V("ffn_g", k, k + 1), None, ALU.mult))
                dve.nop().then_inc(emptied(f"xg{k}"), 1)
                dve.nop().then_inc(sem("xg_read"), 1)
            first1 = order.index("e0gu0")

            dve.nop().then_inc(sem("gated"), 1)
            dve.nop().then_inc(sem("scatter_read"), 1)

            def hidden_of(it, j):
                dve.wait_ge(sem("gate_silu"), it * 4 + (j + 1))
                dve.tensor_tensor(hid1[j % 2], gate1[j % 2], bank[2 + j % 2][0:3 * CAP, :],
                                  ALU.mult).then_inc(sem("gated"), 1)

            def hiddenT_of(it, j):
                dve.wait_ge(sem("hidden_turned"), it * 4 + (j + 1))
                dve.wait_ge(piece_used, it * 72 + (first1 + 12 + 18 * (j - 1)))
                dve.tensor_copy(hid1T[j % 2], cols(bank[7], 0, 4, 3, CAP)).then_inc(sem("hiddenT_ready"), 1)

            def add_back(it):
                for i in range(4):
                    t, half = divmod(i, 2)
                    dve.wait_ge(sem("scattered"), it * 4 + (i + 2))
                    v = x_t[:, t, half * 512:(half + 1) * 512]
                    tt(v, v, bank[6 + i % 2], ALU.add).then_inc(sem("scatter_read"), 1)

            hidden_of(0, 0)
            if e1_groups > 1:
                with dve.Fori(0, e1_groups - 1) as it:
                    for j in range(4):
                        hiddenT_of(it, j)
                        hidden_of(it, j + 1)
                    add_back(it)
            for j in range(4):
                hiddenT_of(e1_groups - 1, j)
                if j < 3:
                    hidden_of(e1_groups - 1, j + 1)
            add_back(e1_groups - 1)
            dve.wait_ge(sem("scatter_read"), 4 * e1_groups + 1)

            def read_modulated(name, weight, shift, scale):
                steps.link(stt(scol1, scale, 1.0, weight, ALU.add, ALU.mult))
                dve.nop().then_inc(sem("scales_ready"), 1)
                for t in range(TT):
                    out_ = xnT[:, 0:4, t * P:(t + 1) * P]
                    dve.wait_ge(*full(f"{name}{t}0"))
                    steps.link(tt(out_, cols(held(f"{name}{t}0"), 0, 4, P), spread(scol1[:, 0:4], P),
                                  ALU.mult))
                    dve.nop().then_inc(emptied(f"{name}{t}0"), 1)
                    tt(out_, out_, spread(shift[:, 0:4], P), ALU.add).then_inc(sem("xnT_ready"), 1)
                dve.wait_ge(sem("xnT_ready"), 12 if name == "xV" else 16)

            def wide(v):
                return v.rearrange("p a b -> p (a b)")

            tt(lb, V("lb0"), V("lb1"), ALU.subtract).then_inc(sem("lb_diff"), 1)
            steps.mark(dve.memset(pad2[:, :, 0:CONV2 - 1], 0.0))
            scale_x(3)
            steps.link(tt(modc[:, 0:32], modc[:, 0:32], V("b_ada", 0, 32), ALU.add))
            read_modulated("xV", V("n1w"), modc[:, 0:8], modc[:, 8:16])
            read_modulation(2)
            steps.mark(dve.memset(wide(hQ), 0.0))
            steps.mark(dve.memset(wide(hK), 0.0))
            dve.wait_ge(sem("lb_ready"), 1)
            ts(oml, lb, -1.0, 1.0, ALU.mult, ALU.add).then_inc(sem("oml_ready"), 1)
            dve.wait_ge(*was_emptied("rows2"))
            stt(grow[2], grow[1], -1.0, grow[1], ALU.mult, ALU.max).then_inc(sem("decay_abs"), 1)
            dve.wait_ge(sem("oml_ready"), 1)
            dve.wait_ge(sem("keep_sig"), 1)
            for h in range(HH):
                v = hk[:, 2 * h:2 * h + 2, :]
                steps.mark(ts(v, v, oml[:, h:h + 1], None, ALU.mult))
            steps.settle()
            dve.wait_ge(sem("hq_ready"), 1)
            dve.nop().then_inc(sem("hk_ready"), 1)
            dve.wait_ge(sem("logf_ready"), 1)
            for i in range(HH * TT):
                steps.mark(dve.tensor_tensor_scan(hb[:, i, :], ones_row[:, 0:P], hb[:, i, :], 0.0,
                                                  ALU.mult, ALU.add))
            dve.wait_ge(sem("decay_log"), 1)
            dve.wait_ge(sem("decay_rate"), 1)
            steps.link(stt(grow[1], grow[1], 0.0, grow[2], ALU.max, ALU.add))
            steps.link(ts(grow[1], grow[1], nexpa, -1.0, ALU.mult, ALU.mult))
            for t in range(TT):
                c = slice(t * P, (t + 1) * P)
                steps.mark(dve.tensor_tensor_scan(grow[2][:, c], ones_row[0:GH, 0:P], grow[1][:, c], 0.0,
                                                  ALU.mult, ALU.add))
            steps.settle()
            dve.nop().then_inc(sem("g_rows"), 1)

            def level_views(n):
                if n == 1:
                    half = lambda v, i: v.rearrange("p (h t) s -> p h t s", t=TT)[:, :, i, :]
                    return half, P
                hs = 1 << (n - 2)
                return (lambda v, i: wide(v).rearrange("p (b two s) -> p b two s", two=2, s=hs)[:, :, i, :]), hs

            def level_args(n):
                half, hs = level_views(n)
                b0, b1 = half(hb, 0), half(hb, 1)
                mid = b0[:, :, hs - 1:hs].to_broadcast(list(b0.shape))
                steps.mark(tt(half(hE, 0), mid, b0, ALU.subtract))
                if n == 1:
                    steps.mark(dve.tensor_copy(half(hE, 1), b1))
                else:
                    steps.mark(tt(half(hE, 1), b1, mid, ALU.subtract))
                steps.settle()
                dve.nop().then_inc(sem("level_args"), 1)

            def add_level(n):
                for i in range(2):
                    dve.wait_ge(*full(f"hl{n}{i}"))
                    at = AT[:, 4 * i:4 * i + 4, :]
                    mask = ident if n == 0 else C("levels", (n - 2) * P, (n - 1) * P)
                    o = at if n == 0 else hsig[:, 4:8, :]
                    steps.link(tt(o, cols(held(f"hl{n}{i}"), 0, 4, P), repeated(mask, 4), ALU.mult))
                    dve.nop().then_inc(emptied(f"hl{n}{i}"), 1)
                    if n:
                        steps.link(tt(at, at, o, ALU.add))

            def convolve(pair):
                dve.wait_ge(*was_emptied(f"S{pair + 5}"))
                marks = [0] * 2
                for k in range(CONV2):
                    for i, j in enumerate((2 * pair, 2 * pair + 1)):
                        tap = V("conv2_w", CONV2 * j + k, CONV2 * j + k + 1)
                        if k == 0:
                            ins = ts(qkv[:, j, :], pad2[:, j, 0:S], tap, None, ALU.mult)
                        else:
                            steps.settle(marks[i])
                            ins = stt(qkv[:, j, :], pad2[:, j, k:k + S], tap, qkv[:, j, :], ALU.mult, ALU.add)
                        marks[i] = steps.mark(ins)

            level_args(1)
            for n in range(1, 9):
                half, hs = level_views(n)
                dve.wait_ge(sem("level_exps"), n)
                if n >= 2:
                    dve.wait_ge(*full("hx" if n == 2 else f"hl{n - 1}1"))
                steps.mark(tt(half(hK, 0), half(hk, 0), half(hE, 0), ALU.mult))
                steps.mark(tt(half(hQ, 1), half(hq, 1), half(hE, 1), ALU.mult))
                steps.settle()
                dve.nop().then_inc(sem("level_ready"), 1)
                if n < 8:
                    level_args(n + 1)
                    if n >= 2:
                        convolve(n - 2)
                if n == 1:
                    add_level(0)
                elif n > 2:
                    add_level(n - 1)
            add_level(8)
            steps.settle()
            dve.nop().then_inc(sem("AT_ready"), 1)
            dve.nop().then_inc(sem("conv2_done"), 1)
            dve.wait_ge(*full("gcols"))
            steps.link(dve.tensor_copy(small[:, 48:64], held("gcols")[:, 0:16]))
            dve.nop().then_inc(emptied("gcols"), 1)
            dve.wait_ge(sem("bc_read"), 1)
            for h in range(GH):
                steps.link(dve.tensor_copy(glast[:, h:h + 1], dec[:, 2 * h, P - 1:P]))
                for t in range(TT):
                    v = dec[:, 2 * h + t, :]
                    steps.mark(ts(v, v, gcol[:, 4 * t + h:4 * t + h + 1], 0.0, ALU.subtract, ALU.min))
            steps.settle()
            dve.nop().then_inc(sem("dec_args"), 1)
            steps.mark(dve.tensor_copy(ecol, gcol[:, 4:8]))
            steps.mark(tt(tcol, glast, gcol[:, 0:4], ALU.subtract))
            steps.settle()
            dve.nop().then_inc(sem("col_args"), 1)
            dve.wait_ge(sem("dec_exps"), 1)
            steps.link(tt(dec, dec, repeated(tri, 8), ALU.mult))
            dve.wait_ge(sem("unit_ready"), 1)
            q, k = wide(qkv)[:, 0:4 * S], wide(qkv)[:, 4 * S:8 * S]
            r = wide(qk_ss)
            steps.mark(stt(q, q, P ** -0.5, r[:, 0:4 * S], ALU.mult, ALU.mult))
            steps.mark(tt(k, k, r[:, 4 * S:8 * S], ALU.mult))
            steps.settle()
            dve.nop().then_inc(sem("qk_unit"), 1)
            read_modulation(3)
            steps.link(tt(LT, attnT, dec, ALU.mult))
            for h in range(GH):
                dve.wait_ge(*full(f"kk{h}"))
                v = slice(2 * h, 2 * h + 2)
                steps.mark(tt(LT[:, v, :], LT[:, v, :], cols(held(f"kk{h}"), 0, 2, P), ALU.mult))
                steps.mark(tt(attnT[:, v, :], dec[:, v, :], cols(held(f"kk{h}"), S, 2, P), ALU.mult))
                steps.settle()
                dve.nop().then_inc(emptied(f"kk{h}"), 1)

            for h in range(GH):
                dve.wait_ge(*was_emptied(f"bc{h}"))
            for i in range(2):
                h4 = slice(4 * i, 4 * i + 4)
                steps.mark(tt(Lm[:, h4, :], LT[:, h4, :], repeated(C("levels", 0, P), 4), ALU.mult))
            for i in range(2):
                h4 = slice(4 * i, 4 * i + 4)
                steps.settle()
                tt(Ui[:, h4, :], repeated(ident, 4), Lm[:, h4, :], ALU.subtract).then_inc(sem("U_ready"), 1)
            dve.wait_ge(sem("U_ready"), 2)
            for n in range(1, LEVELS):
                if n == LEVELS - 1:
                    dve.wait_ge(sem("kv_turned"), 1)
                    dve.wait_ge(sem("col_exps"), 1)
                    for i in range(2):
                        dve.wait_ge(*full(f"X{n}{i}"))
                    dve.wait_ge(sem("Lm_ready"), 2 * n)
                    steps.mark(tt(vb, v_t, spread(bcol, P), ALU.mult))
                    steps.mark(tt(ecol, ecol, bcol[:, 4:8], ALU.mult))
                    steps.mark(tt(ktail, k_t[:, 0:4, :], spread(tcol, P), ALU.mult))
                    steps.mark(tt(qd, qkv[:, 0:4, P:2 * P], egb, ALU.mult))
                if n < LEVELS - 1:
                    for i in range(2):
                        h4 = slice(4 * i, 4 * i + 4)
                        dve.wait_ge(*full(f"TX{n}{i}"))
                        tt(Ti[:, h4, :], Ti[:, h4, :], cols(held(f"TX{n}{i}"), 0, 4, P),
                           ALU.subtract).then_inc(emptied(f"TX{n}{i}"), 1)
                for i in range(2):
                    h4 = slice(4 * i, 4 * i + 4)
                    dve.wait_ge(*full(f"XU{n}{i}"))
                    steps.link(tt(Ui[:, h4, :], Ui[:, h4, :], cols(held(f"XU{n}{i}"), 0, 4, P),
                                  ALU.subtract))
                    dve.nop().then_inc(emptied(f"XU{n}{i}"), 1)
                    dve.nop().then_inc(sem("U_ready"), 1)
            steps.settle()
            steps.link(tt(kbe, k_t[:, 4:8, :], spread(ecol, P), ALU.mult))
            dve.nop().then_inc(sem("vb_ready"), 1)
            read_modulation(1)
            dve.wait_ge(*full("wS"))
            steps.link(tt(vnew, uu[:, 4:8, :], cols(held("wS"), 0, 4, P), ALU.subtract))
            dve.nop().then_inc(emptied("wS"), 1)
            dve.nop().then_inc(sem("vnew_ready"), 1)
            dve.wait_ge(sem("o_rstd"), 1)
            for t in range(TT):
                a = o_t[:, t, 0:512].rearrange("p (h d) -> p h d", h=GH)
                steps.mark(tt(a, a, spread(ors[:, 4 * t:4 * t + 4], P), ALU.mult))
                steps.mark(ts(o_t[:, t, 512:1024], o_t[:, t, 512:1024], ors[:, 8 + t:9 + t], None, ALU.mult))
            steps.settle()
            for i in range(4):
                dve.wait_ge(*was_emptied(f"U{i + 2}"))
            steps.link(tt(wide(o_t), wide(o_t), wide(z_gate), ALU.mult))
            dve.nop().then_inc(sem("o_ready"), 1)
            read_modulation(2)
            tt(modc[:, 32:48], modc[:, 32:48], V("b_ada", 32, 48), ALU.add).then_inc(sem("mod_ready"), 1)
            for t in range(TT):
                for half in range(2):
                    dve.wait_ge(*full(f"oo{t}{half}"))
                    steps.link(tt(oT2[:, 4 * half:4 * half + 4, t * P:(t + 1) * P],
                                  cols(held(f"oo{t}{half}"), 0, 4, P),
                                  spread(V("og", 4 * half, 4 * half + 4), P), ALU.mult))
                    dve.nop().then_inc(emptied(f"oo{t}{half}"), 1)
                    dve.nop().then_inc(sem("oT2_ready"), 1)
            first2 = order.index("r64a")

            def rest_of(p, it=0):
                n = first2 + p
                dve.wait_ge(sem("high_ready"), it * SLOTS + (p + 1))
                tt(ring_r[n % SLOTS].ap(), ring[n % SLOTS].ap(), w_high[p % HIGHS],
                   ALU.subtract).then_inc(sem("rest_ready"), 1)

            for p in range(AHEAD + 1):
                rest_of(p)
            for g in range(4):
                dve.wait_ge(*was_emptied(f"gate_rows{g}"))
            for t in range(TT):
                for n in range(2):
                    dve.wait_ge(*full(f"wp{t}{n}"))
                    v, tmp = x_t[:, t, n * 512:(n + 1) * 512], ytmp[n]
                    steps.link(tt(tmp, held(f"wp{t}{n}"), gmod[:, n * 512:(n + 1) * 512], ALU.mult))
                    dve.nop().then_inc(emptied(f"wp{t}{n}"), 1)
                    steps.link(tt(v, v, tmp, ALU.add))
                dve.nop().then_inc(sem("x_updated2"), 1)

            scale_x(4)
            read_modulated("xW", V("n2w"), modc[:, 16:24], modc[:, 24:32])
            dve.wait_ge(sem("x_high_ready"), 1)
            tt(x_low, xnT, x_high, ALU.subtract).then_inc(sem("x_low_ready"), 1)

            def chain(ins, n):
                ins.then_inc(sem("hidden_steps"), 1)
                dve.wait_ge(sem("hidden_steps"), n)

            def hidden_of2(e, i, b, used=None):
                n = b * 2 if i == 0 else e * 6 + (b * 3 - 2)
                dve.wait_ge(sem("silu2"), e * 2 + (b + 1))
                if b == 0 and used is not None:
                    dve.wait_ge(piece_used, used)
                chain(tt(part2[b], silu2[b], bank[b][:, S:2 * S], ALU.mult), n + 1)
                if i:
                    dve.wait_ge(sem("gate_spread"), e + 1)
                    n = n + 1
                    chain(tt(part2[b], part2[b], bank[2 + i % 2][:, 0:S], ALU.mult), n + 1)
                high, low = hid2[i % 2]
                chain(dve.tensor_copy(high[b], part2[b]), n + 2)
                tt(low[b], part2[b], high[b], ALU.subtract).then_inc(sem("hidden2"), 1)

            hidden_of2(0, 0, 0)
            dve.wait_ge(sem("scores_ready"), 1)
            steps.link(tt(sel, score, repeated(V("rbias"), TT), ALU.add))
            for i in range(TT * NG2):
                steps.mark(dve.max(gmax[:, i, :], wide(sel)[:, 8 * i:8 * i + 8]))
            steps.settle()
            gs = wide(gsum).unsqueeze(2)
            steps.link(tt(gs, gmax[:, :, 0:1], gmax[:, :, 1:2], ALU.add))
            other = gsum.unsqueeze(2).to_broadcast([P, TT, NG2, NG2])
            own = gsum.unsqueeze(3).to_broadcast([P, TT, NG2, NG2])
            steps.mark(tt(cmpa, other, own, ALU.is_gt))
            steps.link(tt(cmpb, other, own, ALU.is_equal))
            before = C("gbefore").rearrange("p (a b) -> p a b", a=NG2)
            for t in range(TT):
                steps.mark(tt(cmpb[:, t], cmpb[:, t], before, ALU.mult))
            steps.settle()
            steps.link(tt(cmpa, cmpa, cmpb, ALU.add))
            steps.link(dve.tensor_reduce(rank, cmpa, AX.X, ALU.add))
            steps.link(ts(rank, rank, TOPG - 0.5, None, ALU.is_lt))
            in_group = wide(rank).unsqueeze(2).to_broadcast([P, TT * NG2, 8])
            by_group = lambda v: wide(v).rearrange("p (g e) -> p g e", e=8)
            steps.link(tt(by_group(msel), by_group(sel), in_group, ALU.mult))
            steps.link(ts(rank, rank, -1.0, 1e30, ALU.add, ALU.mult))
            steps.link(tt(by_group(msel), by_group(msel), in_group, ALU.add))
            for t in range(TT):
                steps.link(dve.max(top8[:, t, :], msel[:, t, :]))
                steps.link(dve.match_replace(chosen[:, t, :], top8[:, t, :], msel[:, t, :], -3e30))
            steps.link(ts(wide(chosen), wide(chosen), -2e30, None, ALU.is_lt))
            steps.link(tt(chosen, chosen, score, ALU.mult))
            steps.link(dve.tensor_reduce(wsum, chosen, AX.X, ALU.add))
            steps.link(dve.reciprocal(wsum, wsum))
            for t in range(TT):
                steps.mark(ts(chosen[:, t, :], chosen[:, t, :], wsum[:, t:t + 1], ROUTE_SCALE, ALU.mult,
                              ALU.mult))
            steps.settle()
            dve.nop().then_inc(sem("gates2_ready"), 1)
            rest_of(1 + AHEAD)
            hidden_of2(0, 0, 1)
            dve.wait_ge(sem("gates_turned"), 1)
            steps.link(dve.tensor_copy(gT[:, 0:S], bank[7][0:E2, 0:S]))
            tt(gT[:, S:2 * S], bank[7][0:E2, 0:S], gT[:, 0:S], ALU.subtract).then_inc(sem("gT_ready"), 1)
            rest_of(2 + AHEAD)
            hidden_of2(1, 1, 0)
            rest_of(3 + AHEAD)
            rest_of(4 + AHEAD)
            hidden_of2(1, 1, 1)

            def hidden_group(it, n_pieces):
                for q in range(n_pieces):
                    if q + AHEAD < n_pieces or n_pieces == SLOTS:
                        rest_of(5 + q + AHEAD, it)
                    if q % 3 != 1 and (q < 9 or n_pieces == SLOTS):
                        i = 2 + q // 3
                        hidden_of2(it * 4 + i, i, q % 3 // 2, it * SLOTS + (first2 + 5 + 3 * (i - 2) - 1))

            if e2_groups > 1:
                with dve.Fori(0, e2_groups - 1) as it:
                    hidden_group(it, SLOTS)
            hidden_group(e2_groups - 1, SLOTS - 2)
            dve.wait_ge(piece_used, first2 + 4 + 12 * e2_groups - 1)
            for t in range(TT):
                for n in range(2):
                    v, y = x_t[:, t, n * 512:(n + 1) * 512], ytmp[n]
                    steps.link(tt(y, bank[4 + 2 * t + n], gmod[:, D + n * 512:D + (n + 1) * 512], ALU.mult))
                    steps.link(tt(v, v, y, ALU.add))
                dve.nop().then_inc(sem("x_updated3"), 1)
            dve.wait_ge(sem("final_w_landed"), 16)
            for t in range(TT):
                dve.wait_ge(sem("rstd_ready"), 4 + t + 1)
                stt(xn_t[:, t, :], x_t[:, t, :], rstd[:, t:t + 1], finw, ALU.mult,
                    ALU.mult).then_inc(sem("out_ready"), 1)

        @block.gpsimd
        def _(pool):
            pool.wait_ge(sem("xg_read"), KD)
            first1 = order.index("e0gu0")

            def load_tokens(it, j):
                pool.wait_ge(piece_used, it * 72 + max(first1 + 6 + 18 * (j - 2), first1 + 12 if j == 2 else 1))
                nc.gpsimd.tensor_copy(xe[j % 2], xg[:, :, bass.ds((it * 4 + j) * CAP, CAP)]
                                      ).then_inc(sem("tokens_loaded"), 1)

            def load_back(it):
                pool.wait_ge(sem("scattered"), it * 4 + 1)
                nc.gpsimd.tensor_copy(back_now.unsqueeze(1), backT[:, bass.ds(it, 1), :]
                                      ).then_inc(sem("back_loaded"), 1)

            load_tokens(0, 0)
            pool.wait_ge(sem("back_ready"), 2)
            if e1_groups > 1:
                with pool.Fori(0, e1_groups - 1) as it:
                    for j in range(1, 5):
                        load_tokens(it, j)
                        if j == 1:
                            load_back(it)
            for j in range(1, 4):
                load_tokens(e1_groups - 1, j)
                if j == 1:
                    load_back(e1_groups - 1)
            for n in range(1, LEVELS):
                for i in range(2):
                    if n == 1:
                        pool.wait_ge(sem("U_ready"), 2)
                    else:
                        pool.wait_ge(*full(f"X{n - 1}{i}"))
                    h4 = slice(4 * i, 4 * i + 4)
                    nc.gpsimd.tensor_tensor(Lm[:, h4, :], LT[:, h4, :],
                                            repeated(C("levels", n * P, (n + 1) * P), 4),
                                            ALU.mult).then_inc(sem("Lm_ready"), 1)
            pool.wait_ge(sem("gT_ready"), 1)

            def gate_row(e, i):
                if i is not None:
                    pool.wait_ge(sem("gate_spread"), e - 1)
                own = ident[0:E2, bass.ds(e - 1, 1)].to_broadcast([E2, 2 * S])
                nc.gpsimd.tensor_tensor(grow2[(i or 1) % 2], gT, own, ALU.mult).then_inc(sem("gate_row"), 1)

            gate_row(1, None)
            if e2_groups > 1:
                with pool.Fori(0, e2_groups - 1) as it:
                    for i in range(2, 6):
                        gate_row(it * 4 + i, i)
            for i in range(2, 5):
                gate_row((e2_groups - 1) * 4 + i, i)

        @block.sync
        def _(sp):
            sp.dma_start(x_t, x_in.rearrange("o (t p) d -> p (o t) d", p=P)).then_inc(inputs_landed, 16)
            sp.dma_start(cst, cst_in).then_inc(inputs_landed, 16)
            sp.dma_start(vec, vec_in).then_inc(inputs_landed, 16)
            n_pieces = len(order)
            for n in range(min(SLOTS, n_pieces)):
                sp.dma_start(ring[n % SLOTS].ap(), stream_in[n]).then_inc(landed[n % SLOTS], 16)
            full_rounds = n_pieces // SLOTS
            if full_rounds > 1:
                with sp.Fori(1, full_rounds) as i:
                    for s in range(SLOTS):
                        sp.wait_ge(piece_used, i * SLOTS + (s + 1 - SLOTS))
                        sp.dma_start(ring[s].ap(), stream_in[i * SLOTS + s]).then_inc(landed[s], 16)
            for n in range(max(full_rounds, 1) * SLOTS, n_pieces):
                sp.wait_ge(piece_used, n + 1 - SLOTS)
                sp.dma_start(ring[n % SLOTS].ap(), stream_in[n]).then_inc(landed[n % SLOTS], 16)
            for t in range(TT):
                sp.wait_ge(sem("out_ready"), t + 1)
                sp.dma_start(out[0, t * P:(t + 1) * P], xn_t[:, t, :]).then_inc(sem("stored"), 16)
            sp.wait_ge(sem("stored"), 16 * TT)


def k_major(w):
    return w.reshape(w.shape[0] // P, P, w.shape[1]).transpose(1, 0, 2)


def layout(a):
    f = np.float32
    z = {}
    at = 0
    for name, n in (("q", 512), ("k", 512), ("v", 512), ("o", 512), ("g", 16), ("glu", 1024),
                    ("cq", CQR), ("ckv", CKR), ("kr", CR), ("gts", 3 * D)):
        z[name] = a["w_in"][0][:, at:at + n]
        at += n
    pieces = {}

    def put_k(name, w, width=S):
        full_w = np.zeros((w.shape[0], width), f)
        full_w[:, :w.shape[1]] = w
        pieces[name] = k_major(full_w).reshape(P, -1)

    gate = np.zeros((D, S), f)
    for at, kind in ((0, 0), (32, 2), (64, 1), (96, 3)):
        gate[:, at:at + AH] = z["g"][:, AH * kind:AH * (kind + 1)]
    put_k("F0", gate)
    for j in range(4):
        c = slice(j * P, (j + 1) * P)
        c2 = slice(BW + j * P, BW + (j + 1) * P)
        put_k(f"F{j + 1}", np.concatenate([z["glu"][:, c], z["glu"][:, c2]], 1))
        put_k(f"F{j + 5}", np.concatenate([z["q"][:, c], z["k"][:, c]], 1))
    lat = np.concatenate([z["cq"], z["ckv"], z["kr"]], 1)
    vo = np.concatenate([z["v"], z["o"]], 1)
    for i in range(3):
        put_k(f"lat{i}", lat[:, S * i:S * (i + 1)])
    for i in range(4):
        put_k(f"vo{i}", vo[:, S * i:S * (i + 1)])
    for half in range(2):
        pieces[f"uq{half}"] = k_major(a["w_uq"][0][:, 384 * half:384 * (half + 1)]).reshape(P, -1)
    pieces["ukv"] = k_major(a["w_ukv"][0]).reshape(P, -1)
    for j in range(4):
        ys = []
        for i in range(3):
            put_k(f"g{j}{i}", z["gts"][:, D * i + S * j:D * i + S * (j + 1)])
            w = (a["w_a_out"], a["w_b_out"], a["w_c_out"])[i][0]
            ys.append(k_major(w[:, S * j:S * (j + 1)]).reshape(P, -1))
        pieces[f"y{j}0"] = np.concatenate(ys[0:2], 1)
        pieces[f"y{j}2"] = ys[2]
    for q in range(4):
        pieces[f"wo{q}"] = k_major(a["w_out"][0][S * q:S * (q + 1)]).reshape(P, -1)
        pieces[f"wp{q}"] = k_major(a["w_out_2"][0][S * q:S * (q + 1)]).reshape(P, -1)
    ada = a["w_ada_2"][0]
    for i, kind in enumerate((0, 1, 3, 4, 2, 5)):
        for q in range(4):
            put_k(f"ada{4 * i + q}", ada[:, D * kind + S * q:D * kind + S * (q + 1)])
    z2, at = {}, 0
    for name, n in (("q", 512), ("k", 512), ("v", 512), ("gateA", 512), ("beta", 4), ("a", 4), ("f", 512),
                    ("i", 512), ("qB", 512), ("gateB", 512)):
        z2[name] = a["w_in_2"][0][:, at:at + n]
        at += n
    ab = np.zeros((D, S), f)
    ab[:, 0:GH], ab[:, 32:32 + GH] = z2["beta"], z2["a"]
    put_k("S0", ab)
    f2 = np.concatenate([z2["f"], z2["qB"], z2["q"], z2["k"], z2["v"]], 1)
    for i in range(10):
        put_k(f"S{i + 1}", f2[:, S * i:S * (i + 1)])
    t2 = np.concatenate([z2["i"], z2["gateA"], z2["gateB"]], 1)
    for i in range(6):
        put_k(f"U{i}", t2[:, S * i:S * (i + 1)])
    for e in range(E1):
        g, u, d = k_major(a["w_e_gate"][0, e]), k_major(a["w_e_up"][0, e]), k_major(a["w_e_down"][0, e])
        gu = np.concatenate([g, u], 2).reshape(P, -1)
        for p in range(12):
            pieces[f"e{e}gu{p}"] = gu[:, PC * p:PC * (p + 1)]
        for q in range(6):
            pieces[f"e{e}d{q}"] = d[:, 2 * q:2 * q + 2].reshape(P, -1)
    for e in range(E2 + 1):
        g, u, d = ((a["w_gate_2"][0, e], a["w_up_2"][0, e], a["w_down_2"][0, e]) if e < E2 else
                   (a["ws_gate_2"][0], a["ws_up_2"][0], a["ws_down_2"][0]))
        g, u = k_major(g), k_major(u)
        for b, n in enumerate("ab"):
            c = slice(b * P, (b + 1) * P)
            pieces[f"r{e}{n}"] = np.concatenate([g[:, :, c], u[:, :, c]], 2).reshape(P, -1)
        pieces[f"r{e}d"] = k_major(d).reshape(P, -1)

    def column(v):
        return v.reshape(-1, P).T

    def everywhere(v):
        return np.broadcast_to(v.reshape(1, -1), (P, v.size))

    def gate_column(fw, bw):
        v = np.zeros((P, 1), f)
        v[0:AH, 0], v[32:32 + AH, 0] = fw, bw
        return v

    b = a["b_if"][0].reshape(4, AH)
    vals = dict(
        mix_g=column(a["mix_norm_g"][0]),
        conv_w=a["conv_w"][0].T.reshape(4, P, BK).transpose(1, 0, 2).reshape(P, -1),
        conv_b=column(a["conv_b"][0]), ln_g=column(a["conv_ln_g"][0]), ln_b=column(a["conv_ln_b"][0]),
        a_g=a["a_norm_g"][0].T, cq_g=column(a["cq_norm_g"][0]), ckv_g=column(a["ckv_norm_g"][0]),
        qn_g=everywhere(a["q_norm_g"][0]), kn_g=everywhere(a["k_norm_g"][0]),
        b_i=gate_column(b[0], b[2]), b_f=gate_column(b[1], b[3]),
        ffn_g=column(a["ffn_norm_g"][0]), router=k_major(a["w_router"][0]).reshape(P, -1),
        c=column(a["c_2"][0]),
        b_ada=np.concatenate([column(a["b_ada_2"][0][D * i:D * (i + 1)]) for i in (0, 1, 3, 4, 2, 5)], 1),
        n1w=column(a["norm1_w_2"][0]),
        conv2_w=a["conv_w_2"][0].T.reshape(12, P, CONV2).transpose(1, 0, 2).reshape(P, -1),
        a_log=np.pad(a["gdn_a_log_2"][0].reshape(GH, 1), ((0, P - GH), (0, 0))),
        dt=np.pad(a["gdn_dt_bias_2"][0].reshape(GH, 1), ((0, P - GH), (0, 0))),
        og=np.concatenate([np.repeat(a["gdn_norm_w_2"][0].reshape(P, 1), GH, 1),
                           column(a["hg_norm_w_2"][0])], 1),
        lb0=column(a["hg_lb_2"][0]), lb1=column(a["hg_lb_2"][1]), n2w=column(a["norm2_w_2"][0]),
        router2=k_major(a["w_router_2"][0]).reshape(P, -1), rbias=everywhere(a["router_bias_2"][0]))
    vec = np.concatenate([vals[n].reshape(P, w) for n, w in VEC.items()], 1)
    return pieces, np.ascontiguousarray(vec)


def constants():
    f = np.float32
    i = np.arange(P)
    s, t = i[:, None], i[None, :]
    tri = (s <= t).astype(f)
    one = np.ones((P, P), f)
    mask = np.concatenate([tri, one, tri, tri.T, one, tri.T], 1) * f(AD ** -0.5)
    levels = [((s < t) & ((s ^ t) >= 2 ** n) & ((s ^ t) < 2 ** (n + 1))).astype(f) for n in range(LEVELS)]
    g = np.arange(NG2)
    inv = (np.float32(10000.0) ** (-np.arange(0, CR, 2, dtype=f) / f(CR))).astype(f)
    ang = np.arange(S, dtype=f)[:, None] * inv[None, :]
    by_tile = lambda v: v.reshape(TT, P, -1).transpose(1, 0, 2).reshape(P, -1)
    vals = dict(ident=np.eye(P, dtype=f), ones=one, tri=tri, mmask=mask, levels=np.concatenate(levels, 1),
                iota=np.tile(np.arange(1, CAP + 1, dtype=f), (P, 1)),
                gbefore=np.tile((g[None, :] < g[:, None]).astype(f).reshape(1, -1), (P, 1)),
                cos=by_tile(np.cos(ang)), sin=by_tile(np.sin(ang)), eps=np.full((P, 1), EPS, f))
    return np.concatenate([vals[n].astype(f).reshape(P, w) for n, w in CST.items()], 1)


def make(nc, **kw):
    order = []
    n_pieces = kw.pop("n_pieces")
    dram = lambda n, s, k: nc.dram_tensor(n, s, F32, kind=k).ap()
    build(nc, dram("x", (1, S, D), "ExternalInput"), dram("stream", (n_pieces, P, PC), "ExternalInput"),
          dram("vec_pack", (P, VN), "ExternalInput"), dram("const_pack", (P, CN_ALL), "ExternalInput"),
          dram("final_w", (P, D), "ExternalInput"),
          dram("result", (1, S, D), "ExternalOutput"), order, **kw)
    return order


def arrays(inputs, order):
    a = {k: np.asarray(v) for k, v in inputs.items()}
    pieces, vec = layout(a)
    stream = np.zeros((len(order), P, PC), np.float32)
    for n, name in enumerate(order):
        p = pieces[name]
        stream[n, :, :p.shape[1]] = p
    return {"x": a["x"], "stream": stream, "vec_pack": vec, "const_pack": constants(),
            "final_w": np.tile(a["final_norm_w_2"], (P, 1))}


def kernel(**inputs):
    from concourse import bacc
    from concourse.bass_utils import run_bass_kernel_spmd

    nc = bacc.Bacc("TRN2", target_bir_lowering=False, num_devices=1)
    order = make(nc, n_pieces=N_PIECES)
    assert len(order) == N_PIECES, len(order)
    r = run_bass_kernel_spmd(nc, [arrays(inputs, order)], core_ids=[0])
    return r.results[0]["result"]
```
